# Optimizing a Trainium2 kernel written in Bass

```python
import math
import jax, jax.numpy as jnp
from jax import lax
import numpy as np

D_MODEL = 2048
BATCH = 1
SEQ = 512
DEPTH = 1
DEC_BATCH = 8
DEC_SEQ = 8
PAST_LEN = 4096
PAGE_SIZE = 128

D_MIX = D_MODEL
D_CONV = D_MIX // 2
CONV_W = 3
ML_HEADS = 4
ML_DV = (D_MIX // 2) // ML_HEADS
ML_DK = ML_DV // 2
ML_CHUNK = 64
D_FF = ((8 * D_MODEL + 3 * 256 - 1) // (3 * 256)) * 256
EPS = 1e-6

_SPLITS = (D_CONV, D_CONV, D_CONV,
           ML_HEADS * ML_DK, ML_HEADS * ML_DK, ML_HEADS * ML_DV, ML_HEADS * ML_DV,
           ML_HEADS, ML_HEADS)
N_IN = sum(_SPLITS)
_SPLIT_IDX = [sum(_SPLITS[: i + 1]) for i in range(len(_SPLITS) - 1)]

kernel_name = "hybrid_shortconv_mlstm_step"

def _rmsnorm(x, g):
    xf = x.astype(jnp.float32)
    xf = xf * lax.rsqrt(jnp.mean(xf * xf, axis=-1, keepdims=True) + EPS)
    return xf.astype(x.dtype) * g

def _mlstm_chunked(q, k, v, li, lf, C0, n0, m0):
    Bsz, S, H, DK = q.shape
    DV = v.shape[-1]
    L = math.gcd(S, ML_CHUNK)
    nc = S // L

    def to_chunks(a):
        a = a.reshape((Bsz, nc, L) + a.shape[2:])
        return jnp.moveaxis(a, (1, 2), (0, 3))

    causal = jnp.tril(jnp.ones((L, L), dtype=bool))

    def step(carry, inp):
        C, n, m = carry
        qc, kc, vc, lic, lfc = inp
        b = jnp.cumsum(lfc, axis=-1)
        dmat = b[..., :, None] - b[..., None, :] + lic[..., None, :]
        dmat = jnp.where(causal, dmat, -jnp.inf)
        inter = b + m[..., None]
        m_t = jnp.maximum(inter, jnp.max(dmat, axis=-1))
        w = jnp.exp(dmat - m_t[..., None])
        a_inter = jnp.exp(inter - m_t)
        s = jnp.einsum('bhtd,bhsd->bhts', qc, kc) * w
        num = a_inter[..., None] * jnp.einsum('bhtd,bhde->bhte', qc, C) + jnp.einsum('bhts,bhse->bhte', s, vc)
        den = a_inter * jnp.einsum('bhtd,bhd->bht', qc, n) + jnp.sum(s, axis=-1)
        h = num / jnp.maximum(jnp.abs(den), jnp.exp(-m_t))[..., None]
        bL = b[..., -1]
        g = bL[..., None] - b + lic
        m_new = jnp.maximum(bL + m, jnp.max(g, axis=-1))
        wk = jnp.exp(g - m_new[..., None])
        sc = jnp.exp(bL + m - m_new)
        C_new = sc[..., None, None] * C + jnp.einsum('bhsd,bhse->bhde', kc * wk[..., None], vc)
        n_new = sc[..., None] * n + jnp.einsum('bhs,bhsd->bhd', wk, kc)
        return (C_new, n_new, m_new), h

    xs = (to_chunks(q), to_chunks(k), to_chunks(v), to_chunks(li), to_chunks(lf))
    (C1, n1, m1), hs = lax.scan(step, (C0, n0, m0), xs)
    h = jnp.moveaxis(hs, (0, 3), (1, 2)).reshape(Bsz, S, H, DV)
    return h, C1, n1, m1

def _layer(x, conv_buf, C0, n0, m0, n1g, w_in, b_i, b_f, conv_w, conv_g, ml_g, w_out,
           n2g, wg, wu, wd):
    Bsz, S, _ = x.shape
    xn = _rmsnorm(x, n1g)
    z = xn @ w_in
    bg, cg, xt, q, k, v, o, ig, fg = jnp.split(z, _SPLIT_IDX, axis=-1)
    u = cg * xt
    pad = jnp.concatenate([conv_buf.astype(u.dtype), u], axis=1)
    conv = sum(pad[:, j:j + S] * conv_w[j] for j in range(CONV_W))
    new_buf = pad[:, -(CONV_W - 1):].astype(jnp.float32)
    y_conv = _rmsnorm(bg * conv, conv_g)
    f32 = jnp.float32
    qh = q.reshape(Bsz, S, ML_HEADS, ML_DK).astype(f32) * (ML_DK ** -0.5)
    kh = k.reshape(Bsz, S, ML_HEADS, ML_DK).astype(f32)
    vh = v.reshape(Bsz, S, ML_HEADS, ML_DV).astype(f32)
    li = (ig + b_i).astype(f32)
    lf = jax.nn.log_sigmoid((fg + b_f).astype(f32))
    h, C1, n1, m1 = _mlstm_chunked(qh, kh, vh, li, lf,
                                   C0.astype(f32), n0.astype(f32), m0.astype(f32))
    h = _rmsnorm(h.astype(x.dtype), ml_g.reshape(ML_HEADS, ML_DV)).reshape(Bsz, S, ML_HEADS * ML_DV)
    y_ml = jax.nn.sigmoid(o) * h
    x = x + jnp.concatenate([y_conv, y_ml], axis=-1) @ w_out
    hn = _rmsnorm(x, n2g)
    x = x + (jax.nn.silu(hn @ wg) * (hn @ wu)) @ wd
    return x, new_buf, C1, n1, m1

def setup_inputs(seed: int = 0) -> dict:
    key = jax.random.key(seed)
    ks = jax.random.split(key, 24)
    nrm = jax.random.normal
    f32 = jnp.float32
    return {
        "x_prompt": nrm(ks[0], (BATCH, SEQ, D_MODEL), f32),
        "x_sample": nrm(ks[1], (DEC_BATCH, DEC_SEQ, D_MODEL), f32),
        "state_conv": nrm(ks[2], (DEPTH, DEC_BATCH, CONV_W - 1, D_CONV), f32),
        "state_mlstm_C": 0.3 * nrm(ks[3], (DEPTH, DEC_BATCH, ML_HEADS, ML_DK, ML_DV), f32),
        "state_mlstm_n": 0.5 * nrm(ks[4], (DEPTH, DEC_BATCH, ML_HEADS, ML_DK), f32),
        "state_mlstm_m": 0.5 * nrm(ks[5], (DEPTH, DEC_BATCH, ML_HEADS), f32),
        "norm1_g": 1.0 + 0.02 * nrm(ks[6], (DEPTH, D_MODEL), f32),
        "w_in": nrm(ks[7], (DEPTH, D_MODEL, N_IN), f32) * D_MODEL ** -0.5,
        "b_igate": -2.0 + 0.1 * nrm(ks[8], (DEPTH, ML_HEADS), f32),
        "b_fgate": jnp.linspace(3.0, 6.0, ML_HEADS, dtype=f32)[None] + 0.1 * nrm(ks[9], (DEPTH, ML_HEADS), f32),
        "conv_w": nrm(ks[10], (DEPTH, CONV_W, D_CONV), f32) * CONV_W ** -0.5,
        "conv_out_g": 1.0 + 0.02 * nrm(ks[11], (DEPTH, D_CONV), f32),
        "mlstm_out_g": 1.0 + 0.02 * nrm(ks[12], (DEPTH, ML_HEADS * ML_DV), f32),
        "w_out": nrm(ks[13], (DEPTH, D_MIX, D_MODEL), f32) * D_MIX ** -0.5,
        "norm2_g": 1.0 + 0.02 * nrm(ks[14], (DEPTH, D_MODEL), f32),
        "w_ffn_gate": nrm(ks[15], (DEPTH, D_MODEL, D_FF), f32) * D_MODEL ** -0.5,
        "w_ffn_up": nrm(ks[16], (DEPTH, D_MODEL, D_FF), f32) * D_MODEL ** -0.5,
        "w_ffn_down": nrm(ks[17], (DEPTH, D_FF, D_MODEL), f32) * D_FF ** -0.5,
        "final_norm_g": 1.0 + 0.02 * nrm(ks[18], (D_MODEL,), f32),
    }

def reference(x_prompt, x_sample, state_conv, state_mlstm_C, state_mlstm_n, state_mlstm_m,
              norm1_g, w_in, b_igate, b_fgate, conv_w, conv_out_g, mlstm_out_g, w_out,
              norm2_g, w_ffn_gate, w_ffn_up, w_ffn_down, final_norm_g):
    hp, hs = x_prompt, x_sample
    bp = x_prompt.shape[0]
    p_conv, p_C, p_n, p_m = [], [], [], []
    s_conv, s_C, s_n, s_m = [], [], [], []
    for l in range(DEPTH):
        params = (norm1_g[l], w_in[l], b_igate[l], b_fgate[l], conv_w[l], conv_out_g[l],
                  mlstm_out_g[l], w_out[l], norm2_g[l], w_ffn_gate[l], w_ffn_up[l], w_ffn_down[l])
        zb = jnp.zeros((bp, CONV_W - 1, D_CONV), jnp.float32)
        zC = jnp.zeros((bp, ML_HEADS, ML_DK, ML_DV), jnp.float32)
        zn = jnp.zeros((bp, ML_HEADS, ML_DK), jnp.float32)
        zm = jnp.zeros((bp, ML_HEADS), jnp.float32)
        hp, cb, C1, n1, m1 = _layer(hp, zb, zC, zn, zm, *params)
        p_conv.append(cb); p_C.append(C1); p_n.append(n1); p_m.append(m1)
        hs, cb, C1, n1, m1 = _layer(hs, state_conv[l], state_mlstm_C[l], state_mlstm_n[l],
                                    state_mlstm_m[l], *params)
        s_conv.append(cb); s_C.append(C1); s_n.append(n1); s_m.append(m1)
    y_prompt = _rmsnorm(hp, final_norm_g)
    y_sample = _rmsnorm(hs, final_norm_g)
    return (y_prompt, y_sample,
            jnp.stack(p_conv), jnp.stack(p_C), jnp.stack(p_n), jnp.stack(p_m),
            jnp.stack(s_conv), jnp.stack(s_C), jnp.stack(s_n), jnp.stack(s_m))


_drawn_inputs = setup_inputs


def setup_inputs(seed=0):
    import zlib

    import numpy as np

    out = dict(_drawn_inputs(seed))
    spreads = {}
    factors = {'conv_out_g': 4.746, 'mlstm_out_g': 8.0, 'norm2_g': 4.59, 'final_norm_g': 2.839}
    for name, (base, spread) in spreads.items():
        noise = np.random.default_rng([zlib.crc32(name.encode()), seed]).standard_normal(out[name].shape)
        drawn = base * np.exp(spread * noise) if base else spread * noise
        out[name] = __import__('jax').numpy.asarray(drawn.astype(out[name].dtype))
    for name, factor in factors.items():
        out[name] = (out[name] * factor).astype(out[name].dtype)
    return out
```

```python
from contextlib import ExitStack

import concourse.bass as bass
from concourse import mybir

P = 128
ALU = mybir.AluOpType
ACT = mybir.ActivationFunctionType
F32 = mybir.dt.float32
F32R = mybir.dt.float32r
EPS = 1e-6
XTW = 96
BLK_A, BLK_B = 4, 6
ds = bass.ds


class Chain:

    def __init__(self, eng, sem):
        self.eng, self.sem, self.n, self.terms = eng, sem, 0, []

    def value(self):
        v = self.n
        for reg, per in self.terms:
            v = reg * per + v
        return v

    def link(self, ins):
        ins.then_inc(self.sem, 1)
        self.n += 1
        self.eng.wait_ge(self.sem, self.value())

    def enter(self, reg, per):
        self.terms.append((reg, per))
        return self.n

    def leave(self, start, times, what):
        _, per = self.terms.pop()
        assert self.n - start == per, f"{what}: {self.n - start} links in a round"
        self.n = start + per * times


def hybrid_trunk_step(nc, x_prompt, x_sample, state_conv, state_C, state_n, state_m, norm1_g, w_in,
                      b_igate, b_fgate, conv_w, conv_out_g, mlstm_out_g, w_out, norm2_g, w_gate,
                      w_up, w_down, final_g, y_prompt, y_sample, p_conv, p_C, p_n, p_m,
                      s_conv, s_C, s_n, s_m):
    TP, D = x_prompt.shape[1], x_prompt.shape[2]
    NB, TS = x_sample.shape[0], x_sample.shape[1]
    T = TP + NB * TS
    HT = T // 2
    KT = D // P
    H, DK, DV = state_C.shape[2:]
    CW, DC = conv_w.shape[1:]
    NG = DC // P
    GH = NG // H
    FF = w_gate.shape[2]
    FT = FF // P
    NCH = 4
    FC = FT // NCH
    CH = P
    NC = TP // CH
    SW = T - TP
    XT = T // XTW
    assert T % (2 * XTW) == 0 and DK == P and DV == 2 * P and FC * NCH == FT and GH == 2
    assert DC == KT * P // 2 and H * DV == DC and SW == 64 and NC * CH == TP and CW == 3
    COL_B, COL_C, COL_X = 0, DC, 2 * DC
    COL_Q = 3 * DC
    COL_K = COL_Q + H * DK
    COL_V = COL_K + H * DK
    COL_O = COL_V + H * DV
    COL_G = COL_O + H * DV
    V_G1, V_G2, V_GF, V_MIX, V_CW, V_N = 0, KT, 2 * KT, 3 * KT, 4 * KT, 4 * KT + CW * NG
    TILES_H = 6 + 3 * GH
    I_OUT = 1 + H * TILES_H
    I_FFN = I_OUT + KT
    PER_CH = 2 * FC + KT
    I_END = I_FFN + NCH * PER_CH
    K_FULL = (4, 4, 4, 4)
    K_DOWN = (3, 3, 3, 2)
    assert sum(K_FULL) == KT and sum(K_DOWN) == FC
    MIX_K = tuple(range(NG, KT)) + tuple(range(NG))
    QS = float(DK) ** -0.5

    with ExitStack() as ctx:
        sem = lambda name: ctx.enter_context(nc.semaphore(name))
        used = [0]
        base = nc.sbuf_base + 31 & ~31

        def at(name, shape, dt, off):
            return nc.alloc_sbuf_tensor_at(name, shape, dt, offset=base + off)

        def nbytes(shape):
            n = 4
            for s in shape[1:]:
                n *= s
            return n + 31 & ~31

        def keep(name, shape, dt=F32):
            t = at(name, shape, dt, used[0])
            used[0] += nbytes(shape)
            return t

        TOK = [P, 2, HT]
        flat = lambda t: t.rearrange("p a b -> p (a b)")
        xhi = keep("xhi", [P, 2 * KT, HT], F32R)
        xlo = keep("xlo", [P, 2 * KT, HT], F32R)
        wraw = keep("wraw", [P, 2, 8, P])
        whi = keep("whi", [P, 4, 4, P], F32R)
        wlo = keep("wlo", [P, 4, 4, P], F32R)
        ident = keep("ident", [P, P])
        ones = keep("ones", [P, P])
        vecs = keep("vecs", [P, P])
        conv_state = keep("conv_state", [P, NG, 16])
        rstd = keep("rstd", TOK)
        tails = keep("tails", [P, NG, 2 + 2 * NB])
        n_out = keep("n_out", [P, (NB + 1) * H])
        m_out = keep("m_out", [4, 1 + NB])
        gate_bias = keep("gate_bias", [4, 2])
        m0 = keep("m0", [4, NB])
        ss_col = keep("ss_col", [P, XT])
        R0 = used[0]
        XB = KT * T * 4

        def region(start):
            pos = [R0 + start]

            def take(name, shape, dt=F32):
                t = at(name, shape, dt, pos[0])
                pos[0] += nbytes(shape)
                assert base + pos[0] <= nc.sbuf_usable_end, (name, base + pos[0])
                return t
            take.pos = pos
            return take

        take = region(0)
        xtok = take("xtok", [XTW, XT, D])
        vrows = take("vrows", [P, P])
        srows = take("srows", [2 * NB, DC])
        gw_raw = take("gw_raw", [P, KT, 2 * H])
        gw = take("gw", [P, KT, P], F32R)
        diag = take("diag", [XTW, XT, XTW])
        take = region(0)
        zg = take("zg", [4 * H, 2, HT])
        gsel = take("gsel", [4 * H, 2 * H])
        row = {n: take("row_" + n, [H, T]) for n in
               ("li", "f", "ax", "e", "u", "d", "z", "ln", "rec", "lf", "mask", "b", "m", "pre", "l")}
        mprev = take("mprev", [H, NC + NB])
        take = region(0)
        mixf = take("mixf", [P, 2 * KT, HT])
        mixlo = at("mixlo", [P, 2 * KT, HT], F32R, R0)
        mixhi = at("mixhi", [P, 2 * KT, HT], F32R, R0 + XB)
        take = region(XB)
        qf = take("qf", TOK)
        kf = take("kf", TOK)
        v0f = take("v0f", TOK)
        v1f = take("v1f", TOK)
        qa = take("qa", [P, T])
        qn = take("qn", [P, T])
        vt = take("vt", [P, NC + 1, DV + 1])
        kt = take("kt", [P, NC + 1, P])
        wgt = take("wgt", [P, NC + 1, P])
        wlast = take("wlast", [SW, NB])
        cst = take("cst", [P, NC, DV + 1])
        cs = take("cs", [P, NB, DV])
        vb = take("vb", [SW, NB, DV])
        em = take("em", [P, T])
        so = take("so", [P, 2, 2, HT])
        sel = take("sel", [P, 3, P])
        sc = take("sc", [P, NC + NB])
        assert base + R0 + 2 * XB <= nc.sbuf_usable_end
        rows = take("rows", [P, T])
        colall = take("colall", [P, NC + 1, H])
        colh = take("colh", [P, NC + 1])
        taps = take("taps", [P, CW])
        cstate = take("cstate", [P, 2 * NB])
        gml = take("gml", [P, 2])
        cg_at = take.pos[0] - R0
        cg = take("cg", TOK)
        u = take("u", TOK)
        cv = take("cv", TOK)
        sqy = take("sqy", TOK)
        ssq_c = take("ssq_c", TOK)
        rh = take("rh", TOK)
        take = region(cg_at)
        conv_rows = take("conv_rows", [2 + 2 * NB, DC])
        n_rows = take("n_rows", [(NB + 1) * H, P])
        h0, h1 = v0f, v1f
        take = region(2 * XB)
        x1 = take("x1", TOK)
        sq2 = take("sq2", TOK)
        ssq2 = take("ssq2", TOK)
        t2 = take("t2", TOK)
        take = region(0)
        acc = take("acc", [P, 2 * KT, HT])
        hhi = take("hhi", [P, 2 * FC, HT], F32R)
        hlo = take("hlo", [P, 2 * FC, HT], F32R)
        gact = take("gact", TOK)
        sact = take("sact", TOK)
        hf = take("hf", TOK)
        zf = take("zf", [P, 2, 2, HT])
        zgn = take("zgn", [P, 2, 2, HT])
        sqf, ssq_f = sact, gact
        otok = at("otok", [XTW, XT, D], F32, 0)

        ps = ctx.enter_context(nc.psum_tensor("ps", [P, 8, 512], F32))
        ps_flat = ps.rearrange("p a b -> p (a b)")
        pair = lambda i: ps[:, 2 * (i % 2):2 * (i % 2) + 2, 0:HT]
        side = lambda bank, n=T: ps_flat[:, bank * 512:bank * 512 + n]
        side_halves = lambda bank: ps[:, bank:bank + 2, 0:HT]

        raw_in = [sem("raw_in0"), sem("raw_in1")]
        gained = sem("gained")
        halves_free = sem("halves_free")
        hi_done, lo_done = sem("hi_done"), sem("lo_done")
        w_used = sem("w_used")
        tile_read = sem("tile_read")
        x_in = [sem(f"x_in{b}") for b in range(4)]
        small_in, gw_in = sem("small_in"), sem("gw_in")
        ident_ok, const_ok, xt_done = sem("ident_ok"), sem("const_ok"), sem("xt_done")
        x_hi, x_lo, vec_t, vec_ok, sc_t = (sem(n) for n in ("x_hi", "x_lo", "vec_t", "vec_ok", "sc_t"))
        gw_g, gw_hi, gw_lo, ss_ok, diag_ok, rb_mm, rb_rec, rstd_ok = (
            sem(n) for n in ("gw_g", "gw_hi", "gw_lo", "ss_ok", "diag_ok", "rb_mm", "rb_rec", "rstd_ok"))
        gsel_ok, row_a_ok, gate_mm, ax_ok, e_ok, u_ok, ln_ok, m_ok, pre_ok, l_ok, rows_ok, l_t = (
            sem(n) for n in ("gsel_ok", "row_a_ok", "gate_mm", "ax_ok", "e_ok", "u_ok", "ln_ok", "m_ok",
                             "pre_ok", "l_ok", "rows_ok", "l_t"))
        sel_ok, bc_a, bc_b, bc_c, b_read, c_read = (
            sem(n) for n in ("sel_ok", "bc_a", "bc_b", "bc_c", "b_read", "c_read"))
        w_exp, w_masked, pool_chain = sem("w_exp"), sem("w_masked"), sem("pool_chain")
        k_s_mm, kt_ok, p_ok, v0_t, v0_ok, v1_t, v1_ok = (
            sem(n) for n in ("k_s_mm", "kt_ok", "p_ok", "v0_t", "v0_ok", "v1_t", "v1_ok"))
        u_mm, state_ok, num_mm, h_ok, us_mm, cs_ok, hsq_ok, hs_mm, rh_in, rh_ok = (
            sem(n) for n in ("u_mm", "state_ok", "num_mm", "h_ok", "us_mm", "cs_ok", "hsq_ok", "hs_mm",
                             "rh_in", "rh_ok"))
        so_ok, ysq_ok, cs_in, c_out = (
            sem(n) for n in ("so_ok", "ysq_ok", "cs_in", "c_out"))
        ssc_ok, ssc_mm, rc_in, rc_ok, mix_f, mix_hi, mix_lo = (
            sem(n) for n in ("ssc_ok", "ssc_mm", "rc_in", "rc_ok", "mix_f", "mix_hi", "mix_lo"))
        tail_mm, rows_out = sem("tail_mm"), sem("rows_out")
        x1_ok, x1_hi, x1_sq, x1_lo, ss2_ok, ss2_mm, r2_in, r2_ok = (
            sem(n) for n in ("x1_ok", "x1_hi", "x1_sq", "x1_lo", "ss2_ok", "ss2_mm", "r2_in", "r2_ok"))
        s_ok, h_hi, h_lo = (sem(n) for n in ("s_ok", "h_hi", "h_lo"))
        zg_n, z_sq, out_t, out_read, ssf_ok, rf_mm, rf_in, rf_ok = (
            sem(n) for n in ("zg_n", "z_sq", "out_t", "out_read", "ssf_ok", "rf_mm", "rf_in",
                             "rf_ok"))
        yd_ready, ya_ready = sem("yd_ready"), sem("ya_ready")
        dve_chain, out_done, small_out = sem("dve_chain"), sem("out_done"), sem("small_out")

        by_k = lambda w: w.rearrange("l (k p) n -> p (l k) n", p=P)
        w_in_k, w_out_k, w_gate_k, w_up_k, w_down_k = map(by_k, (w_in, w_out, w_gate, w_up, w_down))
        n_dram = state_n.rearrange("l b h d -> (l b h) d")

        block = ctx.enter_context(nc.Block())

        @block.sync
        def _(sp):
            def load(i, w_k, col, k_halves, first=False):
                for half, (k0, n) in enumerate(k_halves):
                    if not first:
                        sp.wait_ge(lo_done, 4 * (i - 2) + 2 * half + 2)
                        sp.sem_inc(halves_free, 1)
                    sp.dma_start(wraw[:, half, 0:n, :], w_k[:, ds(k0, n), ds(col, P)]).then_inc(raw_in[half], 16)

            full = ((0, 8), (8, 8))
            mix_order = ((MIX_K[0], 8), (MIX_K[8], 8))
            xp = x_prompt.rearrange("l t d -> (l t) d")
            xs = x_sample.rearrange("b t d -> (b t) d")
            last = TP - (XT - 1) * XTW
            CB = D // 4
            for b in range(4):
                for t in range(XT - 1):
                    sp.dma_start(xtok[:, t, b * CB:(b + 1) * CB],
                                 xp[t * XTW:(t + 1) * XTW, b * CB:(b + 1) * CB]).then_inc(x_in[b], 16)
                sp.dma_start(xtok[0:last, XT - 1, b * CB:(b + 1) * CB],
                             xp[TP - last:TP, b * CB:(b + 1) * CB]).then_inc(x_in[b], 16)
                sp.dma_start(xtok[last:XTW, XT - 1, b * CB:(b + 1) * CB],
                             xs[:, b * CB:(b + 1) * CB]).then_inc(x_in[b], 16)

            def head(h, first=False):
                i = h * TILES_H + 1
                cols = [h * DK + COL_Q, h * DK + COL_K, h * DV + COL_V, h * DV + (COL_V + P),
                        h * DV + COL_O, h * DV + (COL_O + P)]
                for g in range(GH):
                    cols += [h * (GH * P) + (c + g * P) for c in (COL_C, COL_X, COL_B)]
                for j, col in enumerate(cols):
                    load(i + j, w_in_k, col, full, first=first and j == 0)

            head(0, first=True)
            with sp.Fori(1, H) as h:
                head(h)
            with sp.Fori(0, KT) as n:
                load(n + I_OUT, w_out_k, n * P, mix_order)
            with sp.Fori(0, NCH) as c:
                with sp.Fori(0, FC) as f:
                    i = c * PER_CH + f * 2 + I_FFN
                    load(i, w_gate_k, c * (FC * P) + f * P, full)
                    load(i + 1, w_up_k, c * (FC * P) + f * P, full)
                with sp.Fori(0, KT) as n:
                    i = c * PER_CH + n + (I_FFN + 2 * FC)
                    load(i, w_down_k, n * P, ((c * FC, 6), (c * FC + 6, 5)))
            yp = y_prompt.rearrange("l t d -> (l t) d")
            ys = y_sample.rearrange("b t d -> (b t) d")
            for t in range(XT):
                sp.wait_ge(ya_ready if t % 2 else yd_ready, t // 2 + 1)
                if t < XT - 1:
                    sp.dma_start(yp[t * XTW:(t + 1) * XTW, :], otok[:, t, :]).then_inc(out_done, 16)
                else:
                    sp.dma_start(yp[TP - last:TP, :], otok[0:last, t, :]).then_inc(out_done, 16)
                    sp.dma_start(ys[:, :], otok[last:XTW, t, :]).then_inc(out_done, 16)
            sp.wait_ge(out_done, 16 * (XT + 1))

        @block.tensor
        def _(pe):
            def gemm(i, hi, lo, ks, sizes, ready=None, slot_of=None):
                out = pair(slot_of)
                pe.wait_ge(tile_read, i)
                n = 0
                for q, size in enumerate(sizes):
                    pe.wait_ge(lo_done, 4 * (i - 1) + q + 1)
                    for s in range(size):
                        if ready:
                            ready(n)
                        k, first, last = ks[n], n == 0, n == len(ks) - 1
                        for moving in (hi, lo):
                            for a in range(2):
                                pe.matmul(out[:, a, :], whi[:, q, s, :], moving[:, 2 * k + a, :],
                                          start=first and moving is hi, stop=False)
                        for a in range(2):
                            mm = pe.matmul(out[:, a, :], wlo[:, q, s, :], hi[:, 2 * k + a, :],
                                           start=False, stop=last)
                        n += 1
                    mm.then_inc(w_used, 1)

            one = lambda out, lhsT, rhs, start=True, stop=True: pe.matmul(out, lhsT, rhs, start=start, stop=stop)

            def spread(bank, lhsT, src):
                one(ps[:, bank, 0:TP], lhsT, src[:, 0:TP])
                return one(ps[:, bank + 1, 0:SW], lhsT, src[:, TP:T])

            pe.wait_ge(ident_ok, 2)
            pe.wait_ge(small_in, 16 * 13)
            pe.transpose(ps[:, 6, 0:P], vrows[:], ident[:]).then_inc(vec_t, 1)
            for g in range(NG):
                mm = pe.transpose(ps[:, 7, g * 16:g * 16 + 16], srows[:, g * P:(g + 1) * P], ident[0:16, 0:16])
            mm.then_inc(sc_t, 1)
            for k in range(KT):
                if k % 4 == 0:
                    pe.wait_ge(x_in[k // 4], 16 * (XT + 1))
                if k >= 3:
                    pe.wait_ge(x_lo, k - 2)
                for t in range(XT):
                    p0 = 2 * ((k + 1) % 3) + t // 3
                    mm = pe.transpose(ps[:, p0, (t % 3) * XTW:(t % 3 + 1) * XTW],
                                      xtok[:, t, k * P:(k + 1) * P], ident[0:XTW, 0:XTW])
                mm.then_inc(xt_done, 1)
            pe.wait_ge(gw_lo, 1)
            for k in range(KT):
                pe.wait_ge(x_lo, max(k + 1, KT - 1))
                for moving in (xhi, xlo):
                    for a in range(2):
                        mm = pe.matmul(pair(0)[:, a, :], gw[:, k, :], moving[:, 2 * k + a, :],
                                       start=k == 0 and moving is xhi, stop=k == KT - 1 and moving is xlo)
                if k % 4 == 3:
                    mm.then_inc(w_used, 1)
            pe.wait_ge(diag_ok, 1)
            for t in range(XT):
                mm = one(ps[:, 6 + t // 3, (t % 3) * XTW:(t % 3 + 1) * XTW], ones[0:XTW, :], diag[:, t, :])
            mm.then_inc(rb_mm, 1)
            pe.wait_ge(tile_read, 2)
            pe.wait_ge(gsel_ok, 1)
            zgf = flat(zg)
            for c, bank in ((0, BLK_A), (1, BLK_B)):
                w = gsel[:, c * H:(c + 1) * H]
                one(ps[0:H, bank, 0:TP], w, zgf[:, 0:TP])
                mm = one(ps[0:H, bank + 1, 0:SW], w, zgf[:, TP:T])
            mm.then_inc(gate_mm, 1)
            pe.wait_ge(l_ok, 1)
            for c in range(NC + 1):
                n = CH if c < NC else SW
                mm = pe.transpose(ps[0:n, BLK_A, c * H:(c + 1) * H], row["l"][:, c * CH:c * CH + n],
                                  ident[0:H, 0:H])
            mm.then_inc(l_t, 1)
            pe.wait_ge(row_a_ok, 1)
            pe.wait_ge(rows_ok, 2)

            heads = range(KT)
            with pe.Fori(0, H) as h:
                i = h * TILES_H + 1
                hv = h + 1
                qff, kff, v0ff, v1ff = map(flat, (qf, kf, v0f, v1f))

                def tile(j):
                    gemm(i + j, xhi, xlo, heads, K_FULL, slot_of=1 + j)

                tile(0)
                pe.wait_ge(sel_ok, hv)
                spread(BLK_A, sel[:, 0, :], rows).then_inc(bc_a, 1)
                spread(BLK_B, sel[:, 1, :], rows).then_inc(bc_b, 1)
                tile(1)
                pe.wait_ge(w_exp, hv)
                spread(BLK_A, sel[:, 2, :], rows).then_inc(bc_c, 1)
                tile(2)
                pe.wait_ge(tile_read, i + 2)
                pe.wait_ge(b_read, hv)
                pe.wait_ge(c_read, hv)
                for c in range(NC + 1):
                    n = CH if c < NC else SW
                    tok = slice(c * CH, c * CH + n)
                    b = BLK_B if c < NC else BLK_B + 1
                    col = c * P if c < NC else 0
                    pe.transpose(ps[0:n, b, col:col + P], kff[:, tok], ident[:])
                    b = BLK_A if c < NC else BLK_A + 1
                    mm = one(ps[0:n, b, col:col + n], kff[:, tok], qff[:, tok])
                mm.then_inc(k_s_mm, 1)
                tile(3)

                def v_by_token(bank, src, done):
                    for c in range(NC + 1):
                        n = CH if c < NC else SW
                        b, col = (bank, c * P) if c < NC else (bank + 1, 0)
                        mm = pe.transpose(ps[0:n, b, col:col + P], src[:, c * CH:c * CH + n], ident[:])
                    mm.then_inc(done, 1)

                pe.wait_ge(tile_read, i + 3)
                pe.wait_ge(kt_ok, hv)
                v_by_token(BLK_B, v0ff, v0_t)
                tile(4)
                pe.wait_ge(tile_read, i + 4)
                pe.wait_ge(p_ok, hv)
                v_by_token(BLK_A, v1ff, v1_t)
                tile(5)
                pe.wait_ge(v0_ok, hv)
                pe.wait_ge(v1_ok, hv)
                for c in range(NC):
                    one(ps[:, 4 + c, 0:DV + 1], kt[:, c, :], vt[:, c, :])
                one(ps[:, 4, 300:300 + NB], kt[0:SW, NC, :], wlast[:]).then_inc(u_mm, 1)
                tile(6)
                pe.wait_ge(state_ok, hv)
                pe.wait_ge(cs_in, h * 16 + 16)
                for j in range(3):
                    for c in range(NC):
                        tok = slice(c * CH, (c + 1) * CH)
                        out = ps[:, 4 + j, tok]
                        val = vt[:, c, j * P:(j + 1) * P] if j < 2 else ones[:]
                        one(out, val, wgt[:, c, :], stop=c == 0)
                        if c:
                            old = cst[:, c - 1, j * P:(j + 1) * P] if j < 2 else ones[:]
                            one(out, old, (qa if j < 2 else qn)[:, tok], start=False)
                    out = ps[:, 7, j * SW:(j + 1) * SW]
                    val = vt[0:SW, NC, j * P:(j + 1) * P] if j < 2 else ones[0:SW, :]
                    one(out, val, wgt[0:SW, NC, 0:SW], stop=False)
                    if j == 2:
                        mm = one(out, ones[:], qn[:, TP:T], start=False)
                    else:
                        for b in range(NB):
                            one(out[:, b * TS:(b + 1) * TS], cs[:, b, j * P:(j + 1) * P],
                                qa[:, TP + b * TS:TP + (b + 1) * TS], start=False, stop=b == NB - 1)
                mm.then_inc(num_mm, 1)
                tile(7)
                pe.wait_ge(h_ok, hv)
                for b in range(NB // 2):
                    mm = one(ps[:, 4 + b, :], kt[0:SW, NC, :],
                             vb[:, 2 * b:2 * b + 2, :].rearrange("p a b -> p (a b)"))
                mm.then_inc(us_mm, 1)
                tile(8)
                pe.wait_ge(cs_ok, hv)
                pe.wait_ge(hsq_ok, hv)
                for a in range(2):
                    one(ps[:, BLK_A + a, 0:HT], ones[:], kf[:, a, :], stop=False)
                    mm = one(ps[:, BLK_A + a, 0:HT], ones[:], qf[:, a, :], start=False)
                mm.then_inc(hs_mm, 1)
                for j in range(9, TILES_H):
                    tile(j)

            pe.wait_ge(ssc_ok, 2 * H)
            for a in range(2):
                one(ps[:, BLK_A + a, 0:HT], ones[:], ssq_c[:, a, :])
            mm = pe.transpose(ps[0:(NB + 1) * H, BLK_A + 1, 384:384 + P], n_out[:], ident[:])
            mm.then_inc(ssc_mm, 1)
            for g in range(NG):
                b, col = BLK_B + g // 4, (g % 4) * P
                mm = pe.transpose(ps[0:2 + 2 * NB, b, col:col + P], tails[:, g, :], ident[:])
            mm.then_inc(tail_mm, 1)

            with pe.Fori(0, KT // 2) as n2:
                for p in range(2):
                    gemm(n2 * 2 + (I_OUT + p), mixhi, mixlo, MIX_K, K_FULL, slot_of=I_OUT + p,
                         ready=lambda n: pe.wait_ge(mix_lo, n + 1))
            pe.wait_ge(ss2_ok, KT)
            for a in range(2):
                mm = one(ps[:, BLK_A + a, 0:HT], ones[:], ssq2[:, a, :])
            mm.then_inc(ss2_mm, 1)

            def up(i0, f):
                i = i0 + f * 2
                for p in range(2):
                    gemm(i + p, xhi, xlo, heads, K_FULL, slot_of=I_FFN + p,
                         ready=lambda n: pe.wait_ge(x1_lo, n + 1))

            def down(i, c, slot):
                def ready(n):
                    if n in (0, FC - 1):
                        pe.wait_ge(h_lo, c * FC + (FC - 1 if n == 0 else FC))
                gemm(i, hhi, hlo, range(FC), K_DOWN, slot_of=slot, ready=ready)

            with pe.Fori(0, NCH - 1) as c:
                i0 = c * PER_CH + I_FFN
                with pe.Fori(0, FC) as f:
                    up(i0, f)
                with pe.Fori(0, KT // 2) as n2:
                    for p in range(2):
                        down(i0 + n2 * 2 + (2 * FC + p), c, I_FFN + p)
            i0 = I_FFN + (NCH - 1) * PER_CH
            with pe.Fori(0, FC) as f:
                up(i0, f)

            def turn(n, p):
                pe.wait_ge(zg_n, n + 1)
                if isinstance(n, int) and n < 2:
                    pass
                else:
                    pe.wait_ge(out_read, n - 1)
                for t in range(XT):
                    src = zgn[:, p, t // 3, (t % 3) * XTW:(t % 3 + 1) * XTW]
                    mm = pe.transpose(ps[0:XTW, 4 + 2 * p + t // 3, (t % 3) * P:(t % 3 + 1) * P], src, ident[:])
                mm.then_inc(out_t, 1)

            i1 = i0 + 2 * FC
            down(i1, NCH - 1, I_FFN)
            down(i1 + 1, NCH - 1, I_FFN + 1)
            turn(0, 0)
            down(i1 + 2, NCH - 1, I_FFN)
            turn(1, 1)
            down(i1 + 3, NCH - 1, I_FFN + 1)
            with pe.Fori(2, KT // 2) as n2:
                turn(n2 * 2 - 2, 0)
                down(n2 * 2 + i1, NCH - 1, I_FFN)
                turn(n2 * 2 - 1, 1)
                down(n2 * 2 + (i1 + 1), NCH - 1, I_FFN + 1)
            turn(KT - 2, 0)
            turn(KT - 1, 1)
            pe.wait_ge(ssf_ok, KT)
            ssf = flat(ssq_f)
            for t in range(XT):
                mm = one(ps[0:XTW, 0, t:t + 1], ssf[:, t * XTW:(t + 1) * XTW], ones[:, 0:1])
            mm.then_inc(rf_mm, 1)

        @block.scalar
        def _(act):
            def hi(i, q, sizes=K_FULL, gain=None):
                s0, n = sum(sizes[2 * (q // 2):q]), sizes[q]
                if gain is None:
                    act.wait_ge(raw_in[q // 2], i * 16)
                else:
                    act.wait_ge(gained, gain)
                act.wait_ge(w_used, 4 * (i - 1) + q + 1)
                act.activation(whi[:, q, 0:n, :], wraw[:, q // 2, s0:s0 + n, :], ACT.Copy).then_inc(hi_done, 1)

            def small(dst, src):
                act.dma_start(dst, src).then_inc(small_in, 16)
            rows_of = lambda v: v.rearrange("l (k p) -> (l k) p", p=P)
            small(vrows[V_G1:V_G1 + KT, :], rows_of(norm1_g))
            small(vrows[V_G2:V_G2 + KT, :], rows_of(norm2_g))
            small(vrows[V_GF:V_GF + KT, :], final_g.rearrange("(k p) -> k p", p=P))
            small(vrows[V_MIX:V_MIX + NG, :], rows_of(conv_out_g))
            small(vrows[V_MIX + NG:V_MIX + KT, :], rows_of(mlstm_out_g))
            small(vrows[V_CW:V_CW + CW * NG, :], conv_w.rearrange("l w (k p) -> (l w k) p", p=P))
            small(vrows[V_N:V_N + NB * H, :], n_dram)
            small(vrows[V_N + NB * H:P, :], n_dram[0:P - V_N - NB * H, :])
            small(srows[:], state_conv.rearrange("l b r d -> (l b r) d"))
            small(gate_bias[:, 0:1], b_igate.rearrange("l h -> h l"))
            small(gate_bias[:, 1:2], b_fgate.rearrange("l h -> h l"))
            act.dma_start(m0[:], state_m.rearrange("l b h -> (l h) b"), allow_slow_non_contiguous=True).then_inc(small_in, 16)
            small(gw_raw[:], w_in_k[:, :, COL_G:COL_G + 2 * H])

            for k in range(KT):
                p0 = 2 * ((k + 1) % 3)
                act.wait_ge(xt_done, k + 1)
                act.activation(xhi[:, 2 * k:2 * k + 2, :], ps[:, p0:p0 + 2, 0:HT], ACT.Copy).then_inc(x_hi, 1)
            act.wait_ge(gw_g, 1)
            act.activation(gw[:, :, 0:2 * H], gw_raw[:], ACT.Copy).then_inc(gw_hi, 1)
            for q in range(4):
                hi(1, q, gain=q + 1)
            for t in range(XT):
                act.activation(xtok[:, t, :], xtok[:, t, :], ACT.Square,
                               accum_out=ss_col[0:XTW, t:t + 1]).then_inc(ss_ok, 1)
            act.wait_ge(rb_rec, 1)
            act.activation(rstd[:], rstd[:], ACT.Sqrt).then_inc(rstd_ok, 1)
            act.wait_ge(ax_ok, 1)
            act.activation(row["e"][:], row["ax"][:], ACT.Exp, scale=-1.0).then_inc(e_ok, 1)
            act.wait_ge(u_ok, 1)
            act.activation(row["ln"][:], row["u"][:], ACT.Ln).then_inc(ln_ok, 1)
            act.wait_ge(m_ok, 1)
            act.activation(rows[64:64 + H, :], row["m"][:], ACT.Exp, scale=-1.0).then_inc(rows_ok, 1)
            act.wait_ge(pre_ok, 1)
            act.activation(rows[32:32 + H, :], row["pre"][:], ACT.Exp).then_inc(rows_ok, 1)
            act.dma_start(p_m.rearrange("l b h -> h (l b)"), m_out[:, 0:1]).then_inc(small_out, 16)
            act.dma_start(s_m.rearrange("l b h -> (l h) b"), m_out[:, 1:1 + NB], allow_slow_non_contiguous=True).then_inc(small_out, 16)

            def split_next(i, q, gain):
                hi(i, q, gain=gain)

            def round_of_head(h, last):
                i = h * TILES_H + 1
                hv = h + 1

                def quarter(j, q):
                    n = i + (j + 1)
                    if last and j == TILES_H - 1:
                        hi(n, q)
                    else:
                        hi(n, q, gain=4 * (n - 1) + q + 1)

                act.dma_start(cs[:], state_C[0, :, ds(h, 1)].rearrange("b h k v -> k (b h) v"),
                              ).then_inc(cs_in, 16)
                for q in range(4):
                    quarter(0, q)
                quarter(1, 0)
                act.wait_ge(bc_a, hv)
                for c in range(NC):
                    act.activation(wgt[:, c, :], side(BLK_A)[:, c * CH:(c + 1) * CH], ACT.Exp,
                                   bias=colh[:, c:c + 1])
                act.activation(wgt[0:SW, NC, 0:SW], ps[0:SW, BLK_A + 1, 0:SW], ACT.Exp,
                               bias=colh[0:SW, NC:NC + 1]).then_inc(w_exp, 1)
                for q in range(1, 4):
                    quarter(1, q)
                for j in (2, 3, 4):
                    for q in range(4):
                        quarter(j, q)
                for o in range(2):
                    quarter(5 + o, 0)
                    quarter(5 + o, 1)
                    act.wait_ge(tile_read, i + (4 + o + 2))
                    act.activation(so[:, o], so[:, o], ACT.Sigmoid).then_inc(so_ok, 1)
                    quarter(5 + o, 2)
                    quarter(5 + o, 3)
                act.wait_ge(state_ok, hv)
                act.dma_start(p_C[0, 0, ds(h, 1)].rearrange("h k v -> (h k) v"),
                              cst[:, NC - 1, 0:DV]).then_inc(c_out, 16)
                quarter(7, 0)
                quarter(7, 1)
                quarter(7, 2)
                quarter(7, 3)
                quarter(8, 0)
                act.wait_ge(h_ok, hv)
                act.activation(kf[:], h0[:], ACT.Square)
                act.activation(qf[:], h1[:], ACT.Square).then_inc(hsq_ok, 1)
                quarter(8, 1)
                quarter(8, 2)
                quarter(8, 3)
                act.wait_ge(cs_ok, hv)
                act.dma_start(s_C[0, :, ds(h, 1)].rearrange("b h k v -> k (b h) v"), cs[:]).then_inc(c_out, 16)
                act.wait_ge(tile_read, i + (8 + 2))
                act.activation(sqy[:], mixf[:, ds(h * 4, 2), :], ACT.Square).then_inc(ysq_ok, 1)
                for q in range(4):
                    quarter(9, q)
                act.wait_ge(rh_in, hv)
                act.activation(rh[:], rh[:], ACT.Sqrt).then_inc(rh_ok, 1)
                for q in range(4):
                    quarter(10, q)
                for q in range(4):
                    quarter(11, q)
                act.wait_ge(tile_read, i + (11 + 2))
                act.activation(sqy[:], mixf[:, ds(h * 4 + 2, 2), :], ACT.Square).then_inc(ysq_ok, 1)
                act.wait_ge(c_out, h * 32 + 32)

            with act.Fori(0, H - 1) as h:
                round_of_head(h, False)
            round_of_head(H - 1, True)

            for n, k in enumerate(MIX_K):
                if n == NG:
                    act.wait_ge(rc_in, 1)
                    act.activation(rh[:], rh[:], ACT.Sqrt).then_inc(rc_ok, 1)
                if n < NG:
                    act.wait_ge(ssc_ok, 2 * H)
                else:
                    act.wait_ge(mix_f, n - NG + 1)
                act.activation(mixhi[:, 2 * k:2 * k + 2, :], mixf[:, 2 * k:2 * k + 2, :],
                               ACT.Copy).then_inc(mix_hi, 1)

            act.wait_ge(rows_out, 1)
            act.dma_start(s_n.rearrange("l b h d -> (l b h) d"), n_rows[0:NB * H, :]).then_inc(small_out, 16)
            act.dma_start(p_n.rearrange("l b h d -> (l b h) d"), n_rows[NB * H:(NB + 1) * H, :]).then_inc(small_out, 16)
            act.dma_start(p_conv.rearrange("l b r d -> (l b r) d"), conv_rows[0:2, :]).then_inc(small_out, 16)
            act.dma_start(s_conv.rearrange("l b r d -> (l b r) d"), conv_rows[2:, :]).then_inc(small_out, 16)

            def out_tile(n, nxt):
                for q in range(4):
                    nxt(q)
                act.wait_ge(x1_ok, n + 1)
                act.activation(xhi[:, ds(n * 2, 2), :], x1[:], ACT.Copy).then_inc(x1_hi, 1)
                act.activation(sq2[:], x1[:], ACT.Square).then_inc(x1_sq, 1)

            GB = 4 * (I_OUT - 1)

            def ffn_gain(c, f, p, q):
                return GB + c * (8 * FC) + f * 8 + (4 * p + q + 1)

            with act.Fori(0, KT - 1) as n:
                out_tile(n, lambda q: hi(n + (I_OUT + 1), q))
            out_tile(KT - 1, lambda q: hi(I_FFN, q, gain=GB + q + 1))
            act.wait_ge(r2_in, 1)
            act.activation(rstd[:], rstd[:], ACT.Sqrt).then_inc(r2_ok, 1)

            def up(c, f, i, nxt):
                for q in range(4):
                    hi(i + 1, q, gain=ffn_gain(c, f, 1, q))
                act.wait_ge(tile_read, i + 2)
                act.activation(sact[:], gact[:], ACT.Sigmoid).then_inc(s_ok, 1)
                for q in range(4):
                    nxt(q)
                act.wait_ge(tile_read, i + 3)
                act.activation(hhi[:, ds(f * 2, 2), :], hf[:], ACT.Copy).then_inc(h_hi, 1)

            def up_phase(c, i0):
                with act.Fori(0, FC - 1) as f:
                    up(c, f, i0 + f * 2, lambda q: hi(i0 + f * 2 + 2, q, gain=ffn_gain(c, f + 1, 0, q)))
                i = i0 + 2 * (FC - 1)
                up(c, FC - 1, i, lambda q: hi(i + 2, q, K_DOWN))

            with act.Fori(0, NCH - 1) as c:
                i0 = c * PER_CH + I_FFN
                up_phase(c, i0)
                with act.Fori(0, KT - 1) as n:
                    for q in range(4):
                        hi(i0 + n + (2 * FC + 1), q, K_DOWN)
                for q in range(4):
                    hi(i0 + PER_CH, q, gain=ffn_gain(c + 1, 0, 0, q))
            c, i0 = NCH - 1, I_FFN + (NCH - 1) * PER_CH
            up_phase(c, i0)

            def last_down(n, p, nxt=None):
                if nxt:
                    for q in range(4):
                        nxt(q)
                act.wait_ge(tile_read, n + (i1 + 2))
                act.activation(sqf[:], zf[:, p], ACT.Square).then_inc(z_sq, 1)

            def put(n, p):
                act.wait_ge(out_t, n + 1)
                for b in range(2):
                    ins = act.activation(otok[:, 3 * b:3 * b + 3, ds(n * P, P)],
                                         ps[0:XTW, 4 + 2 * p + b, 0:3 * P].rearrange("p (c f) -> p c f", f=P),
                                         ACT.Copy)
                ins.then_inc(out_read, 1)

            i1 = i0 + 2 * FC
            last_down(0, 0, lambda q: hi(i1 + 1, q, K_DOWN))
            last_down(1, 1, lambda q: hi(i1 + 2, q, K_DOWN))
            put(0, 0)
            last_down(2, 0, lambda q: hi(i1 + 3, q, K_DOWN))
            with act.Fori(1, KT // 2 - 1) as m:
                last_down(m * 2 + 1, 1, lambda q: hi(m * 2 + (i1 + 2), q, K_DOWN))
                put(m * 2 - 1, 1)
                last_down(m * 2 + 2, 0, lambda q: hi(m * 2 + (i1 + 3), q, K_DOWN))
                put(m * 2, 0)
            last_down(KT - 1, 1)
            put(KT - 3, 1)
            put(KT - 2, 0)
            put(KT - 1, 1)
            act.wait_ge(rf_in, 1)
            act.activation(ss_col[0:XTW, :], ss_col[0:XTW, :], ACT.Sqrt).then_inc(rf_ok, 1)
            act.wait_ge(rf_ok, 1)
            for t in range(1, XT, 2):
                act.mul(otok[:, t, :], otok[:, t, :], ss_col[0:XTW, t:t + 1]).then_inc(ya_ready, 1)
            act.wait_ge(small_out, 16 * 6)

        @block.gpsimd
        def _(pool):
            pool.memset(ident[:], 0.0).then_inc(ident_ok, 1)
            pool.wait_ge(ident_ok, 1)
            pool.affine_select(out=ident[:], in_=ident[:], compare_op=ALU.not_equal, fill=1.0, base=0,
                               pattern=[[-1, P]], channel_multiplier=1).then_inc(ident_ok, 1)
            for h in range(H):
                pool.wait_ge(w_exp, h + 1)
                wp = wgt[:, 0:NC, :]
                pool.affine_select(out=wp, in_=wp, compare_op=ALU.is_ge, fill=0.0, base=0,
                                   pattern=[[0, NC], [1, CH]], channel_multiplier=-1)
                ws = wgt[0:SW, NC, 0:SW].rearrange("p (b t) -> p b t", t=TS)
                pool.affine_select(out=ws, in_=ws, compare_op=ALU.is_ge, fill=0.0, base=0,
                                   pattern=[[TS, NB], [1, TS]], channel_multiplier=-1).then_inc(pool_chain, 1)
                pool.wait_ge(pool_chain, h + 1)
                pool.affine_select(out=ws, in_=ws, compare_op=ALU.is_ge, fill=0.0, base=0,
                                   pattern=[[-TS, NB], [0, TS]], channel_multiplier=1).then_inc(w_masked, 1)

        @block.vector
        def _(dve):
            chain = Chain(dve, dve_chain)
            LINKS = {"head": 32, "up": 2, "chunk": 2 * FC}
            link = chain.link
            tt, ts, stt = dve.tensor_tensor, dve.tensor_scalar, dve.scalar_tensor_tensor

            def gain(i, q, col):
                dve.wait_ge(raw_in[q // 2], i * 16)
                w = wraw[:, q // 2, 4 * (q % 2):4 * (q % 2) + 4, :]
                g = vecs[:, col + 4 * q:col + 4 * q + 4].unsqueeze(2).to_broadcast([P, 4, P])
                tt(w, w, g, ALU.mult).then_inc(gained, 1)

            def low(i, q, sizes=K_FULL):
                s0, n = sum(sizes[2 * (q // 2):q]), sizes[q]
                dve.wait_ge(hi_done, 4 * (i - 1) + q + 1)
                tt(wlo[:, q, 0:n, :], wraw[:, q // 2, s0:s0 + n, :], whi[:, q, 0:n, :].bitcast(F32),
                   ALU.subtract).then_inc(lo_done, 1)

            def split(i, q, col=None, sizes=K_FULL):
                if col is not None:
                    if q == 0:
                        gain(i, 0, col)
                    if q < 3:
                        gain(i, q + 1, col)
                low(i, q, sizes)

            def tile_done(i):
                dve.wait_ge(w_used, 4 * i + 4)

            def to_rms(out, total, n):
                link(ts(out, total, 1.0 / n, EPS, ALU.mult, ALU.add))

            link(dve.memset(gw[:].bitcast(F32), 0.0))
            dve.memset(ones[:], 1.0).then_inc(const_ok, 1)
            dve.memset(rows[:], 0.0)
            dve.memset(ssq_c[:], 0.0)
            dve.wait_ge(vec_t, 1)
            dve.tensor_copy(vecs[:], ps[:, 6, 0:P]).then_inc(vec_ok, 1)
            dve.wait_ge(vec_ok, 1)
            dve.wait_ge(sc_t, 1)
            dve.tensor_copy(conv_state[:], ps[:, 7, 0:P].rearrange("p (g r) -> p g r", r=16)).then_inc(tile_read, 1)
            g1 = vecs[:, V_G1:V_G1 + KT].unsqueeze(2).to_broadcast([P, KT, 2 * H])
            tt(gw_raw[:], gw_raw[:], g1, ALU.mult).then_inc(gw_g, 1)
            for k in range(KT):
                p0 = 2 * ((k + 1) % 3)
                dve.wait_ge(x_hi, k + 1)
                ins = tt(xlo[:, 2 * k:2 * k + 2, :], ps[:, p0:p0 + 2, 0:HT],
                         xhi[:, 2 * k:2 * k + 2, :].bitcast(F32), ALU.subtract)
                ins.then_inc(x_lo, 1)
            dve.wait_ge(gw_hi, 1)
            tt(gw[:, :, 2 * H:4 * H], gw_raw[:], gw[:, :, 0:2 * H].bitcast(F32), ALU.subtract).then_inc(gw_lo, 1)
            for q in range(4):
                split(1, q, V_G1)
            dve.wait_ge(ss_ok, XT)
            for t in range(XT):
                ins = ts(diag[:, t, :], ident[0:XTW, 0:XTW], ss_col[0:XTW, t:t + 1], None, ALU.mult)
            ins.then_inc(diag_ok, 1)
            dve.wait_ge(rb_mm, 1)
            to_rms(rstd[:], side_halves(6), D)
            dve.reciprocal(rstd[:], rstd[:]).then_inc(rb_rec, 1)
            dve.wait_ge(rstd_ok, 1)
            tile_done(0)
            tt(zg[:], pair(0)[0:4 * H], rstd[0:4 * H], ALU.mult).then_inc(tile_read, 1)
            tt(gsel[:], ident[0:4 * H, 0:2 * H], ident[0:4 * H, 2 * H:4 * H], ALU.add).then_inc(gsel_ok, 1)
            dve.memset(vt[:, :, DV:DV + 1], 1.0)
            dve.memset(mprev[:, 0:1], 0.0)
            dve.tensor_copy(mprev[:, NC:NC + NB], m0[:])
            r = row
            link(dve.memset(r["mask"][:], 1.0))
            dve.memset(r["mask"][:, 0:TP:CH], 0.0)
            link(dve.memset(r["mask"][:, TP:T:TS], 0.0))
            dve.wait_ge(gate_mm, 1)
            link(ts(r["li"][:], side(BLK_A)[0:H], gate_bias[:, 0:1], None, ALU.add))
            link(ts(r["f"][:], side(BLK_B)[0:H], gate_bias[:, 1:2], None, ALU.add))
            stt(r["ax"][:], r["f"][:], -1.0, r["f"][:], ALU.mult, ALU.max).then_inc(ax_ok, 1)
            dve.wait_ge(e_ok, 1)
            ts(r["u"][:], r["e"][:], 1.0, None, ALU.add).then_inc(u_ok, 1)
            dve.wait_ge(u_ok, 1)
            link(ts(r["d"][:], r["u"][:], 1.0, None, ALU.subtract))
            link(ts(r["z"][:], r["d"][:], 0.0, None, ALU.is_equal))
            link(tt(r["d"][:], r["d"][:], r["z"][:], ALU.add))
            link(dve.reciprocal(r["rec"][:], r["d"][:]))
            link(tt(r["rec"][:], r["rec"][:], r["e"][:], ALU.mult))
            dve.wait_ge(ln_ok, 1)
            link(tt(r["z"][:], r["z"][:], r["ln"][:], ALU.add))
            link(tt(r["z"][:], r["z"][:], r["rec"][:], ALU.mult))
            link(stt(r["lf"][:], r["f"][:], 0.0, r["z"][:], ALU.min, ALU.subtract))
            dve.tensor_tensor_scan(r["b"][:], r["mask"][:], r["lf"][:], 0.0, ALU.mult, ALU.add)
            ins = dve.tensor_tensor_scan(r["m"][:, 0:TP], r["lf"][:, 0:TP], r["li"][:, 0:TP], 0.0, ALU.add, ALU.max)
            for b in range(NB):
                s = slice(TP + b * TS, TP + (b + 1) * TS)
                ins = dve.tensor_tensor_scan(r["m"][:, s], r["lf"][:, s], r["li"][:, s], m0[:, b:b + 1],
                                             ALU.add, ALU.max)
            ins.then_inc(m_ok, 1)
            dve.wait_ge(m_ok, 1)
            dve.tensor_copy(m_out[:, 0:1], r["m"][:, TP - 1:TP])
            dve.tensor_copy(m_out[:, 1:1 + NB], r["m"][:, TP + TS - 1:T:TS])
            dve.tensor_copy(mprev[:, 1:NC], r["m"][:, CH - 1:TP - 1:CH])
            tt(r["l"][:], r["li"][:], r["b"][:], ALU.subtract).then_inc(l_ok, 1)
            tt(rows[0:H, :], r["b"][:], r["m"][:], ALU.subtract).then_inc(row_a_ok, 1)
            dve.wait_ge(row_a_ok, 1)
            tt(r["pre"][:, 0:TP].rearrange("p (c t) -> p c t", t=CH), rows[0:H, 0:TP].rearrange("p (c t) -> p c t", t=CH),
               mprev[:, 0:NC].unsqueeze(2).to_broadcast([H, NC, CH]), ALU.add)
            tt(r["pre"][:, TP:T].rearrange("p (b t) -> p b t", t=TS), rows[0:H, TP:T].rearrange("p (b t) -> p b t", t=TS),
               mprev[:, NC:].unsqueeze(2).to_broadcast([H, NB, TS]), ALU.add).then_inc(pre_ok, 1)
            dve.wait_ge(l_t, 1)
            dve.tensor_copy(colall[:, 0:NC, :], ps[:, BLK_A, 0:NC * H].rearrange("p (c h) -> p c h", h=H))
            link(dve.tensor_copy(colall[0:SW, NC, :], ps[0:SW, BLK_A, NC * H:(NC + 1) * H]))

            def round_of_head(h, last):
                i = h * TILES_H + 1
                hv = h + 1

                def quarter(j, q):
                    n = i + (j + 1)
                    if last and j == TILES_H - 1:
                        split(n, q)
                    else:
                        split(n, q, V_G1)

                def done(j):
                    tile_done(i + j)

                def evac(ins):
                    ins.then_inc(tile_read, 1)

                quarter(0, 0)
                for s in range(3):
                    dve.tensor_copy(sel[:, s, :], ident[:, ds(h + 32 * s, 1)].to_broadcast([P, P]))
                dve.tensor_copy(gml[:], vecs[:, ds(h * 2 + (V_MIX + NG), 2)])
                dve.tensor_copy(colh[:, 0:NC], colall[:, 0:NC, ds(h, 1)].rearrange("p c h -> p (c h)"))
                dve.tensor_copy(colh[0:SW, NC:NC + 1], colall[0:SW, NC, ds(h, 1)]).then_inc(sel_ok, 1)
                quarter(0, 1)
                quarter(0, 2)
                done(0)
                evac(stt(qf[:], pair(1), QS, rstd[:], ALU.mult, ALU.mult))
                quarter(0, 3)
                quarter(1, 0)
                dve.wait_ge(bc_b, hv)
                dve.wait_ge(tile_read, i + 2)
                bb = side(BLK_B)
                tt(qa[:], flat(qf), bb, ALU.mult)
                dve.tensor_copy(sc[:, 0:NC], bb[:, CH - 1:TP:CH])
                dve.tensor_copy(sc[:, NC:], bb[:, TP + TS - 1:T:TS]).then_inc(b_read, 1)
                quarter(1, 1)
                quarter(1, 2)
                done(1)
                evac(tt(kf[:], pair(2), rstd[:], ALU.mult))
                quarter(1, 3)
                quarter(2, 0)
                dve.wait_ge(bc_c, hv)
                dve.tensor_copy(em[:], side(BLK_A)).then_inc(c_read, 1)
                quarter(2, 1)
                quarter(2, 2)
                done(2)
                evac(tt(v0f[:], pair(3), rstd[:], ALU.mult))
                quarter(2, 3)
                quarter(3, 0)
                dve.wait_ge(k_s_mm, hv)
                dve.wait_ge(w_masked, hv)
                for c in range(NC):
                    ts(kt[:, c, :], ps[:, BLK_B, c * P:(c + 1) * P], wgt[:, c, CH - 1:CH], None, ALU.mult)
                dve.tensor_copy(wlast[:], wgt[0:SW, NC, TS - 1:SW:TS])
                dve.tensor_copy(kt[0:SW, NC, :], ps[0:SW, BLK_B + 1, 0:P]).then_inc(kt_ok, 1)
                quarter(3, 1)
                dve.wait_ge(kt_ok, hv)
                tt(wgt[:, 0:NC, :], ps[:, BLK_A, :].rearrange("p (c t) -> p c t", t=CH), wgt[:, 0:NC, :], ALU.mult)
                tt(wgt[0:SW, NC, 0:SW], ps[0:SW, BLK_A + 1, 0:SW], wgt[0:SW, NC, 0:SW], ALU.mult).then_inc(p_ok, 1)
                quarter(3, 2)
                done(3)
                evac(tt(v1f[:], pair(4), rstd[:], ALU.mult))
                quarter(3, 3)

                def v_evac(half, bank, ok):
                    cols = slice(half * P, (half + 1) * P)
                    dve.tensor_copy(vt[:, 0:NC, cols], ps[:, bank, :].rearrange("p (c v) -> p c v", v=P))
                    dve.tensor_copy(vt[0:SW, NC, cols], ps[0:SW, bank + 1, 0:P]).then_inc(ok, 1)

                quarter(4, 0)
                dve.wait_ge(v0_t, hv)
                v_evac(0, BLK_B, v0_ok)
                quarter(4, 1)
                quarter(4, 2)
                done(4)
                evac(tt(so[:, 0], pair(5), rstd[:], ALU.mult))
                quarter(4, 3)
                quarter(5, 0)
                dve.wait_ge(v1_t, hv)
                v_evac(1, BLK_A, v1_ok)
                quarter(5, 1)
                quarter(5, 2)
                done(5)
                evac(tt(so[:, 1], pair(6), rstd[:], ALU.mult))
                quarter(5, 3)

                def sum_squares():
                    tt(ssq_c[:], ssq_c[:], sqy[:], ALU.add).then_inc(ssc_ok, 1)

                def conv_columns(g):
                    for w in range(CW):
                        dve.tensor_copy(taps[:, w:w + 1], vecs[:, ds(h * 2 + (V_CW + w * NG + g), 1)])
                    link(dve.tensor_copy(cstate[:], conv_state[:, ds(h * 2 + g, 1), :].rearrange("p g r -> p (g r)")))

                def conv_gate(j):
                    done(j)
                    evac(tt(cg[:], pair(1 + j), rstd[:], ALU.mult))
                    dve.wait_ge(tile_read, i + (j + 2))
                    link(tt(cg[:], cg[:], rstd[:], ALU.mult))

                uf, cf = flat(u), flat(cv)
                us = uf[:, TP:T].rearrange("p (b t) -> p b t", t=TS)
                cvs = cf[:, TP:T].rearrange("p (b t) -> p b t", t=TS)
                st = cstate.rearrange("p (b r) -> p b r", r=2)

                def add_tap(dst, src, w):
                    link(stt(dst, src, taps[:, w:w + 1], dst, ALU.mult, ALU.add))

                def conv_input(j):
                    done(j)
                    evac(tt(u[:], pair(1 + j), cg[:], ALU.mult))
                    dve.wait_ge(tile_read, i + (j + 2))

                def conv_sum(g):
                    link(ts(cf, uf, taps[:, 2:3], None, ALU.mult))
                    add_tap(cf[:, 1:TP], uf[:, 0:TP - 1], 1)
                    add_tap(cf[:, 2:TP], uf[:, 0:TP - 2], 0)
                    add_tap(cvs[:, :, 1:TS], us[:, :, 0:TS - 1], 1)
                    add_tap(cvs[:, :, 0:1], st[:, :, 1:2], 1)
                    add_tap(cvs[:, :, 2:TS], us[:, :, 0:TS - 2], 0)
                    add_tap(cvs[:, :, 0:2], st, 0)
                    dve.tensor_copy(tails[:, ds(h * 2 + g, 1), 0:2], uf[:, TP - 2:TP].unsqueeze(1))
                    dve.tensor_copy(tails[:, ds(h * 2 + g, 1), 2:].rearrange("p g (b r) -> p (g b) r", r=2),
                                    us[:, :, TS - 2:TS])
                    link(tt(cv[:], cv[:], rstd[:], ALU.mult))

                def conv_out(j, g):
                    done(j)
                    evac(tt(mixf[:, ds(h * 4 + 2 * g, 2), :], pair(1 + j), cv[:], ALU.mult))

                quarter(6, 0)
                conv_columns(0)
                dve.wait_ge(u_mm, hv)
                link(dve.tensor_copy(cst[:, 0, :], ps[:, 4, 0:DV + 1]))
                for c in range(1, NC):
                    link(stt(cst[:, c, :], cst[:, c - 1, :], sc[:, c:c + 1], ps[:, 4 + c, 0:DV + 1],
                             ALU.mult, ALU.add))
                quarter(6, 1)
                n_old = vecs[:, V_N:V_N + NB * H].rearrange("p (b h) -> p b h", h=H)[:, :, ds(h, 1)]
                n_new = n_out[:, 0:NB * H].rearrange("p (b h) -> p b h", h=H)[:, :, ds(h, 1)]
                qs3 = qa[:, TP:T].rearrange("p (b t) -> p b t", t=TS)
                tt(qn[:, TP:T].rearrange("p (b t) -> p b t", t=TS), qs3, n_old.to_broadcast([P, NB, TS]), ALU.mult)
                link(tt(n_new, n_old, sc[:, NC:].unsqueeze(2), ALU.mult))
                link(tt(n_new, n_new, ps[:, 4, 300:300 + NB].unsqueeze(2), ALU.add))
                dve.tensor_copy(n_out[:, ds(h + NB * H, 1)], cst[:, NC - 1, DV:DV + 1])
                for c in range(1, NC):
                    ins = ts(qn[:, c * CH:(c + 1) * CH], qa[:, c * CH:(c + 1) * CH], cst[:, c - 1, DV:DV + 1],
                             None, ALU.mult)
                ins.then_inc(state_ok, 1)
                quarter(6, 2)
                for b in range(NB):
                    ts(vb[:, b, :], vt[0:SW, NC, 0:DV], wlast[:, b:b + 1], None, ALU.mult)
                conv_gate(6)
                quarter(6, 3)
                quarter(7, 0)
                dve.wait_ge(num_mm, hv)
                den_p, den_s = ps[:, 6, :], ps[:, 7, 2 * SW:3 * SW]
                stt(em[:, 0:TP], den_p, -1.0, em[:, 0:TP], ALU.mult, ALU.max)
                link(stt(em[:, TP:T], den_s, -1.0, em[:, TP:T], ALU.mult, ALU.max))
                tt(em[:, 0:TP], den_p, em[:, 0:TP], ALU.max)
                link(tt(em[:, TP:T], den_s, em[:, TP:T], ALU.max))
                dve.reciprocal(em[:, 0:HT], em[:, 0:HT])
                quarter(7, 1)
                link(dve.reciprocal(em[:, HT:T], em[:, HT:T]))
                for j, hh in ((0, flat(h0)), (1, flat(h1))):
                    tt(hh[:, 0:TP], ps[:, 4 + j, :], em[:, 0:TP], ALU.mult)
                    ins = tt(hh[:, TP:T], ps[:, 7, j * SW:(j + 1) * SW], em[:, TP:T], ALU.mult)
                ins.then_inc(h_ok, 1)
                quarter(7, 2)
                conv_input(7)
                quarter(7, 3)
                quarter(8, 0)
                dve.wait_ge(us_mm, hv)
                dve.wait_ge(cs_in, h * 16 + 16)
                for b in range(NB):
                    ins = stt(cs[:, b, :], cs[:, b, :], sc[:, NC + b:NC + b + 1],
                              ps[:, 4 + b // 2, (b % 2) * DV:(b % 2 + 1) * DV], ALU.mult, ALU.add)
                ins.then_inc(cs_ok, 1)
                quarter(8, 1)
                conv_sum(0)
                quarter(8, 2)
                conv_out(8, 0)
                quarter(8, 3)
                quarter(9, 0)
                conv_columns(1)
                dve.wait_ge(hs_mm, hv)
                to_rms(rh[:], side_halves(BLK_A), DV)
                dve.reciprocal(rh[:, 0, :], rh[:, 0, :])
                quarter(9, 1)
                dve.reciprocal(rh[:, 1, :], rh[:, 1, :]).then_inc(rh_in, 1)
                dve.wait_ge(ysq_ok, 2 * h + 1)
                sum_squares()
                quarter(9, 2)
                conv_gate(9)
                quarter(9, 3)
                quarter(10, 0)
                dve.wait_ge(rh_ok, hv)
                dve.wait_ge(so_ok, 2 * h + 2)
                for j, hh in ((0, h0), (1, h1)):
                    link(stt(hh[:], hh[:], gml[:, j:j + 1], rh[:], ALU.mult, ALU.mult))
                    tt(mixf[:, ds(h * 4 + (2 * NG + 2 * j), 2), :], hh[:], so[:, j], ALU.mult)
                quarter(10, 1)
                quarter(10, 2)
                conv_input(10)
                quarter(10, 3)
                quarter(11, 0)
                quarter(11, 1)
                conv_sum(1)
                quarter(11, 2)
                conv_out(11, 1)
                quarter(11, 3)
                dve.wait_ge(ysq_ok, 2 * h + 2)
                sum_squares()

            LINKS_H = LINKS["head"]
            with dve.Fori(0, H - 1) as h:
                start = chain.enter(h, LINKS_H)
                round_of_head(h, False)
                chain.leave(start, H - 1, "head")
            round_of_head(H - 1, True)

            def mix_low(n):
                k = MIX_K[n]
                dve.wait_ge(mix_hi, n + 1)
                tt(mixlo[:, 2 * k:2 * k + 2, :], mixf[:, 2 * k:2 * k + 2, :],
                   mixhi[:, 2 * k:2 * k + 2, :].bitcast(F32), ALU.subtract).then_inc(mix_lo, 1)

            mix_low(0)
            dve.wait_ge(ssc_mm, 1)
            to_rms(rh[:], side_halves(BLK_A), DC)
            dve.reciprocal(rh[:, 0, :], rh[:, 0, :])
            mix_low(1)
            mix_low(2)
            dve.reciprocal(rh[:, 1, :], rh[:, 1, :]).then_inc(rc_in, 1)
            for n in range(3, NG):
                mix_low(n)
            dve.wait_ge(rc_ok, 1)
            for g in range(NG):
                y = mixf[:, 2 * g:2 * g + 2, :]
                stt(y, y, vecs[:, V_MIX + g:V_MIX + g + 1], rh[:], ALU.mult, ALU.mult).then_inc(mix_f, 1)
                if g:
                    mix_low(NG + g - 1)
            mix_low(KT - 1)
            dve.tensor_copy(n_rows[:], ps[0:(NB + 1) * H, BLK_A + 1, 384:384 + P])
            dve.wait_ge(tail_mm, 1)
            dve.tensor_copy(conv_rows[:], side(BLK_B, DC)[0:2 + 2 * NB]).then_inc(rows_out, 1)
            link(dve.memset(ssq2[:], 0.0))

            def out_tile(n, parity, nxt):
                i = n + I_OUT
                x_n = ds(n * 2, 2)
                for q in range(3):
                    nxt(q)
                tile_done(i)
                tt(t2[:], pair(parity), xhi[:, x_n, :].bitcast(F32), ALU.add).then_inc(tile_read, 1)
                dve.wait_ge(tile_read, i + 2)
                tt(x1[:], t2[:], xlo[:, x_n, :].bitcast(F32), ALU.add).then_inc(x1_ok, 1)
                nxt(3)
                dve.wait_ge(x1_hi, n + 1)
                tt(xlo[:, x_n, :], x1[:], xhi[:, x_n, :].bitcast(F32), ALU.subtract).then_inc(x1_lo, 1)
                dve.wait_ge(x1_sq, n + 1)
                tt(ssq2[:], ssq2[:], sq2[:], ALU.add).then_inc(ss2_ok, 1)
                dve.wait_ge(ss2_ok, n + 1)

            with dve.Fori(0, KT // 2 - 1) as n2:
                for p in range(2):
                    n = n2 * 2 + p
                    out_tile(n, I_OUT + p, lambda q: split(n + (I_OUT + 1), q))
            out_tile(KT - 2, I_OUT, lambda q: split(I_OUT + KT - 1, q))
            out_tile(KT - 1, I_OUT + 1, lambda q: split(I_FFN, q, V_G2))
            dve.wait_ge(ss2_mm, 1)
            to_rms(rstd[:], side_halves(BLK_A), D)
            dve.reciprocal(rstd[:], rstd[:]).then_inc(r2_in, 1)
            dve.wait_ge(r2_ok, 1)

            def up(c, f, i, nxt):
                for q in range(3):
                    split(i + 1, q, V_G2)
                tile_done(i)
                tt(gact[:], pair(I_FFN), rstd[:], ALU.mult).then_inc(tile_read, 1)
                split(i + 1, 3, V_G2)
                nxt(0)
                dve.wait_ge(s_ok, c * FC + (f + 1))
                link(tt(sact[:], sact[:], gact[:], ALU.mult))
                link(tt(sact[:], sact[:], rstd[:], ALU.mult))
                nxt(1)
                nxt(2)
                tile_done(i + 1)
                tt(hf[:], pair(I_FFN + 1), sact[:], ALU.mult).then_inc(tile_read, 1)
                nxt(3)
                dve.wait_ge(h_hi, c * FC + (f + 1))
                f_n = ds(f * 2, 2)
                tt(hlo[:, f_n, :], hf[:], hhi[:, f_n, :].bitcast(F32), ALU.subtract).then_inc(h_lo, 1)

            def up_phase(c, i0, what):
                with dve.Fori(0, FC - 1) as f:
                    start = chain.enter(f, LINKS["up"])
                    up(c, f, i0 + f * 2, lambda q: split(i0 + f * 2 + 2, q, V_G2))
                    chain.leave(start, FC - 1, "up")
                i = i0 + 2 * (FC - 1)
                up(c, FC - 1, i, lambda q: split(i + 2, q, sizes=K_DOWN))

            def down(n, i, parity, first, nxt):
                for q in range(3):
                    nxt(q)
                tile_done(i)
                a = acc[:, ds(n * 2, 2), :]
                if first:
                    tt(gact[:], pair(parity), xhi[:, ds(n * 2, 2), :].bitcast(F32), ALU.add).then_inc(tile_read, 1)
                    dve.wait_ge(tile_read, i + 2)
                    tt(a, gact[:], xlo[:, ds(n * 2, 2), :].bitcast(F32), ALU.add)
                else:
                    tt(a, pair(parity), a, ALU.add).then_inc(tile_read, 1)
                nxt(3)

            def chunk(c, first):
                i0 = c * PER_CH + I_FFN
                up_phase(c, i0, "up")
                i1 = i0 + 2 * FC
                with dve.Fori(0, KT // 2 - 1) as n2:
                    for p in range(2):
                        down(n2 * 2 + p, i1 + n2 * 2 + p, I_FFN + p, first,
                             lambda q: split(i1 + n2 * 2 + (p + 1), q, sizes=K_DOWN))
                down(KT - 2, i1 + (KT - 2), I_FFN, first, lambda q: split(i1 + (KT - 1), q, sizes=K_DOWN))
                down(KT - 1, i1 + (KT - 1), I_FFN + 1, first, lambda q: split(i0 + PER_CH, q, V_G2))

            dve.wait_ge(small_out, 16 * 6)
            chunk(0, True)
            with dve.Fori(1, NCH - 1) as c:
                start = chain.enter(c - 1, LINKS["chunk"])
                chunk(c, False)
                chain.leave(start, NCH - 2, "chunk")
            c, i0 = NCH - 1, I_FFN + (NCH - 1) * PER_CH
            i1 = i0 + 2 * FC
            up_phase(c, i0, "up")
            link(dve.memset(ssq_f[:], 0.0))

            def last_down(n, p, nxt=None):
                if nxt:
                    for q in range(3):
                        nxt(q)
                tile_done(n + i1)
                tt(zf[:, p], pair(I_FFN + p), acc[:, ds(n * 2, 2), :], ALU.add).then_inc(tile_read, 1)
                dve.wait_ge(tile_read, n + (i1 + 2))
                if not (isinstance(n, int) and n < 2):
                    dve.wait_ge(out_t, n - 1)
                ts(zgn[:, p], zf[:, p], vecs[:, ds(n + V_GF, 1)], None, ALU.mult).then_inc(zg_n, 1)
                if nxt:
                    nxt(3)
                dve.wait_ge(z_sq, n + 1)
                tt(ssq_f[:], ssq_f[:], sqf[:], ALU.add).then_inc(ssf_ok, 1)
                dve.wait_ge(ssf_ok, n + 1)

            for n in range(2):
                last_down(n, n, lambda q: split(i1 + n + 1, q, sizes=K_DOWN))
            with dve.Fori(1, KT // 2 - 1) as m:
                for p in range(2):
                    last_down(m * 2 + p, p, lambda q: split(m * 2 + (i1 + p + 1), q, sizes=K_DOWN))
            last_down(KT - 2, 0, lambda q: split(i1 + KT - 1, q, sizes=K_DOWN))
            last_down(KT - 1, 1)
            dve.wait_ge(rf_mm, 1)
            to_rms(ss_col[0:XTW, :], ps[0:XTW, 0, 0:XT], D)
            dve.reciprocal(ss_col[0:XTW, :], ss_col[0:XTW, :]).then_inc(rf_in, 1)
            dve.wait_ge(rf_ok, 1)
            dve.wait_ge(out_read, KT)
            for t in range(0, XT, 2):
                ts(otok[:, t, :], otok[:, t, :], ss_col[0:XTW, t:t + 1], None, ALU.mult).then_inc(yd_ready, 1)


_INS = ["x_prompt", "x_sample", "state_conv", "state_mlstm_C", "state_mlstm_n", "state_mlstm_m",
        "norm1_g", "w_in", "b_igate", "b_fgate", "conv_w", "conv_out_g", "mlstm_out_g", "w_out",
        "norm2_g", "w_ffn_gate", "w_ffn_up", "w_ffn_down", "final_norm_g"]


def kernel(**inputs):
    import numpy as _np
    import concourse.bacc as _bacc
    from concourse import mybir as _mybir
    from concourse.bass_utils import run_bass_kernel_spmd as _run

    xp, xs = inputs["x_prompt"].shape, inputs["x_sample"].shape
    _, nb, heads, dk, dv = inputs["state_mlstm_C"].shape
    taps, dc = inputs["conv_w"].shape[1:]
    out_shapes = [xp, xs, (1, 1, taps - 1, dc), (1, 1, heads, dk, dv), (1, 1, heads, dk), (1, 1, heads),
                  (1, nb, taps - 1, dc), (1, nb, heads, dk, dv), (1, nb, heads, dk), (1, nb, heads)]
    nc = _bacc.Bacc("TRN2", target_bir_lowering=False, num_devices=1)
    arrays, args = {}, []
    for name in _INS:
        a = _np.ascontiguousarray(inputs[name])
        arrays[f"in_{name}_dram"] = a
        args.append(nc.dram_tensor(f"in_{name}_dram", a.shape, _mybir.dt.from_np(a.dtype), kind="ExternalInput").ap())
    for i, shape in enumerate(out_shapes):
        args.append(nc.dram_tensor(f"out_{i}_dram", shape, _mybir.dt.float32, kind="ExternalOutput").ap())
    hybrid_trunk_step(nc, *args)
    r = _run(nc, [arrays], core_ids=[0])
    return tuple(r.results[0][f"out_{i}_dram"] for i in range(len(out_shapes)))
```

```python
from contextlib import ExitStack

import concourse.bass as bass
from concourse import mybir

P = 128
ALU = mybir.AluOpType
ACT = mybir.ActivationFunctionType
F32 = mybir.dt.float32
F32R = mybir.dt.float32r
EPS = 1e-6
XTW = 96
BLK_A, BLK_B = 4, 6
ds = bass.ds


class Chain:

    def __init__(self, eng, sem):
        self.eng, self.sem, self.n, self.terms = eng, sem, 0, []

    def value(self):
        v = self.n
        for reg, per in self.terms:
            v = reg * per + v
        return v

    def link(self, ins):
        ins.then_inc(self.sem, 1)
        self.n += 1
        self.eng.wait_ge(self.sem, self.value())

    def enter(self, reg, per):
        self.terms.append((reg, per))
        return self.n

    def leave(self, start, times, what):
        _, per = self.terms.pop()
        assert self.n - start == per, f"{what}: {self.n - start} links in a round"
        self.n = start + per * times


def hybrid_trunk_step(nc, x_prompt, x_sample, state_conv, state_C, state_n, state_m, norm1_g, w_in,
                      b_igate, b_fgate, conv_w, conv_out_g, mlstm_out_g, w_out, norm2_g, w_gate,
                      w_up, w_down, final_g, y_prompt, y_sample, p_conv, p_C, p_n, p_m,
                      s_conv, s_C, s_n, s_m):
    TP, D = x_prompt.shape[1], x_prompt.shape[2]
    NB, TS = x_sample.shape[0], x_sample.shape[1]
    T = TP + NB * TS
    HT = T // 2
    KT = D // P
    H, DK, DV = state_C.shape[2:]
    CW, DC = conv_w.shape[1:]
    NG = DC // P
    GH = NG // H
    FF = w_gate.shape[2]
    FT = FF // P
    NCH = 4
    FC = FT // NCH
    CH = P
    NC = TP // CH
    SW = T - TP
    XT = T // XTW
    assert T % (2 * XTW) == 0 and DK == P and DV == 2 * P and FC * NCH == FT and GH == 2
    assert DC == KT * P // 2 and H * DV == DC and SW == 64 and NC * CH == TP and CW == 3
    COL_B, COL_C, COL_X = 0, DC, 2 * DC
    COL_Q = 3 * DC
    COL_K = COL_Q + H * DK
    COL_V = COL_K + H * DK
    COL_O = COL_V + H * DV
    COL_G = COL_O + H * DV
    V_G2, V_GF, V_MIX, V_CW, V_N = 0, KT, 2 * KT, 3 * KT, 3 * KT + CW * NG
    V_G1 = V_N + NB * H
    assert V_G1 + KT <= P
    TILES_H = 6 + 3 * GH
    I_OUT = 1 + H * TILES_H
    I_FFN = I_OUT + KT
    PER_CH = 2 * FC + KT
    I_END = I_FFN + NCH * PER_CH
    K_FULL = (4, 4, 4, 4)
    K_DOWN = (3, 3, 3, 2)
    assert sum(K_FULL) == KT and sum(K_DOWN) == FC
    MIX_K = tuple(range(NG, KT)) + tuple(range(NG))
    X_PIECES = ((0, 2), (2, 2), (4, 4), (8, 4), (12, 4))
    SMALLS = 10
    SQ_ACT = 4
    assert sum(n for _, n in X_PIECES) == KT
    QS = float(DK) ** -0.5

    with ExitStack() as ctx:
        sem = lambda name: ctx.enter_context(nc.semaphore(name))
        used = [0]
        base = nc.sbuf_base + 31 & ~31

        def at(name, shape, dt, off):
            return nc.alloc_sbuf_tensor_at(name, shape, dt, offset=base + off)

        def nbytes(shape):
            n = 4
            for s in shape[1:]:
                n *= s
            return n + 31 & ~31

        def keep(name, shape, dt=F32):
            t = at(name, shape, dt, used[0])
            used[0] += nbytes(shape)
            return t

        TOK = [P, 2, HT]
        flat = lambda t: t.rearrange("p a b -> p (a b)")
        xhi = keep("xhi", [P, 2 * KT, HT], F32R)
        xlo = keep("xlo", [P, 2 * KT, HT], F32R)
        wraw = keep("wraw", [P, 2, 8, P])
        whi = keep("whi", [P, 4, 4, P], F32R)
        wlo = keep("wlo", [P, 4, 4, P], F32R)
        ident = keep("ident", [P, P])
        ones = keep("ones", [P, P])
        vecs = keep("vecs", [P, P])
        conv_state = keep("conv_state", [P, NG, 16])
        rstd = keep("rstd", TOK)
        tails = keep("tails", [P, NG, 2 + 2 * NB])
        n_out = keep("n_out", [P, (NB + 1) * H])
        m_out = keep("m_out", [4, 1 + NB])
        m0 = keep("m0", [4, NB])
        ss_col = keep("ss_col", [P, XT])
        rstd_col = keep("rstd_col", [P, XT])
        R0 = used[0]
        XB = KT * T * 4

        def region(start):
            pos = [R0 + start]

            def take(name, shape, dt=F32):
                t = at(name, shape, dt, pos[0])
                pos[0] += nbytes(shape)
                assert base + pos[0] <= nc.sbuf_usable_end, (name, base + pos[0])
                return t
            take.pos = pos
            return take

        take = region(0)
        xtok = take("xtok", [XTW, XT, D])
        vrows = take("vrows", [V_G1, P])
        g1_rows = take("g1_rows", [KT, P])
        srows = take("srows", [2 * NB, DC])
        gw_raw = take("gw_raw", [P, KT, 2 * H])
        gw = take("gw", [P, KT, P], F32R)
        diag = take("diag", [XTW, XT, XTW])
        ss_part = take("ss_part", [XTW, XT, len(X_PIECES)])
        zg = take("zg", [4 * H, 2, HT])
        bias_c = take("bias_c", [XTW, 2 * H])
        zc = take("zc", [XTW, XT, 4 * H])
        gate = take("gate", [XTW, XT, 2 * H])
        col = {n: take("col_" + n, [XTW, XT, H]) for n in ("ax", "e", "u", "d", "z", "ln", "rec", "lf")}
        take = region(0)
        row = {n: take("row_" + n, [H, T]) for n in ("li", "lf", "mask", "b", "m", "pre", "l")}
        mprev = take("mprev", [H, NC + NB])
        take = region(0)
        mixf = take("mixf", [P, 2 * KT, HT])
        mixlo = at("mixlo", [P, 2 * KT, HT], F32R, R0)
        mixhi = at("mixhi", [P, 2 * KT, HT], F32R, R0 + XB)
        take = region(XB)
        qf = take("qf", TOK)
        kf = take("kf", TOK)
        v0f = take("v0f", TOK)
        v1f = take("v1f", TOK)
        qa = take("qa", [P, T])
        qn = take("qn", [P, T])
        vt = take("vt", [P, NC + 1, DV + 1])
        kt = take("kt", [P, NC + 1, P])
        wgt = take("wgt", [P, NC + 1, P])
        wlast = take("wlast", [SW, NB])
        cst = take("cst", [P, NC, DV + 1])
        cs = take("cs", [P, NB, DV])
        vb = take("vb", [SW, NB, DV])
        em = take("em", [P, T])
        so = take("so", [P, 2, 2, HT])
        sel = take("sel", [P, 3, P])
        sc = take("sc", [P, NC + NB])
        assert base + R0 + 2 * XB <= nc.sbuf_usable_end
        rows = take("rows", [P, T])
        colall = take("colall", [P, NC + 1, H])
        colh = take("colh", [P, NC + 1])
        taps = take("taps", [P, CW])
        cstate = take("cstate", [P, 2 * NB])
        gml = take("gml", [P, 2])
        cg_at = take.pos[0] - R0
        cg = take("cg", TOK)
        u = take("u", TOK)
        cv = take("cv", TOK)
        sqy = take("sqy", TOK)
        ssq_c = take("ssq_c", TOK)
        rh = take("rh", TOK)
        take = region(cg_at)
        conv_rows = take("conv_rows", [2 + 2 * NB, DC])
        n_rows = take("n_rows", [(NB + 1) * H, P])
        h0, h1 = v0f, v1f
        take = region(2 * XB)
        x1 = take("x1", TOK)
        sq2 = take("sq2", TOK)
        ssq2 = take("ssq2", TOK)
        t2 = take("t2", TOK)
        take = region(0)
        acc = take("acc", [P, 2 * KT, HT])
        hhi = take("hhi", [P, 2 * FC, HT], F32R)
        hlo = take("hlo", [P, 2 * FC, HT], F32R)
        gact = take("gact", TOK)
        sact = take("sact", TOK)
        hf = take("hf", TOK)
        zf = take("zf", [P, 2, 2, HT])
        zgn = take("zgn", [P, 2, 2, HT])
        sqf, ssq_f = sact, gact
        otok = at("otok", [XTW, XT, D], F32, 0)

        ps = ctx.enter_context(nc.psum_tensor("ps", [P, 8, 512], F32))
        ps_flat = ps.rearrange("p a b -> p (a b)")
        pair = lambda i: ps[:, 2 * (i % 2):2 * (i % 2) + 2, 0:HT]
        side = lambda bank, n=T: ps_flat[:, bank * 512:bank * 512 + n]
        side_halves = lambda bank: ps[:, bank:bank + 2, 0:HT]
        conv_pair = lambda i: side_halves(BLK_A + 2 * (i % 2))

        raw_in = [sem("raw_in0"), sem("raw_in1")]
        gained = sem("gained")
        halves_free = sem("halves_free")
        hi_done, lo_done = sem("hi_done"), sem("lo_done")
        w_used = sem("w_used")
        tile_read = sem("tile_read")
        x_in = [sem(f"x_in{b}") for b in range(len(X_PIECES))]
        g1_in, gw_in, small_in = sem("g1_in"), sem("gw_in"), sem("small_in")
        ident_ok, xt_done = sem("ident_ok"), sem("xt_done")
        x_hi, x_lo, g1_t, vec_t = (sem(n) for n in ("x_hi", "x_lo", "g1_t", "vec_t"))
        gw_g, gw_hi, gw_lo, ss_ok, diag_ok, rb_mm, rb_rec, rstd_c_ok = (
            sem(n) for n in ("gw_g", "gw_hi", "gw_lo", "ss_ok", "diag_ok", "rb_mm", "rb_rec", "rstd_c_ok"))
        zg_t, lf_c_ok, gates_t, row_a_ok, ax_ok, e_ok, u_ok, ln_ok, m_ok, pre_ok, l_ok, rows_ok, l_t = (
            sem(n) for n in ("zg_t", "lf_c_ok", "gates_t", "row_a_ok", "ax_ok", "e_ok", "u_ok", "ln_ok",
                             "m_ok", "pre_ok", "l_ok", "rows_ok", "l_t"))
        sel_ok, bc_mm, bc_read = (sem(n) for n in ("sel_ok", "bc_mm", "bc_read"))
        w_exp, w_masked, pool_chain = sem("w_exp"), sem("w_masked"), sem("pool_chain")
        k_s_mm, kt_ok, p_ok, v0_t, v0_ok, v1_t, v1_ok = (
            sem(n) for n in ("k_s_mm", "kt_ok", "p_ok", "v0_t", "v0_ok", "v1_t", "v1_ok"))
        u_mm, state_ok, num_mm, h_ok, us_mm, cs_ok, hsq_ok, hsum_ok, hs_mm, rh_in, rh_ok = (
            sem(n) for n in ("u_mm", "state_ok", "num_mm", "h_ok", "us_mm", "cs_ok", "hsq_ok", "hsum_ok",
                             "hs_mm", "rh_in", "rh_ok"))
        so_ok, ysq_ok, cs_in, c_out = (
            sem(n) for n in ("so_ok", "ysq_ok", "cs_in", "c_out"))
        ssc_ok, ssc_mm, rc_in, rc_ok, mix_heads, mix_hi, mix_lo = (
            sem(n) for n in ("ssc_ok", "ssc_mm", "rc_in", "rc_ok", "mix_heads", "mix_hi", "mix_lo"))
        tails_ok, tail_mm, rows_out = sem("tails_ok"), sem("tail_mm"), sem("rows_out")
        x1_ok, x1_hi, x1_sq, x1_lo, ss2_ok, ss2_mm, r2_in, r2_ok = (
            sem(n) for n in ("x1_ok", "x1_hi", "x1_sq", "x1_lo", "ss2_ok", "ss2_mm", "r2_in", "r2_ok"))
        s_ok, h_hi, h_lo = (sem(n) for n in ("s_ok", "h_hi", "h_lo"))
        zg_n, z_sq, out_t, out_read, ssf_ok, rf_mm, rf_in, rf_ok = (
            sem(n) for n in ("zg_n", "z_sq", "out_t", "out_read", "ssf_ok", "rf_mm", "rf_in",
                             "rf_ok"))
        yd_ready, ya_ready = sem("yd_ready"), sem("ya_ready")
        dve_chain, out_done, small_out = sem("dve_chain"), sem("out_done"), sem("small_out")

        by_k = lambda w: w.rearrange("l (k p) n -> p (l k) n", p=P)
        w_in_k, w_out_k, w_gate_k, w_up_k, w_down_k = map(by_k, (w_in, w_out, w_gate, w_up, w_down))
        n_dram = state_n.rearrange("l b h d -> (l b h) d")

        block = ctx.enter_context(nc.Block())

        @block.sync
        def _(sp):
            def load(i, w_k, col, k_halves, first=False):
                for half, (k0, n) in enumerate(k_halves):
                    if not first:
                        sp.wait_ge(lo_done, 4 * (i - 2) + 2 * half + 2)
                        sp.sem_inc(halves_free, 1)
                    sp.dma_start(wraw[:, half, 0:n, :], w_k[:, ds(k0, n), ds(col, P)]).then_inc(raw_in[half], 16)

            full = ((0, 8), (8, 8))
            mix_order = ((MIX_K[0], 8), (MIX_K[8], 8))
            xp = x_prompt.rearrange("l t d -> (l t) d")
            xs = x_sample.rearrange("b t d -> (b t) d")
            last = TP - (XT - 1) * XTW
            for b, (k0, n) in enumerate(X_PIECES):
                c = slice(k0 * P, (k0 + n) * P)
                sp.dma_start(xtok[:, 0:XT - 1, c],
                             xp[0:TP - last, c].rearrange("(t p) d -> p t d", p=XTW)).then_inc(x_in[b], 16)
                sp.dma_start(xtok[0:last, XT - 1, c], xp[TP - last:TP, c]).then_inc(x_in[b], 16)
                sp.dma_start(xtok[last:XTW, XT - 1, c], xs[:, c]).then_inc(x_in[b], 16)

            def head(h, first=False):
                i = h * TILES_H + 1
                cols = [h * DK + COL_Q, h * DK + COL_K, h * DV + COL_V, h * DV + (COL_V + P),
                        h * DV + COL_O, h * DV + (COL_O + P)]
                for g in range(GH):
                    cols += [h * (GH * P) + (c + g * P) for c in (COL_C, COL_X, COL_B)]
                for j, col in enumerate(cols):
                    load(i + j, w_in_k, col, full, first=first and j == 0)

            head(0, first=True)
            with sp.Fori(1, H) as h:
                head(h)
            with sp.Fori(0, KT) as n:
                load(n + I_OUT, w_out_k, n * P, mix_order)
            with sp.Fori(0, NCH) as c:
                with sp.Fori(0, FC) as f:
                    i = c * PER_CH + f * 2 + I_FFN
                    load(i, w_gate_k, c * (FC * P) + f * P, full)
                    load(i + 1, w_up_k, c * (FC * P) + f * P, full)
                with sp.Fori(0, KT) as n:
                    i = c * PER_CH + n + (I_FFN + 2 * FC)
                    load(i, w_down_k, n * P, ((c * FC, 6), (c * FC + 6, 5)))
            yp = y_prompt.rearrange("l t d -> (l t) d")
            ys = y_sample.rearrange("b t d -> (b t) d")
            for t in range(XT):
                sp.wait_ge(ya_ready if t % 2 else yd_ready, t // 2 + 1)
                if t < XT - 1:
                    sp.dma_start(yp[t * XTW:(t + 1) * XTW, :], otok[:, t, :]).then_inc(out_done, 16)
                else:
                    sp.dma_start(yp[TP - last:TP, :], otok[0:last, t, :]).then_inc(out_done, 16)
                    sp.dma_start(ys[:, :], otok[last:XTW, t, :]).then_inc(out_done, 16)
            sp.wait_ge(out_done, 16 * (XT + 1))

        @block.tensor
        def _(pe):
            def gemm(i, hi, lo, ks, sizes, parts, ready=None, between={}):
                pe.wait_ge(tile_read, i)
                where = [(out, j == 0, j == count - 1) for count, out in parts for j in range(count)]
                n = 0
                for q, size in enumerate(sizes):
                    pe.wait_ge(lo_done, 4 * (i - 1) + q + 1)
                    for s in range(size):
                        if n in between:
                            between[n]()
                        if ready:
                            ready(n)
                        k, (out, first, last) = ks[n], where[n]
                        for moving in (hi, lo):
                            for a in range(2):
                                pe.matmul(out[:, a, :], whi[:, q, s, :], moving[:, 2 * k + a, :],
                                          start=first and moving is hi, stop=False)
                        for a in range(2):
                            mm = pe.matmul(out[:, a, :], wlo[:, q, s, :], hi[:, 2 * k + a, :],
                                           start=False, stop=last)
                        n += 1
                    mm.then_inc(w_used, 1)

            one = lambda out, lhsT, rhs, start=True, stop=True: pe.matmul(out, lhsT, rhs, start=start, stop=stop)

            pe.wait_ge(ident_ok, 2)
            pe.wait_ge(g1_in, 16)
            pe.transpose(ps[:, 0, 0:KT], g1_rows[:], ident[0:KT, 0:KT]).then_inc(g1_t, 1)

            def gates(k):
                pe.wait_ge(x_lo, k + 1)
                for moving in (xhi, xlo):
                    for a in range(2):
                        mm = pe.matmul(pair(0)[:, a, :], gw[:, k, :], moving[:, 2 * k + a, :],
                                       start=k == 0 and moving is xhi, stop=k == KT - 1 and moving is xlo)
                if k % 4 == 3:
                    mm.then_inc(w_used, 1)

            piece = {k0: b for b, (k0, _) in enumerate(X_PIECES)}
            for k in range(KT):
                if k in piece:
                    pe.wait_ge(x_in[piece[k]], 16 * 3)
                if k >= 3:
                    pe.wait_ge(x_lo, k - 2)
                for t in range(XT):
                    p0 = 2 * (k % 3 + 1) + t // 3
                    mm = pe.transpose(ps[:, p0, (t % 3) * XTW:(t % 3 + 1) * XTW],
                                      xtok[:, t, k * P:(k + 1) * P], ident[0:XTW, 0:XTW])
                mm.then_inc(xt_done, 1)
                if k == 3:
                    pe.wait_ge(gw_lo, 1)
                if k >= 3:
                    gates(k - 3)
            for k in range(KT - 3, KT):
                gates(k)

            def gates_by_token():
                pe.wait_ge(tile_read, 2)
                zgf = flat(zg)
                for t in range(XT):
                    mm = pe.transpose(ps[0:XTW, BLK_A, t * 4 * H:(t + 1) * 4 * H], zgf[:, t * XTW:(t + 1) * XTW],
                                      ident[0:4 * H, 0:4 * H])
                mm.then_inc(zg_t, 1)
                pe.wait_ge(small_in, 16 * SMALLS)
                pe.transpose(ps[:, BLK_A + 1, 0:V_G1], vrows[:], ident[0:V_G1, 0:V_G1])
                for g in range(NG):
                    mm = pe.transpose(ps[:, BLK_A + 1, P + g * 16:P + g * 16 + 16], srows[:, g * P:(g + 1) * P],
                                      ident[0:16, 0:16])
                mm.then_inc(vec_t, 1)

            def spread_rstd():
                pe.wait_ge(diag_ok, 1)
                for t in range(XT):
                    mm = one(ps[:, BLK_B + t // 3, (t % 3) * XTW:(t % 3 + 1) * XTW], ones[0:XTW, :], diag[:, t, :])
                mm.then_inc(rb_mm, 1)

            def gates_by_head():
                pe.wait_ge(lf_c_ok, 1)
                pe.wait_ge(tile_read, 3)
                for src, c0, bank in ((gate, 0, BLK_A), (col["lf"], 0, BLK_B)):
                    for t in range(XT):
                        mm = pe.transpose(ps[0:H, bank + t // 3, (t % 3) * XTW:(t % 3 + 1) * XTW],
                                          src[:, t, c0:c0 + H], ident[0:XTW, 0:XTW])
                mm.then_inc(gates_t, 1)

            def columns_l():
                pe.wait_ge(l_ok, 1)
                for c in range(NC + 1):
                    n = CH if c < NC else SW
                    mm = pe.transpose(ps[0:n, BLK_A, c * H:(c + 1) * H], row["l"][:, c * CH:c * CH + n],
                                      ident[0:H, 0:H])
                mm.then_inc(l_t, 1)

            heads = range(KT)

            def head_tile(h, j, between={}):
                i = h * TILES_H + 1 + j
                gemm(i, xhi, xlo, heads, K_FULL, [(KT, pair(1 + j))], between=between)

            head_tile(0, 0, {1: gates_by_token, 10: spread_rstd})
            head_tile(0, 1, {2: gates_by_head, 13: columns_l})
            pe.wait_ge(row_a_ok, 1)
            pe.wait_ge(rows_ok, 2)

            def round_of_head(h, last):
                i = h * TILES_H + 1
                hv = h + 1
                qff, kff, v0ff, v1ff = map(flat, (qf, kf, v0f, v1f))

                def tile(j, between={}):
                    head_tile(h, j, between)

                pe.wait_ge(sel_ok, hv)
                for s in range(3):
                    one(ps[:, BLK_A + s, 0:TP], sel[:, s, :], rows[:, 0:TP])
                for s in range(3):
                    mm = one(ps[:, BLK_A + 3, s * SW:(s + 1) * SW], sel[:, s, :], rows[:, TP:T])
                mm.then_inc(bc_mm, 1)
                tile(2)
                pe.wait_ge(tile_read, i + 2)
                pe.wait_ge(bc_read, hv)
                for c in range(NC + 1):
                    n = CH if c < NC else SW
                    tok = slice(c * CH, c * CH + n)
                    b = BLK_B if c < NC else BLK_B + 1
                    col = c * P if c < NC else 0
                    pe.transpose(ps[0:n, b, col:col + P], kff[:, tok], ident[:])
                    b = BLK_A if c < NC else BLK_A + 1
                    mm = one(ps[0:n, b, col:col + n], kff[:, tok], qff[:, tok])
                mm.then_inc(k_s_mm, 1)
                tile(3)

                def v_by_token(bank, src, done):
                    for c in range(NC + 1):
                        n = CH if c < NC else SW
                        b, col = (bank, c * P) if c < NC else (bank + 1, 0)
                        mm = pe.transpose(ps[0:n, b, col:col + P], src[:, c * CH:c * CH + n], ident[:])
                    mm.then_inc(done, 1)

                pe.wait_ge(tile_read, i + 3)
                pe.wait_ge(kt_ok, hv)
                v_by_token(BLK_B, v0ff, v0_t)
                tile(4)
                pe.wait_ge(tile_read, i + 4)
                pe.wait_ge(p_ok, hv)
                v_by_token(BLK_A, v1ff, v1_t)
                tile(5)
                pe.wait_ge(v0_ok, hv)
                pe.wait_ge(v1_ok, hv)
                for c in range(NC):
                    one(ps[:, 4 + c, 0:DV + 1], kt[:, c, :], vt[:, c, :])
                one(ps[:, 4, 300:300 + NB], kt[0:SW, NC, :], wlast[:]).then_inc(u_mm, 1)
                tile(6)
                pe.wait_ge(state_ok, hv)
                pe.wait_ge(cs_in, h * 16 + 16)
                for j in range(3):
                    for c in range(NC):
                        tok = slice(c * CH, (c + 1) * CH)
                        out = ps[:, 4 + j, tok]
                        val = vt[:, c, j * P:(j + 1) * P] if j < 2 else ones[:]
                        one(out, val, wgt[:, c, :], stop=c == 0)
                        if c:
                            old = cst[:, c - 1, j * P:(j + 1) * P] if j < 2 else ones[:]
                            one(out, old, (qa if j < 2 else qn)[:, tok], start=False)
                    out = ps[:, 7, j * SW:(j + 1) * SW]
                    val = vt[0:SW, NC, j * P:(j + 1) * P] if j < 2 else ones[0:SW, :]
                    one(out, val, wgt[0:SW, NC, 0:SW], stop=False)
                    if j == 2:
                        mm = one(out, ones[:], qn[:, TP:T], start=False)
                    else:
                        for b in range(NB):
                            one(out[:, b * TS:(b + 1) * TS], cs[:, b, j * P:(j + 1) * P],
                                qa[:, TP + b * TS:TP + (b + 1) * TS], start=False, stop=b == NB - 1)
                mm.then_inc(num_mm, 1)
                tile(7)
                pe.wait_ge(h_ok, hv)
                for b in range(NB // 2):
                    mm = one(ps[:, 4 + b, :], kt[0:SW, NC, :],
                             vb[:, 2 * b:2 * b + 2, :].rearrange("p a b -> p (a b)"))
                mm.then_inc(us_mm, 1)
                tile(8)
                pe.wait_ge(cs_ok, hv)
                pe.wait_ge(hsum_ok, hv)
                for a in range(2):
                    mm = one(ps[:, BLK_A + a, 0:HT], ones[:], kf[:, a, :])
                mm.then_inc(hs_mm, 1)
                tile(9)
                tile(10)
                if last:
                    tile(11, {13: tails_by_row})
                else:
                    tile(11)
                    head_tile(h + 1, 0)
                    head_tile(h + 1, 1)

            def tails_by_row():
                pe.wait_ge(tails_ok, 1)
                pe.wait_ge(rh_in, H)
                pe.transpose(ps[0:(NB + 1) * H, BLK_A + 1, 384:384 + P], n_out[:], ident[:])
                for g in range(NG):
                    b, c = BLK_B + g // 4, (g % 4) * P
                    mm = pe.transpose(ps[0:2 + 2 * NB, b, c:c + P], tails[:, g, :], ident[:])
                mm.then_inc(tail_mm, 1)

            with pe.Fori(0, H - 1) as h:
                round_of_head(h, False)
            round_of_head(H - 1, True)

            def conv_squares():
                pe.wait_ge(ssc_ok, 2 * H)
                pe.wait_ge(rows_out, 1)
                for a in range(2):
                    mm = one(ps[:, BLK_A + a, 0:HT], ones[:], ssq_c[:, a, :])
                mm.then_inc(ssc_mm, 1)

            def mix_ready(n):
                pe.wait_ge(mix_lo, n + 1)
                if n == NG:
                    pe.wait_ge(rows_out, 1)

            def out_tile(i, slot, between={}, ready=None):
                gemm(i, mixhi, mixlo, MIX_K, K_FULL, [(KT - NG, pair(slot)), (NG, conv_pair(slot))],
                     ready=ready, between=between)

            out_tile(I_OUT, I_OUT, {3: conv_squares}, mix_ready)
            out_tile(I_OUT + 1, I_OUT + 1, {NG: lambda: pe.wait_ge(rc_in, 1)})
            with pe.Fori(1, KT // 2) as n2:
                for p in range(2):
                    out_tile(n2 * 2 + (I_OUT + p), I_OUT + p)

            def up_tile(i, p, between={}, ready=None):
                gemm(i, xhi, xlo, heads, K_FULL, [(KT, pair(I_FFN + p))], ready=ready, between=between)

            def up(i):
                for p in range(2):
                    up_tile(i + p, p)

            def down(i, c, slot):
                def ready(n):
                    if n in (0, FC - 1):
                        pe.wait_ge(h_lo, c * FC + (FC - 1 if n == 0 else FC))
                gemm(i, hhi, hlo, range(FC), K_DOWN, [(FC, pair(slot))], ready=ready)

            def norm_squares():
                pe.wait_ge(ss2_ok, KT)
                for a in range(2):
                    mm = one(ps[:, BLK_A + a, 0:HT], ones[:], ssq2[:, a, :])
                mm.then_inc(ss2_mm, 1)

            up_tile(I_FFN, 0, {8: norm_squares}, lambda n: pe.wait_ge(x1_lo, n + 1))
            up_tile(I_FFN + 1, 1)
            with pe.Fori(0, NCH - 1) as c:
                i0 = c * PER_CH + I_FFN
                with pe.Fori(1, FC) as f:
                    up(i0 + f * 2)
                with pe.Fori(0, KT // 2) as n2:
                    for p in range(2):
                        down(i0 + n2 * 2 + (2 * FC + p), c, I_FFN + p)
                up(i0 + PER_CH)
            i0 = I_FFN + (NCH - 1) * PER_CH
            with pe.Fori(1, FC) as f:
                up(i0 + f * 2)

            def turn(n, p):
                pe.wait_ge(zg_n, n + 1)
                if isinstance(n, int) and n < 2:
                    pass
                else:
                    pe.wait_ge(out_read, n - 1)
                for t in range(XT):
                    src = zgn[:, p, t // 3, (t % 3) * XTW:(t % 3 + 1) * XTW]
                    mm = pe.transpose(ps[0:XTW, 4 + 2 * p + t // 3, (t % 3) * P:(t % 3 + 1) * P], src, ident[:])
                mm.then_inc(out_t, 1)

            i1 = i0 + 2 * FC
            down(i1, NCH - 1, I_FFN)
            down(i1 + 1, NCH - 1, I_FFN + 1)
            turn(0, 0)
            down(i1 + 2, NCH - 1, I_FFN)
            turn(1, 1)
            down(i1 + 3, NCH - 1, I_FFN + 1)
            with pe.Fori(2, KT // 2) as n2:
                turn(n2 * 2 - 2, 0)
                down(n2 * 2 + i1, NCH - 1, I_FFN)
                turn(n2 * 2 - 1, 1)
                down(n2 * 2 + (i1 + 1), NCH - 1, I_FFN + 1)
            turn(KT - 2, 0)
            turn(KT - 1, 1)
            pe.wait_ge(ssf_ok, KT)
            ssf = flat(ssq_f)
            for t in range(XT):
                mm = one(ps[0:XTW, 0, t:t + 1], ssf[:, t * XTW:(t + 1) * XTW], ones[:, 0:1])
            mm.then_inc(rf_mm, 1)

        @block.scalar
        def _(act):
            def hi(i, q, sizes=K_FULL, gain=None):
                s0, n = sum(sizes[2 * (q // 2):q]), sizes[q]
                if gain is None:
                    act.wait_ge(raw_in[q // 2], i * 16)
                else:
                    act.wait_ge(gained, gain)
                act.wait_ge(w_used, 4 * (i - 1) + q + 1)
                act.activation(whi[:, q, 0:n, :], wraw[:, q // 2, s0:s0 + n, :], ACT.Copy).then_inc(hi_done, 1)

            def small(dst, src):
                act.dma_start(dst, src).then_inc(small_in, 16)
            rows_of = lambda v: v.rearrange("l (k p) -> (l k) p", p=P)
            act.dma_start(g1_rows[:], rows_of(norm1_g)).then_inc(g1_in, 16)
            act.dma_start(gw_raw[:], w_in_k[:, :, COL_G:COL_G + 2 * H]).then_inc(gw_in, 16)
            small(vrows[V_G2:V_G2 + KT, :], rows_of(norm2_g))
            small(vrows[V_GF:V_GF + KT, :], final_g.rearrange("(k p) -> k p", p=P))
            small(vrows[V_MIX:V_MIX + NG, :], rows_of(conv_out_g))
            small(vrows[V_MIX + NG:V_MIX + KT, :], rows_of(mlstm_out_g))
            small(vrows[V_CW:V_CW + CW * NG, :], conv_w.rearrange("l w (k p) -> (l w k) p", p=P))
            small(vrows[V_N:V_N + NB * H, :], n_dram)
            small(srows[:], state_conv.rearrange("l b r d -> (l b r) d"))
            small(bias_c[:, 0:H], b_igate.to_broadcast([XTW, H]))
            small(bias_c[:, H:2 * H], b_fgate.to_broadcast([XTW, H]))
            act.dma_start(m0[:], state_m.rearrange("l b h -> (l h) b"), allow_slow_non_contiguous=True).then_inc(small_in, 16)

            act.wait_ge(gw_g, 1)
            act.activation(gw[:, :, 0:2 * H], gw_raw[:], ACT.Copy).then_inc(gw_hi, 1)

            def square(b, t):
                k0, n = X_PIECES[b]
                x = xtok[:, t, k0 * P:(k0 + n) * P]
                act.activation(x, x, ACT.Square, accum_out=ss_part[:, t, b:b + 1]).then_inc(ss_ok, 1)

            for b, (k0, n) in enumerate(X_PIECES):
                for k in range(k0, k0 + n):
                    p0 = 2 * (k % 3 + 1)
                    act.wait_ge(xt_done, k + 1)
                    act.activation(xhi[:, 2 * k:2 * k + 2, :], ps[:, p0:p0 + 2, 0:HT], ACT.Copy).then_inc(x_hi, 1)
                if b == len(X_PIECES) - 1:
                    hi(1, 0, gain=1)
                    hi(1, 1, gain=2)
                for t in range(SQ_ACT):
                    square(b, t)
            hi(1, 2, gain=3)
            hi(1, 3, gain=4)
            act.wait_ge(rb_rec, 1)
            act.activation(rstd_col[0:XTW, :], ss_col[0:XTW, :], ACT.Sqrt).then_inc(rstd_c_ok, 1)
            hi(2, 0, gain=5)
            act.wait_ge(ax_ok, 1)
            act.activation(col["e"][:], col["ax"][:], ACT.Exp, scale=-1.0).then_inc(e_ok, 1)
            act.wait_ge(u_ok, 1)
            act.activation(col["ln"][:], col["u"][:], ACT.Ln).then_inc(ln_ok, 1)
            hi(2, 1, gain=6)
            hi(2, 2, gain=7)
            hi(2, 3, gain=8)
            hi(3, 0, gain=9)
            act.wait_ge(m_ok, 1)
            act.activation(rows[64:64 + H, :], row["m"][:], ACT.Exp, scale=-1.0).then_inc(rows_ok, 1)
            act.wait_ge(pre_ok, 1)
            act.activation(rows[32:32 + H, :], row["pre"][:], ACT.Exp).then_inc(rows_ok, 1)
            act.dma_start(p_m.rearrange("l b h -> h (l b)"), m_out[:, 0:1]).then_inc(small_out, 16)
            act.dma_start(s_m.rearrange("l b h -> (l h) b"), m_out[:, 1:1 + NB], allow_slow_non_contiguous=True).then_inc(small_out, 16)

            def load_state(h):
                act.dma_start(cs[:], state_C[0, :, ds(h, 1)].rearrange("b h k v -> k (b h) v")).then_inc(cs_in, 16)

            load_state(0)
            for q in range(1, 4):
                hi(3, q, gain=4 * 2 + q + 1)

            def mix_high(n):
                k = MIX_K[n]
                act.activation(mixhi[:, 2 * k:2 * k + 2, :], mixf[:, 2 * k:2 * k + 2, :],
                               ACT.Copy).then_inc(mix_hi, 1)

            def round_of_head(h, last):
                i = h * TILES_H + 1
                hv = h + 1

                def quarter(j, q):
                    n = i + (j + 1)
                    if last and j == TILES_H - 1:
                        out_hi(0, q)
                    else:
                        hi(n, q, gain=4 * (n - 1) + q + 1)

                act.wait_ge(bc_mm, hv)
                for c in range(NC):
                    act.activation(wgt[:, c, :], side(BLK_A)[:, c * CH:(c + 1) * CH], ACT.Exp,
                                   bias=colh[:, c:c + 1])
                act.activation(wgt[0:SW, NC, 0:SW], ps[0:SW, BLK_A + 3, 0:SW], ACT.Exp,
                               bias=colh[0:SW, NC:NC + 1]).then_inc(w_exp, 1)
                for j in (2, 3, 4):
                    for q in range(4):
                        quarter(j, q)
                for o in range(2):
                    quarter(5 + o, 0)
                    quarter(5 + o, 1)
                    act.wait_ge(tile_read, i + (4 + o + 2))
                    act.activation(so[:, o], so[:, o], ACT.Sigmoid).then_inc(so_ok, 1)
                    quarter(5 + o, 2)
                    quarter(5 + o, 3)
                act.wait_ge(state_ok, hv)
                act.dma_start(p_C[0, 0, ds(h, 1)].rearrange("h k v -> (h k) v"),
                              cst[:, NC - 1, 0:DV]).then_inc(c_out, 16)
                quarter(7, 0)
                quarter(7, 1)
                quarter(7, 2)
                quarter(7, 3)
                quarter(8, 0)
                act.wait_ge(h_ok, hv)
                act.activation(kf[:], h0[:], ACT.Square)
                act.activation(qf[:], h1[:], ACT.Square).then_inc(hsq_ok, 1)
                quarter(8, 1)
                quarter(8, 2)
                quarter(8, 3)
                act.wait_ge(cs_ok, hv)
                act.dma_start(s_C[0, :, ds(h, 1)].rearrange("b h k v -> k (b h) v"), cs[:]).then_inc(c_out, 16)
                act.wait_ge(tile_read, i + (8 + 2))
                act.activation(sqy[:], mixf[:, ds(h * 4, 2), :], ACT.Square).then_inc(ysq_ok, 1)
                for q in range(4):
                    quarter(9, q)
                act.wait_ge(rh_in, hv)
                act.activation(rh[:], rh[:], ACT.Sqrt).then_inc(rh_ok, 1)
                if last:
                    act.wait_ge(c_out, H * 32)
                    mix_high(0)
                    mix_high(1)
                    quarter(10, 0)
                    mix_high(2)
                    mix_high(3)
                    quarter(10, 1)
                    mix_high(4)
                    mix_high(5)
                    quarter(10, 2)
                    quarter(10, 3)
                    act.wait_ge(mix_heads, 1)
                    mix_high(6)
                    mix_high(7)
                    for q in range(4):
                        quarter(11, q)
                        if q < 3:
                            mix_high(8 + 2 * q)
                            mix_high(9 + 2 * q)
                    mix_high(14)
                else:
                    for j in (10, 11):
                        for q in range(4):
                            quarter(j, q)
                act.wait_ge(tile_read, i + (11 + 2))
                act.activation(sqy[:], mixf[:, ds(h * 4 + 2, 2), :], ACT.Square).then_inc(ysq_ok, 1)
                if last:
                    mix_high(15)
                else:
                    act.wait_ge(c_out, h * 32 + 32)
                    load_state(h + 1)
                    for j in (12, 13):
                        for q in range(4):
                            quarter(j, q)

            def out_hi(n, q):
                if q < 2:
                    hi(n + I_OUT, q)
                else:
                    hi(n + I_OUT, q, gain=n * 2 + (4 * (I_OUT - 1) + q - 1))

            with act.Fori(0, H - 1) as h:
                round_of_head(h, False)
            round_of_head(H - 1, True)

            act.wait_ge(rows_out, 1)
            act.dma_start(s_n.rearrange("l b h d -> (l b h) d"), n_rows[0:NB * H, :]).then_inc(small_out, 16)
            act.dma_start(p_n.rearrange("l b h d -> (l b h) d"), n_rows[NB * H:(NB + 1) * H, :]).then_inc(small_out, 16)
            act.dma_start(p_conv.rearrange("l b r d -> (l b r) d"), conv_rows[0:2, :]).then_inc(small_out, 16)
            act.dma_start(s_conv.rearrange("l b r d -> (l b r) d"), conv_rows[2:, :]).then_inc(small_out, 16)

            def out_tile(n, nxt):
                for q in range(4):
                    nxt(q)
                act.wait_ge(x1_ok, n + 1)
                act.activation(xhi[:, ds(n * 2, 2), :], x1[:], ACT.Copy).then_inc(x1_hi, 1)
                act.activation(sq2[:], x1[:], ACT.Square).then_inc(x1_sq, 1)

            GB = 4 * (I_OUT - 1) + 2 * KT

            def ffn_gain(c, f, p, q):
                return GB + c * (8 * FC) + f * 8 + (4 * p + q + 1)

            for q in range(4):
                out_hi(1, q)
            act.wait_ge(rc_in, 1)
            act.activation(rh[:], rh[:], ACT.Sqrt).then_inc(rc_ok, 1)
            out_tile(0, lambda q: None)
            with act.Fori(1, KT - 1) as n:
                out_tile(n, lambda q: out_hi(n + 1, q))
            out_tile(KT - 1, lambda q: hi(I_FFN, q, gain=GB + q + 1))
            act.wait_ge(r2_in, 1)
            act.activation(rstd[:], rstd[:], ACT.Sqrt).then_inc(r2_ok, 1)

            def up(c, f, i, nxt):
                for q in range(4):
                    hi(i + 1, q, gain=ffn_gain(c, f, 1, q))
                act.wait_ge(tile_read, i + 2)
                act.activation(sact[:], gact[:], ACT.Sigmoid).then_inc(s_ok, 1)
                for q in range(4):
                    nxt(q)
                act.wait_ge(tile_read, i + 3)
                act.activation(hhi[:, ds(f * 2, 2), :], hf[:], ACT.Copy).then_inc(h_hi, 1)

            def up_phase(c, i0):
                with act.Fori(0, FC - 1) as f:
                    up(c, f, i0 + f * 2, lambda q: hi(i0 + f * 2 + 2, q, gain=ffn_gain(c, f + 1, 0, q)))
                i = i0 + 2 * (FC - 1)
                up(c, FC - 1, i, lambda q: hi(i + 2, q, K_DOWN))

            with act.Fori(0, NCH - 1) as c:
                i0 = c * PER_CH + I_FFN
                up_phase(c, i0)
                with act.Fori(0, KT - 1) as n:
                    for q in range(4):
                        hi(i0 + n + (2 * FC + 1), q, K_DOWN)
                for q in range(4):
                    hi(i0 + PER_CH, q, gain=ffn_gain(c + 1, 0, 0, q))
            c, i0 = NCH - 1, I_FFN + (NCH - 1) * PER_CH
            up_phase(c, i0)

            def last_down(n, p, nxt=None):
                if nxt:
                    for q in range(4):
                        nxt(q)
                act.wait_ge(tile_read, n + (i1 + 2))
                act.activation(sqf[:], zf[:, p], ACT.Square).then_inc(z_sq, 1)

            def put(n, p):
                act.wait_ge(out_t, n + 1)
                for b in range(2):
                    ins = act.activation(otok[:, 3 * b:3 * b + 3, ds(n * P, P)],
                                         ps[0:XTW, 4 + 2 * p + b, 0:3 * P].rearrange("p (c f) -> p c f", f=P),
                                         ACT.Copy)
                ins.then_inc(out_read, 1)

            i1 = i0 + 2 * FC
            last_down(0, 0, lambda q: hi(i1 + 1, q, K_DOWN))
            last_down(1, 1, lambda q: hi(i1 + 2, q, K_DOWN))
            put(0, 0)
            last_down(2, 0, lambda q: hi(i1 + 3, q, K_DOWN))
            with act.Fori(1, KT // 2 - 1) as m:
                last_down(m * 2 + 1, 1, lambda q: hi(m * 2 + (i1 + 2), q, K_DOWN))
                put(m * 2 - 1, 1)
                last_down(m * 2 + 2, 0, lambda q: hi(m * 2 + (i1 + 3), q, K_DOWN))
                put(m * 2, 0)
            last_down(KT - 1, 1)
            put(KT - 3, 1)
            put(KT - 2, 0)
            put(KT - 1, 1)
            act.wait_ge(rf_in, 1)
            act.activation(ss_col[0:XTW, :], ss_col[0:XTW, :], ACT.Sqrt).then_inc(rf_ok, 1)
            act.wait_ge(rf_ok, 1)
            for t in range(1, XT, 2):
                act.mul(otok[:, t, :], otok[:, t, :], ss_col[0:XTW, t:t + 1]).then_inc(ya_ready, 1)
            act.wait_ge(small_out, 16 * 6)

        @block.gpsimd
        def _(pool):
            pool.memset(ident[:], 0.0).then_inc(ident_ok, 1)
            pool.wait_ge(ident_ok, 1)
            pool.affine_select(out=ident[:], in_=ident[:], compare_op=ALU.not_equal, fill=1.0, base=0,
                               pattern=[[-1, P]], channel_multiplier=1).then_inc(ident_ok, 1)
            for h in range(H):
                pool.wait_ge(w_exp, h + 1)
                wp = wgt[:, 0:NC, :]
                pool.affine_select(out=wp, in_=wp, compare_op=ALU.is_ge, fill=0.0, base=0,
                                   pattern=[[0, NC], [1, CH]], channel_multiplier=-1)
                ws = wgt[0:SW, NC, 0:SW].rearrange("p (b t) -> p b t", t=TS)
                pool.affine_select(out=ws, in_=ws, compare_op=ALU.is_ge, fill=0.0, base=0,
                                   pattern=[[TS, NB], [1, TS]], channel_multiplier=-1).then_inc(pool_chain, 1)
                pool.wait_ge(pool_chain, h + 1)
                pool.affine_select(out=ws, in_=ws, compare_op=ALU.is_ge, fill=0.0, base=0,
                                   pattern=[[-TS, NB], [0, TS]], channel_multiplier=1).then_inc(w_masked, 1)
                pool.wait_ge(hsq_ok, h + 1)
                pool.tensor_tensor(kf[:], kf[:], qf[:], ALU.add).then_inc(hsum_ok, 1)

        @block.vector
        def _(dve):
            chain = Chain(dve, dve_chain)
            LINKS = {"head": 32, "out": 4, "up": 2, "chunk": 2 * FC}
            link = chain.link
            tt, ts, stt = dve.tensor_tensor, dve.tensor_scalar, dve.scalar_tensor_tensor

            def gain(i, q, col):
                dve.wait_ge(raw_in[q // 2], i * 16)
                w = wraw[:, q // 2, 4 * (q % 2):4 * (q % 2) + 4, :]
                g = vecs[:, col + 4 * q:col + 4 * q + 4].unsqueeze(2).to_broadcast([P, 4, P])
                tt(w, w, g, ALU.mult).then_inc(gained, 1)

            def low(i, q, sizes=K_FULL):
                s0, n = sum(sizes[2 * (q // 2):q]), sizes[q]
                dve.wait_ge(hi_done, 4 * (i - 1) + q + 1)
                tt(wlo[:, q, 0:n, :], wraw[:, q // 2, s0:s0 + n, :], whi[:, q, 0:n, :].bitcast(F32),
                   ALU.subtract).then_inc(lo_done, 1)

            def split(i, q, col=None, sizes=K_FULL):
                if col is not None:
                    if q == 0:
                        gain(i, 0, col)
                    if q < 3:
                        gain(i, q + 1, col)
                low(i, q, sizes)

            def split_out(i, q):
                if q in (1, 2):
                    gain(i, q + 1, V_MIX - NG)
                low(i, q)

            def tile_done(i):
                dve.wait_ge(w_used, 4 * i + 4)

            def to_rms(out, total, n):
                link(ts(out, total, 1.0 / n, EPS, ALU.mult, ALU.add))

            link(dve.memset(gw[:].bitcast(F32), 0.0))
            dve.memset(ones[:], 1.0)
            dve.wait_ge(g1_t, 1)
            dve.tensor_copy(vecs[:, V_G1:V_G1 + KT], ps[:, 0, 0:KT]).then_inc(tile_read, 1)
            dve.wait_ge(tile_read, 1)
            dve.wait_ge(gw_in, 16)
            g1 = vecs[:, V_G1:V_G1 + KT].unsqueeze(2).to_broadcast([P, KT, 2 * H])
            tt(gw_raw[:], gw_raw[:], g1, ALU.mult).then_inc(gw_g, 1)
            dve.wait_ge(gw_hi, 1)
            tt(gw[:, :, 2 * H:4 * H], gw_raw[:], gw[:, :, 0:2 * H].bitcast(F32), ALU.subtract).then_inc(gw_lo, 1)
            dve.memset(rows[:], 0.0)
            dve.memset(ssq_c[:], 0.0)
            for b, (k0, n) in enumerate(X_PIECES):
                for k in range(k0, k0 + n):
                    p0 = 2 * (k % 3 + 1)
                    dve.wait_ge(x_hi, k + 1)
                    tt(xlo[:, 2 * k:2 * k + 2, :], ps[:, p0:p0 + 2, 0:HT],
                       xhi[:, 2 * k:2 * k + 2, :].bitcast(F32), ALU.subtract).then_inc(x_lo, 1)
                if b == len(X_PIECES) - 1:
                    split(1, 0, V_G1)
                    split(1, 1, V_G1)
                for t in range(SQ_ACT, XT):
                    x = xtok[:, t, k0 * P:(k0 + n) * P]
                    ins = stt(x, x, 1.0, x, ALU.mult, ALU.mult, accum_out=ss_part[:, t, b:b + 1])
            link(ins)
            tile_done(0)
            dve.tensor_copy(zg[:], pair(0)[0:4 * H]).then_inc(tile_read, 1)
            split(1, 2, V_G1)
            split(1, 3, V_G1)
            dve.wait_ge(ss_ok, len(X_PIECES) * SQ_ACT)
            link(dve.tensor_reduce(ss_col[0:XTW, :], ss_part[:], mybir.AxisListType.X, ALU.add))
            to_rms(ss_col[0:XTW, :], ss_col[0:XTW, :], D)
            dve.reciprocal(ss_col[0:XTW, :], ss_col[0:XTW, :]).then_inc(rb_rec, 1)
            dve.wait_ge(rstd_c_ok, 1)
            for t in range(XT):
                ins = ts(diag[:, t, :], ident[0:XTW, 0:XTW], rstd_col[0:XTW, t:t + 1], None, ALU.mult)
            ins.then_inc(diag_ok, 1)
            dve.wait_ge(zg_t, 1)
            dve.wait_ge(small_in, 16 * SMALLS)
            link(dve.tensor_copy(zc[:], ps[0:XTW, BLK_A, 0:XT * 4 * H].rearrange("p (t c) -> p t c", c=4 * H)))
            link(tt(gate[:], zc[:, :, 0:2 * H], zc[:, :, 2 * H:4 * H], ALU.add))
            link(tt(gate[:], gate[:], rstd_col[0:XTW, :].unsqueeze(2).to_broadcast([XTW, XT, 2 * H]), ALU.mult))
            link(tt(gate[:], gate[:], bias_c[:].unsqueeze(1).to_broadcast([XTW, XT, 2 * H]), ALU.add))
            f = gate[:, :, H:2 * H]
            stt(col["ax"][:], f, -1.0, f, ALU.mult, ALU.max).then_inc(ax_ok, 1)
            split(2, 0, V_G1)
            r = col
            dve.wait_ge(e_ok, 1)
            ts(r["u"][:], r["e"][:], 1.0, None, ALU.add).then_inc(u_ok, 1)
            dve.wait_ge(u_ok, 1)
            link(ts(r["d"][:], r["u"][:], 1.0, None, ALU.subtract))
            link(ts(r["z"][:], r["d"][:], 0.0, None, ALU.is_equal))
            link(tt(r["d"][:], r["d"][:], r["z"][:], ALU.add))
            link(dve.reciprocal(r["rec"][:], r["d"][:]))
            link(tt(r["rec"][:], r["rec"][:], r["e"][:], ALU.mult))
            dve.wait_ge(ln_ok, 1)
            link(tt(r["z"][:], r["z"][:], r["ln"][:], ALU.add))
            link(tt(r["z"][:], r["z"][:], r["rec"][:], ALU.mult))
            stt(r["lf"][:], f, 0.0, r["z"][:], ALU.min, ALU.subtract).then_inc(lf_c_ok, 1)
            dve.wait_ge(vec_t, 1)
            dve.tensor_copy(vecs[:, 0:V_G1], ps[:, BLK_A + 1, 0:V_G1])
            dve.tensor_copy(conv_state[:], ps[:, BLK_A + 1, P:2 * P].rearrange("p (g r) -> p g r", r=16))
            split(2, 1, V_G1)
            dve.wait_ge(rb_mm, 1)
            link(dve.tensor_copy(rstd[:], side_halves(BLK_B)))
            dve.memset(vt[:, :, DV:DV + 1], 1.0)
            dve.memset(mprev[:, 0:1], 0.0)
            dve.tensor_copy(mprev[:, NC:NC + NB], m0[:])
            r = row
            link(dve.memset(r["mask"][:], 1.0))
            dve.memset(r["mask"][:, 0:TP:CH], 0.0)
            link(dve.memset(r["mask"][:, TP:T:TS], 0.0))
            split(2, 2, V_G1)
            tile_done(1)
            stt(qf[:], pair(1), QS, rstd[:], ALU.mult, ALU.mult).then_inc(tile_read, 1)
            split(2, 3, V_G1)
            dve.wait_ge(gates_t, 1)
            dve.tensor_copy(r["li"].rearrange("p (a b) -> p a b", a=2), side_halves(BLK_A)[0:H])
            link(dve.tensor_copy(r["lf"].rearrange("p (a b) -> p a b", a=2), side_halves(BLK_B)[0:H]))
            dve.tensor_tensor_scan(r["b"][:], r["mask"][:], r["lf"][:], 0.0, ALU.mult, ALU.add)
            ins = dve.tensor_tensor_scan(r["m"][:, 0:TP], r["lf"][:, 0:TP], r["li"][:, 0:TP], 0.0, ALU.add, ALU.max)
            for b in range(NB):
                s = slice(TP + b * TS, TP + (b + 1) * TS)
                ins = dve.tensor_tensor_scan(r["m"][:, s], r["lf"][:, s], r["li"][:, s], m0[:, b:b + 1],
                                             ALU.add, ALU.max)
            ins.then_inc(m_ok, 1)
            dve.wait_ge(m_ok, 1)
            split(3, 0, V_G1)
            dve.tensor_copy(m_out[:, 0:1], r["m"][:, TP - 1:TP])
            dve.tensor_copy(m_out[:, 1:1 + NB], r["m"][:, TP + TS - 1:T:TS])
            dve.tensor_copy(mprev[:, 1:NC], r["m"][:, CH - 1:TP - 1:CH])
            tt(r["l"][:], r["li"][:], r["b"][:], ALU.subtract).then_inc(l_ok, 1)
            tt(rows[0:H, :], r["b"][:], r["m"][:], ALU.subtract).then_inc(row_a_ok, 1)
            dve.wait_ge(row_a_ok, 1)
            tt(r["pre"][:, 0:TP].rearrange("p (c t) -> p c t", t=CH), rows[0:H, 0:TP].rearrange("p (c t) -> p c t", t=CH),
               mprev[:, 0:NC].unsqueeze(2).to_broadcast([H, NC, CH]), ALU.add)
            tt(r["pre"][:, TP:T].rearrange("p (b t) -> p b t", t=TS), rows[0:H, TP:T].rearrange("p (b t) -> p b t", t=TS),
               mprev[:, NC:].unsqueeze(2).to_broadcast([H, NB, TS]), ALU.add).then_inc(pre_ok, 1)
            split(3, 1, V_G1)
            split(3, 2, V_G1)
            dve.wait_ge(l_t, 1)
            dve.tensor_copy(colall[:, 0:NC, :], ps[:, BLK_A, 0:NC * H].rearrange("p (c h) -> p c h", h=H))
            link(dve.tensor_copy(colall[0:SW, NC, :], ps[0:SW, BLK_A, NC * H:(NC + 1) * H]))

            def head_columns(h):
                for s in range(3):
                    dve.tensor_copy(sel[:, s, :], ident[:, ds(h + 32 * s, 1)].to_broadcast([P, P]))
                dve.tensor_copy(gml[:], vecs[:, ds(h * 2 + (V_MIX + NG), 2)])
                dve.tensor_copy(colh[:, 0:NC], colall[:, 0:NC, ds(h, 1)].rearrange("p c h -> p (c h)"))
                dve.tensor_copy(colh[0:SW, NC:NC + 1], colall[0:SW, NC, ds(h, 1)]).then_inc(sel_ok, 1)

            head_columns(0)
            tile_done(2)
            tt(kf[:], pair(2), rstd[:], ALU.mult).then_inc(tile_read, 1)
            split(3, 3, V_G1)

            def round_of_head(h, last):
                i = h * TILES_H + 1
                hv = h + 1

                def quarter(j, q):
                    n = i + (j + 1)
                    if last and j == TILES_H - 1:
                        split_out(n, q)
                    else:
                        split(n, q, V_G1)

                def done(j):
                    tile_done(i + j)

                def evac(ins):
                    ins.then_inc(tile_read, 1)

                quarter(2, 0)
                dve.wait_ge(bc_mm, hv)
                dve.wait_ge(tile_read, i + 2)
                decay, low_bound, sampled = ps[:, BLK_A + 1, :], ps[:, BLK_A + 2, :], ps[:, BLK_A + 3, :]
                tt(qa[:, 0:TP], flat(qf)[:, 0:TP], decay, ALU.mult)
                dve.tensor_copy(sc[:, 0:NC], decay[:, CH - 1:TP:CH])
                dve.tensor_copy(em[:, 0:TP], low_bound)
                dve.wait_ge(w_exp, hv)
                tt(qa[:, TP:T], flat(qf)[:, TP:T], sampled[:, SW:2 * SW], ALU.mult)
                dve.tensor_copy(sc[:, NC:], sampled[:, SW + TS - 1:2 * SW:TS])
                dve.tensor_copy(em[:, TP:T], sampled[:, 2 * SW:3 * SW]).then_inc(bc_read, 1)
                quarter(2, 1)
                quarter(2, 2)
                done(2)
                evac(tt(v0f[:], pair(3), rstd[:], ALU.mult))
                quarter(2, 3)
                quarter(3, 0)
                dve.wait_ge(k_s_mm, hv)
                dve.wait_ge(w_masked, hv)
                for c in range(NC):
                    ts(kt[:, c, :], ps[:, BLK_B, c * P:(c + 1) * P], wgt[:, c, CH - 1:CH], None, ALU.mult)
                dve.tensor_copy(wlast[:], wgt[0:SW, NC, TS - 1:SW:TS])
                dve.tensor_copy(kt[0:SW, NC, :], ps[0:SW, BLK_B + 1, 0:P]).then_inc(kt_ok, 1)
                quarter(3, 1)
                dve.wait_ge(kt_ok, hv)
                tt(wgt[:, 0:NC, :], ps[:, BLK_A, :].rearrange("p (c t) -> p c t", t=CH), wgt[:, 0:NC, :], ALU.mult)
                tt(wgt[0:SW, NC, 0:SW], ps[0:SW, BLK_A + 1, 0:SW], wgt[0:SW, NC, 0:SW], ALU.mult).then_inc(p_ok, 1)
                quarter(3, 2)
                done(3)
                evac(tt(v1f[:], pair(4), rstd[:], ALU.mult))
                quarter(3, 3)

                def v_evac(half, bank, ok):
                    cols = slice(half * P, (half + 1) * P)
                    dve.tensor_copy(vt[:, 0:NC, cols], ps[:, bank, :].rearrange("p (c v) -> p c v", v=P))
                    dve.tensor_copy(vt[0:SW, NC, cols], ps[0:SW, bank + 1, 0:P]).then_inc(ok, 1)

                quarter(4, 0)
                dve.wait_ge(v0_t, hv)
                v_evac(0, BLK_B, v0_ok)
                quarter(4, 1)
                quarter(4, 2)
                done(4)
                evac(tt(so[:, 0], pair(5), rstd[:], ALU.mult))
                quarter(4, 3)
                quarter(5, 0)
                dve.wait_ge(v1_t, hv)
                v_evac(1, BLK_A, v1_ok)
                quarter(5, 1)
                quarter(5, 2)
                done(5)
                evac(tt(so[:, 1], pair(6), rstd[:], ALU.mult))
                quarter(5, 3)

                def early(n0, n1):
                    if last:
                        for n in range(n0, n1):
                            mix_low(n)

                def sum_squares():
                    tt(ssq_c[:], ssq_c[:], sqy[:], ALU.add).then_inc(ssc_ok, 1)

                def conv_columns(g):
                    for w in range(CW):
                        dve.tensor_copy(taps[:, w:w + 1], vecs[:, ds(h * 2 + (V_CW + w * NG + g), 1)])
                    link(dve.tensor_copy(cstate[:], conv_state[:, ds(h * 2 + g, 1), :].rearrange("p g r -> p (g r)")))

                def conv_gate(j):
                    done(j)
                    evac(tt(cg[:], pair(1 + j), rstd[:], ALU.mult))
                    dve.wait_ge(tile_read, i + (j + 2))
                    link(tt(cg[:], cg[:], rstd[:], ALU.mult))

                uf, cf = flat(u), flat(cv)
                us = uf[:, TP:T].rearrange("p (b t) -> p b t", t=TS)
                cvs = cf[:, TP:T].rearrange("p (b t) -> p b t", t=TS)
                st = cstate.rearrange("p (b r) -> p b r", r=2)

                def add_tap(dst, src, w):
                    link(stt(dst, src, taps[:, w:w + 1], dst, ALU.mult, ALU.add))

                def conv_input(j):
                    done(j)
                    evac(tt(u[:], pair(1 + j), cg[:], ALU.mult))
                    dve.wait_ge(tile_read, i + (j + 2))

                def conv_sum(g):
                    link(ts(cf, uf, taps[:, 2:3], None, ALU.mult))
                    add_tap(cf[:, 1:TP], uf[:, 0:TP - 1], 1)
                    add_tap(cf[:, 2:TP], uf[:, 0:TP - 2], 0)
                    add_tap(cvs[:, :, 1:TS], us[:, :, 0:TS - 1], 1)
                    add_tap(cvs[:, :, 0:1], st[:, :, 1:2], 1)
                    add_tap(cvs[:, :, 2:TS], us[:, :, 0:TS - 2], 0)
                    add_tap(cvs[:, :, 0:2], st, 0)
                    dve.tensor_copy(tails[:, ds(h * 2 + g, 1), 0:2], uf[:, TP - 2:TP].unsqueeze(1))
                    dve.tensor_copy(tails[:, ds(h * 2 + g, 1), 2:].rearrange("p g (b r) -> p (g b) r", r=2),
                                    us[:, :, TS - 2:TS])
                    ins = tt(cv[:], cv[:], rstd[:], ALU.mult)
                    if last and g == 1:
                        ins.then_inc(tails_ok, 1)
                        dve.wait_ge(tails_ok, 1)
                    else:
                        link(ins)

                def conv_out(j, g):
                    done(j)
                    evac(tt(mixf[:, ds(h * 4 + 2 * g, 2), :], pair(1 + j), cv[:], ALU.mult))

                quarter(6, 0)
                conv_columns(0)
                dve.wait_ge(u_mm, hv)
                link(dve.tensor_copy(cst[:, 0, :], ps[:, 4, 0:DV + 1]))
                for c in range(1, NC):
                    link(stt(cst[:, c, :], cst[:, c - 1, :], sc[:, c:c + 1], ps[:, 4 + c, 0:DV + 1],
                             ALU.mult, ALU.add))
                quarter(6, 1)
                n_old = vecs[:, V_N:V_N + NB * H].rearrange("p (b h) -> p b h", h=H)[:, :, ds(h, 1)]
                n_new = n_out[:, 0:NB * H].rearrange("p (b h) -> p b h", h=H)[:, :, ds(h, 1)]
                qs3 = qa[:, TP:T].rearrange("p (b t) -> p b t", t=TS)
                tt(qn[:, TP:T].rearrange("p (b t) -> p b t", t=TS), qs3, n_old.to_broadcast([P, NB, TS]), ALU.mult)
                link(tt(n_new, n_old, sc[:, NC:].unsqueeze(2), ALU.mult))
                link(tt(n_new, n_new, ps[:, 4, 300:300 + NB].unsqueeze(2), ALU.add))
                dve.tensor_copy(n_out[:, ds(h + NB * H, 1)], cst[:, NC - 1, DV:DV + 1])
                for c in range(1, NC):
                    ins = ts(qn[:, c * CH:(c + 1) * CH], qa[:, c * CH:(c + 1) * CH], cst[:, c - 1, DV:DV + 1],
                             None, ALU.mult)
                ins.then_inc(state_ok, 1)
                quarter(6, 2)
                for b in range(NB):
                    ts(vb[:, b, :], vt[0:SW, NC, 0:DV], wlast[:, b:b + 1], None, ALU.mult)
                conv_gate(6)
                quarter(6, 3)
                quarter(7, 0)
                dve.wait_ge(num_mm, hv)
                den_p, den_s = ps[:, 6, :], ps[:, 7, 2 * SW:3 * SW]
                stt(em[:, 0:TP], den_p, -1.0, em[:, 0:TP], ALU.mult, ALU.max)
                link(stt(em[:, TP:T], den_s, -1.0, em[:, TP:T], ALU.mult, ALU.max))
                tt(em[:, 0:TP], den_p, em[:, 0:TP], ALU.max)
                link(tt(em[:, TP:T], den_s, em[:, TP:T], ALU.max))
                dve.reciprocal(em[:, 0:HT], em[:, 0:HT])
                quarter(7, 1)
                link(dve.reciprocal(em[:, HT:T], em[:, HT:T]))
                for j, hh in ((0, flat(h0)), (1, flat(h1))):
                    tt(hh[:, 0:TP], ps[:, 4 + j, :], em[:, 0:TP], ALU.mult)
                    ins = tt(hh[:, TP:T], ps[:, 7, j * SW:(j + 1) * SW], em[:, TP:T], ALU.mult)
                ins.then_inc(h_ok, 1)
                quarter(7, 2)
                conv_input(7)
                quarter(7, 3)
                quarter(8, 0)
                dve.wait_ge(us_mm, hv)
                dve.wait_ge(cs_in, h * 16 + 16)
                for b in range(NB):
                    ins = stt(cs[:, b, :], cs[:, b, :], sc[:, NC + b:NC + b + 1],
                              ps[:, 4 + b // 2, (b % 2) * DV:(b % 2 + 1) * DV], ALU.mult, ALU.add)
                ins.then_inc(cs_ok, 1)
                quarter(8, 1)
                conv_sum(0)
                quarter(8, 2)
                conv_out(8, 0)
                quarter(8, 3)
                quarter(9, 0)
                conv_columns(1)
                dve.wait_ge(hs_mm, hv)
                to_rms(rh[:], side_halves(BLK_A), DV)
                dve.reciprocal(rh[:, 0, :], rh[:, 0, :])
                quarter(9, 1)
                dve.reciprocal(rh[:, 1, :], rh[:, 1, :]).then_inc(rh_in, 1)
                dve.wait_ge(ysq_ok, 2 * h + 1)
                sum_squares()
                quarter(9, 2)
                conv_gate(9)
                quarter(9, 3)
                quarter(10, 0)
                dve.wait_ge(rh_ok, hv)
                dve.wait_ge(so_ok, 2 * h + 2)
                for j, hh in ((0, h0), (1, h1)):
                    link(stt(hh[:], hh[:], gml[:, j:j + 1], rh[:], ALU.mult, ALU.mult))
                    ins = tt(mixf[:, ds(h * 4 + (2 * NG + 2 * j), 2), :], hh[:], so[:, j], ALU.mult)
                if last:
                    ins.then_inc(mix_heads, 1)
                quarter(10, 1)
                early(0, 2)
                quarter(10, 2)
                early(2, 4)
                conv_input(10)
                quarter(10, 3)
                early(4, 6)
                quarter(11, 0)
                quarter(11, 1)
                conv_sum(1)
                early(6, 8)
                quarter(11, 2)
                if last:
                    rows_from_psum()
                early(8, 10)
                conv_out(11, 1)
                quarter(11, 3)
                dve.wait_ge(ysq_ok, 2 * h + 2)
                sum_squares()
                if last:
                    return
                quarter(12, 0)
                head_columns(h + 1)
                quarter(12, 1)
                quarter(12, 2)
                done(12)
                evac(stt(qf[:], pair(1), QS, rstd[:], ALU.mult, ALU.mult))
                quarter(12, 3)
                for q in range(3):
                    quarter(13, q)
                done(13)
                evac(tt(kf[:], pair(2), rstd[:], ALU.mult))
                quarter(13, 3)

            def mix_low(n):
                k = MIX_K[n]
                dve.wait_ge(mix_hi, n + 1)
                tt(mixlo[:, 2 * k:2 * k + 2, :], mixf[:, 2 * k:2 * k + 2, :],
                   mixhi[:, 2 * k:2 * k + 2, :].bitcast(F32), ALU.subtract).then_inc(mix_lo, 1)

            def rows_from_psum():
                dve.wait_ge(tail_mm, 1)
                dve.tensor_copy(n_rows[:], ps[0:(NB + 1) * H, BLK_A + 1, 384:384 + P])
                dve.tensor_copy(conv_rows[:], side(BLK_B, DC)[0:2 + 2 * NB]).then_inc(rows_out, 1)

            LINKS_H = LINKS["head"]
            with dve.Fori(0, H - 1) as h:
                start = chain.enter(h, LINKS_H)
                round_of_head(h, False)
                chain.leave(start, H - 1, "head")
            round_of_head(H - 1, True)

            for n in range(10, KT):
                mix_low(n)
                if n == 11:
                    dve.wait_ge(ssc_mm, 1)
                    to_rms(rh[:], side_halves(BLK_A), DC)
            dve.reciprocal(rh[:, 0, :], rh[:, 0, :])
            split_out(I_OUT + 1, 0)
            dve.reciprocal(rh[:, 1, :], rh[:, 1, :]).then_inc(rc_in, 1)
            for q in range(1, 4):
                split_out(I_OUT + 1, q)
            link(dve.memset(ssq2[:], 0.0))
            dve.wait_ge(rc_ok, 1)

            def out_tile(n, parity, nxt):
                i = n + I_OUT
                x_n = ds(n * 2, 2)
                for q in range(3):
                    nxt(q)
                tile_done(i)
                link(tt(t2[:], conv_pair(parity), rh[:], ALU.mult))
                tt(t2[:], t2[:], pair(parity), ALU.add).then_inc(tile_read, 1)
                dve.wait_ge(tile_read, i + 2)
                link(tt(t2[:], t2[:], xhi[:, x_n, :].bitcast(F32), ALU.add))
                tt(x1[:], t2[:], xlo[:, x_n, :].bitcast(F32), ALU.add).then_inc(x1_ok, 1)
                nxt(3)
                dve.wait_ge(x1_hi, n + 1)
                tt(xlo[:, x_n, :], x1[:], xhi[:, x_n, :].bitcast(F32), ALU.subtract).then_inc(x1_lo, 1)
                dve.wait_ge(x1_sq, n + 1)
                tt(ssq2[:], ssq2[:], sq2[:], ALU.add).then_inc(ss2_ok, 1)
                dve.wait_ge(ss2_ok, n + 1)

            out_tile(0, I_OUT, lambda q: None)
            out_tile(1, I_OUT + 1, lambda q: split_out(I_OUT + 2, q))
            with dve.Fori(1, KT // 2 - 1) as n2:
                start = chain.enter(n2 - 1, LINKS["out"])
                for p in range(2):
                    n = n2 * 2 + p
                    out_tile(n, I_OUT + p, lambda q: split_out(n + (I_OUT + 1), q))
                chain.leave(start, KT // 2 - 2, "out")
            out_tile(KT - 2, I_OUT, lambda q: split_out(I_OUT + KT - 1, q))
            out_tile(KT - 1, I_OUT + 1, lambda q: split(I_FFN, q, V_G2))
            dve.wait_ge(ss2_mm, 1)
            to_rms(rstd[:], side_halves(BLK_A), D)
            dve.reciprocal(rstd[:], rstd[:]).then_inc(r2_in, 1)
            dve.wait_ge(r2_ok, 1)

            def up(c, f, i, nxt):
                for q in range(3):
                    split(i + 1, q, V_G2)
                tile_done(i)
                tt(gact[:], pair(I_FFN), rstd[:], ALU.mult).then_inc(tile_read, 1)
                split(i + 1, 3, V_G2)
                nxt(0)
                dve.wait_ge(s_ok, c * FC + (f + 1))
                link(tt(sact[:], sact[:], gact[:], ALU.mult))
                link(tt(sact[:], sact[:], rstd[:], ALU.mult))
                nxt(1)
                nxt(2)
                tile_done(i + 1)
                tt(hf[:], pair(I_FFN + 1), sact[:], ALU.mult).then_inc(tile_read, 1)
                nxt(3)
                dve.wait_ge(h_hi, c * FC + (f + 1))
                f_n = ds(f * 2, 2)
                tt(hlo[:, f_n, :], hf[:], hhi[:, f_n, :].bitcast(F32), ALU.subtract).then_inc(h_lo, 1)

            def up_phase(c, i0, what):
                with dve.Fori(0, FC - 1) as f:
                    start = chain.enter(f, LINKS["up"])
                    up(c, f, i0 + f * 2, lambda q: split(i0 + f * 2 + 2, q, V_G2))
                    chain.leave(start, FC - 1, "up")
                i = i0 + 2 * (FC - 1)
                up(c, FC - 1, i, lambda q: split(i + 2, q, sizes=K_DOWN))

            def down(n, i, parity, first, nxt):
                for q in range(3):
                    nxt(q)
                tile_done(i)
                a = acc[:, ds(n * 2, 2), :]
                if first:
                    tt(gact[:], pair(parity), xhi[:, ds(n * 2, 2), :].bitcast(F32), ALU.add).then_inc(tile_read, 1)
                    dve.wait_ge(tile_read, i + 2)
                    tt(a, gact[:], xlo[:, ds(n * 2, 2), :].bitcast(F32), ALU.add)
                else:
                    tt(a, pair(parity), a, ALU.add).then_inc(tile_read, 1)
                nxt(3)

            def chunk(c, first):
                i0 = c * PER_CH + I_FFN
                up_phase(c, i0, "up")
                i1 = i0 + 2 * FC
                with dve.Fori(0, KT // 2 - 1) as n2:
                    for p in range(2):
                        down(n2 * 2 + p, i1 + n2 * 2 + p, I_FFN + p, first,
                             lambda q: split(i1 + n2 * 2 + (p + 1), q, sizes=K_DOWN))
                down(KT - 2, i1 + (KT - 2), I_FFN, first, lambda q: split(i1 + (KT - 1), q, sizes=K_DOWN))
                down(KT - 1, i1 + (KT - 1), I_FFN + 1, first, lambda q: split(i0 + PER_CH, q, V_G2))

            dve.wait_ge(small_out, 16 * 6)
            chunk(0, True)
            with dve.Fori(1, NCH - 1) as c:
                start = chain.enter(c - 1, LINKS["chunk"])
                chunk(c, False)
                chain.leave(start, NCH - 2, "chunk")
            c, i0 = NCH - 1, I_FFN + (NCH - 1) * PER_CH
            i1 = i0 + 2 * FC
            up_phase(c, i0, "up")
            link(dve.memset(ssq_f[:], 0.0))

            def last_down(n, p, nxt=None):
                if nxt:
                    for q in range(3):
                        nxt(q)
                tile_done(n + i1)
                tt(zf[:, p], pair(I_FFN + p), acc[:, ds(n * 2, 2), :], ALU.add).then_inc(tile_read, 1)
                dve.wait_ge(tile_read, n + (i1 + 2))
                if not (isinstance(n, int) and n < 2):
                    dve.wait_ge(out_t, n - 1)
                ts(zgn[:, p], zf[:, p], vecs[:, ds(n + V_GF, 1)], None, ALU.mult).then_inc(zg_n, 1)
                if nxt:
                    nxt(3)
                dve.wait_ge(z_sq, n + 1)
                tt(ssq_f[:], ssq_f[:], sqf[:], ALU.add).then_inc(ssf_ok, 1)
                dve.wait_ge(ssf_ok, n + 1)

            for n in range(2):
                last_down(n, n, lambda q: split(i1 + n + 1, q, sizes=K_DOWN))
            with dve.Fori(1, KT // 2 - 1) as m:
                for p in range(2):
                    last_down(m * 2 + p, p, lambda q: split(m * 2 + (i1 + p + 1), q, sizes=K_DOWN))
            last_down(KT - 2, 0, lambda q: split(i1 + KT - 1, q, sizes=K_DOWN))
            last_down(KT - 1, 1)
            dve.wait_ge(rf_mm, 1)
            to_rms(ss_col[0:XTW, :], ps[0:XTW, 0, 0:XT], D)
            dve.reciprocal(ss_col[0:XTW, :], ss_col[0:XTW, :]).then_inc(rf_in, 1)
            dve.wait_ge(rf_ok, 1)
            dve.wait_ge(out_read, KT)
            for t in range(0, XT, 2):
                ts(otok[:, t, :], otok[:, t, :], ss_col[0:XTW, t:t + 1], None, ALU.mult).then_inc(yd_ready, 1)


_INS = ["x_prompt", "x_sample", "state_conv", "state_mlstm_C", "state_mlstm_n", "state_mlstm_m",
        "norm1_g", "w_in", "b_igate", "b_fgate", "conv_w", "conv_out_g", "mlstm_out_g", "w_out",
        "norm2_g", "w_ffn_gate", "w_ffn_up", "w_ffn_down", "final_norm_g"]


def kernel(**inputs):
    import numpy as _np
    import concourse.bacc as _bacc
    from concourse import mybir as _mybir
    from concourse.bass_utils import run_bass_kernel_spmd as _run

    xp, xs = inputs["x_prompt"].shape, inputs["x_sample"].shape
    _, nb, heads, dk, dv = inputs["state_mlstm_C"].shape
    taps, dc = inputs["conv_w"].shape[1:]
    out_shapes = [xp, xs, (1, 1, taps - 1, dc), (1, 1, heads, dk, dv), (1, 1, heads, dk), (1, 1, heads),
                  (1, nb, taps - 1, dc), (1, nb, heads, dk, dv), (1, nb, heads, dk), (1, nb, heads)]
    nc = _bacc.Bacc("TRN2", target_bir_lowering=False, num_devices=1)
    arrays, args = {}, []
    for name in _INS:
        a = _np.ascontiguousarray(inputs[name])
        arrays[f"in_{name}_dram"] = a
        args.append(nc.dram_tensor(f"in_{name}_dram", a.shape, _mybir.dt.from_np(a.dtype), kind="ExternalInput").ap())
    for i, shape in enumerate(out_shapes):
        args.append(nc.dram_tensor(f"out_{i}_dram", shape, _mybir.dt.float32, kind="ExternalOutput").ap())
    hybrid_trunk_step(nc, *args)
    r = _run(nc, [arrays], core_ids=[0])
    return tuple(r.results[0][f"out_{i}_dram"] for i in range(len(out_shapes)))
```

```python
from contextlib import ExitStack

import concourse.bass as bass
from concourse import mybir

P = 128
ALU = mybir.AluOpType
ACT = mybir.ActivationFunctionType
F32 = mybir.dt.float32
F32R = mybir.dt.float32r
EPS = 1e-6
XTW = 96
BLK_A, BLK_B = 4, 6
ds = bass.ds


class Chain:

    def __init__(self, eng, sem):
        self.eng, self.sem, self.n, self.terms = eng, sem, 0, []

    def value(self):
        v = self.n
        for reg, per in self.terms:
            v = reg * per + v
        return v

    def link(self, ins):
        ins.then_inc(self.sem, 1)
        self.n += 1
        self.eng.wait_ge(self.sem, self.value())

    def enter(self, reg, per):
        self.terms.append((reg, per))
        return self.n

    def leave(self, start, times, what):
        _, per = self.terms.pop()
        assert self.n - start == per, f"{what}: {self.n - start} links in a round"
        self.n = start + per * times


def hybrid_trunk_step(nc, x_prompt, x_sample, state_conv, state_C, state_n, state_m, norm1_g, w_in,
                      b_igate, b_fgate, conv_w, conv_out_g, mlstm_out_g, w_out, norm2_g, w_gate,
                      w_up, w_down, final_g, y_prompt, y_sample, p_conv, p_C, p_n, p_m,
                      s_conv, s_C, s_n, s_m):
    TP, D = x_prompt.shape[1], x_prompt.shape[2]
    NB, TS = x_sample.shape[0], x_sample.shape[1]
    T = TP + NB * TS
    HT = T // 2
    KT = D // P
    H, DK, DV = state_C.shape[2:]
    CW, DC = conv_w.shape[1:]
    NG = DC // P
    GH = NG // H
    FF = w_gate.shape[2]
    FT = FF // P
    NCH = 4
    FC = FT // NCH
    CH = P
    NC = TP // CH
    SW = T - TP
    XT = T // XTW
    assert T % (2 * XTW) == 0 and DK == P and DV == 2 * P and FC * NCH == FT and GH == 2
    assert DC == KT * P // 2 and H * DV == DC and SW == 64 and NC * CH == TP and CW == 3
    COL_B, COL_C, COL_X = 0, DC, 2 * DC
    COL_Q = 3 * DC
    COL_K = COL_Q + H * DK
    COL_V = COL_K + H * DK
    COL_O = COL_V + H * DV
    COL_G = COL_O + H * DV
    V_G2, V_GF, V_MIX, V_CW, V_N = 0, KT, 2 * KT, 3 * KT, 3 * KT + CW * NG
    V_G1 = V_N + NB * H
    assert V_G1 + KT <= P
    TILES_H = 6 + 3 * GH
    I_OUT = 1 + H * TILES_H
    I_FFN = I_OUT + KT
    PER_CH = 2 * FC + KT
    HALVES = tuple((n, a) for a in range(2) for n in (KT - 2, KT - 1))
    XH = XT // 2
    K_FULL = (4, 4, 4, 4)
    K_DOWN = (3, 3, 3, 2)
    assert sum(K_FULL) == KT and sum(K_DOWN) == FC
    MIX_K = tuple(range(NG, KT)) + tuple(range(NG))
    X_PIECES = ((0, 2), (2, 2), (4, 4), (8, 4), (12, 4))
    SMALLS = 10
    SQ_ACT = 4
    X_LAST = {k0 + n - 1: b for b, (k0, n) in enumerate(X_PIECES)}
    assert sum(n for _, n in X_PIECES) == KT
    QS = float(DK) ** -0.5

    with ExitStack() as ctx:
        sem = lambda name: ctx.enter_context(nc.semaphore(name))
        used = [0]
        base = nc.sbuf_base + 31 & ~31

        def at(name, shape, dt, off):
            return nc.alloc_sbuf_tensor_at(name, shape, dt, offset=base + off)

        def nbytes(shape):
            n = 4
            for s in shape[1:]:
                n *= s
            return n + 31 & ~31

        def keep(name, shape, dt=F32):
            t = at(name, shape, dt, used[0])
            used[0] += nbytes(shape)
            return t

        TOK = [P, 2, HT]
        flat = lambda t: t.rearrange("p a b -> p (a b)")
        xhi = keep("xhi", [P, 2 * KT, HT], F32R)
        xlo = keep("xlo", [P, 2 * KT, HT], F32R)
        wraw = keep("wraw", [P, 2, 8, P])
        whi = keep("whi", [P, 4, 4, P], F32R)
        wlo = keep("wlo", [P, 4, 4, P], F32R)
        ident = keep("ident", [P, P])
        ones = keep("ones", [P, P])
        vecs = keep("vecs", [P, P])
        conv_state = keep("conv_state", [P, NG, 16])
        rstd = keep("rstd", TOK)
        tails = keep("tails", [P, NG, 2 + 2 * NB])
        n_out = keep("n_out", [P, (NB + 1) * H])
        m_out = keep("m_out", [4, 1 + NB])
        m0 = keep("m0", [4, NB])
        ss_col = keep("ss_col", [P, XT])
        rstd_col = keep("rstd_col", [P, XT])
        R0 = used[0]
        XB = KT * T * 4

        def region(start):
            pos = [R0 + start]

            def take(name, shape, dt=F32):
                t = at(name, shape, dt, pos[0])
                pos[0] += nbytes(shape)
                assert base + pos[0] <= nc.sbuf_usable_end, (name, base + pos[0])
                return t
            take.pos = pos
            return take

        take = region(0)
        xtok = take("xtok", [XTW, XT, D])
        vrows = take("vrows", [V_G1, P])
        g1_rows = take("g1_rows", [KT, P])
        srows = take("srows", [2 * NB, DC])
        gw_raw = take("gw_raw", [P, KT, 2 * H])
        gw = take("gw", [P, KT, P], F32R)
        diag = take("diag", [XTW, XT, XTW])
        ss_part = take("ss_part", [XTW, XT, len(X_PIECES)])
        zg = take("zg", [4 * H, 2, HT])
        bias_c = take("bias_c", [XTW, 2 * H])
        zc = take("zc", [XTW, XT, 4 * H])
        gate = take("gate", [XTW, XT, 2 * H])
        col = {n: take("col_" + n, [XTW, XT, H]) for n in ("ax", "e", "u", "d", "z", "ln", "rec", "lf")}
        take = region(0)
        row = {n: take("row_" + n, [H, T]) for n in ("li", "lf", "mask", "b", "m", "pre", "l")}
        mprev = take("mprev", [H, NC + NB])
        rows = take("rows", [P, T])
        assert take.pos[0] <= R0 + XB
        take = region(0)
        mixf = take("mixf", [P, 2 * KT, HT])
        mixlo = at("mixlo", [P, 2 * KT, HT], F32R, R0)
        mixhi = at("mixhi", [P, 2 * KT, HT], F32R, R0 + XB)
        take = region(XB)
        qf = take("qf", TOK)
        kf = take("kf", TOK)
        v0f = take("v0f", TOK)
        v1f = take("v1f", TOK)
        qa = take("qa", [P, T])
        qn = take("qn", [P, T])
        vt = take("vt", [P, NC + 1, DV + 1])
        kt = take("kt", [P, NC + 1, P])
        wgt = take("wgt", [P, NC + 1, P])
        wlast = take("wlast", [SW, NB])
        cst = take("cst", [P, NC, DV + 1])
        cs = take("cs", [P, NB, DV])
        vb = take("vb", [SW, NB, DV])
        em = take("em", [P, T])
        so = take("so", [P, 2, 2, HT])
        sel = take("sel", [P, 3, P], F32R)
        sc = take("sc", [P, NC + NB])
        assert base + R0 + 2 * XB <= nc.sbuf_usable_end
        rows_hi = take("rows_hi", [P, T], F32R)
        rows_lo = take("rows_lo", [P, T], F32R)
        colall = take("colall", [P, NC + 1, H])
        colh = take("colh", [P, NC + 1])
        taps = take("taps", [P, CW])
        cstate = take("cstate", [P, 2 * NB])
        gml = take("gml", [P, 2])
        cg_at = take.pos[0] - R0
        cg = take("cg", TOK)
        u = take("u", TOK)
        cv = take("cv", TOK)
        sqy = take("sqy", TOK)
        ssq_c = take("ssq_c", TOK)
        rh = take("rh", TOK)
        take = region(cg_at)
        conv_rows = take("conv_rows", [2 + 2 * NB, DC])
        n_rows = take("n_rows", [(NB + 1) * H, P])
        h0, h1 = v0f, v1f
        take = region(2 * XB)
        x1 = take("x1", TOK)
        sq2 = take("sq2", TOK)
        ssq2 = take("ssq2", TOK)
        t2 = take("t2", TOK)
        take = region(0)
        acc = take("acc", [P, 2 * KT, HT])
        hhi = take("hhi", [P, 2 * FC, HT], F32R)
        hlo = take("hlo", [P, 2 * FC, HT], F32R)
        gact = take("gact", TOK)
        sact = take("sact", TOK)
        hf = take("hf", TOK)
        zf = take("zf", [P, 2, 2, HT])
        zgn = take("zgn", [P, 2, 2, HT])
        sqf, ssq_f = sact, gact
        otok = at("otok", [XTW, XT, D], F32, 0)

        ps = ctx.enter_context(nc.psum_tensor("ps", [P, 8, 512], F32))
        ps_flat = ps.rearrange("p a b -> p (a b)")
        pair = lambda i: ps[:, 2 * (i % 2):2 * (i % 2) + 2, 0:HT]
        side = lambda bank, n=T: ps_flat[:, bank * 512:bank * 512 + n]
        side_halves = lambda bank: ps[:, bank:bank + 2, 0:HT]
        conv_pair = lambda i: side_halves(BLK_A + 2 * (i % 2))

        raw_in = [sem("raw_in0"), sem("raw_in1")]
        gained = sem("gained")
        halves_free = sem("halves_free")
        hi_done, lo_done = sem("hi_done"), sem("lo_done")
        w_used = sem("w_used")
        tile_read = sem("tile_read")
        x_in = [sem(f"x_in{b}") for b in range(len(X_PIECES))]
        g1_in, gw_in, small_in = sem("g1_in"), sem("gw_in"), sem("small_in")
        ident_ok, xt_done, rows_ok = sem("ident_ok"), sem("xt_done"), sem("rows_ok")
        x_hi, x_lo, g1_t, vec_t = (sem(n) for n in ("x_hi", "x_lo", "g1_t", "vec_t"))
        gw_g, gw_hi, gw_lo, ss_ok, diag_ok, rb_mm, rb_rec, rstd_c_ok, rstd_ok = (
            sem(n) for n in ("gw_g", "gw_hi", "gw_lo", "ss_ok", "diag_ok", "rb_mm", "rb_rec", "rstd_c_ok",
                             "rstd_ok"))
        zg_t, lf_c_ok, gates_t, row_a_ok, ax_ok, e_ok, u_ok, ln_ok, m_ok, pre_ok, l_ok, rows_hi_ok, rows_lo_ok, l_t = (
            sem(n) for n in ("zg_t", "lf_c_ok", "gates_t", "row_a_ok", "ax_ok", "e_ok", "u_ok", "ln_ok",
                             "m_ok", "pre_ok", "l_ok", "rows_hi_ok", "rows_lo_ok", "l_t"))
        sel_ok, bc_mm, bc_read = (sem(n) for n in ("sel_ok", "bc_mm", "bc_read"))
        w_exp, w_masked, pool_chain = sem("w_exp"), sem("w_masked"), sem("pool_chain")
        k_s_mm, kt_ok, p_ok, v0_t, v0_ok, v1_t, v1_ok = (
            sem(n) for n in ("k_s_mm", "kt_ok", "p_ok", "v0_t", "v0_ok", "v1_t", "v1_ok"))
        den_ok = sem("den_ok")
        u_mm, state_ok, num_mm, h_ok, us_mm, cs_ok, hsq_ok, hsum_ok, hs_mm, rh_in, rh_ok = (
            sem(n) for n in ("u_mm", "state_ok", "num_mm", "h_ok", "us_mm", "cs_ok", "hsq_ok", "hsum_ok",
                             "hs_mm", "rh_in", "rh_ok"))
        so_ok, ysq_ok, cs_in, c_out = (
            sem(n) for n in ("so_ok", "ysq_ok", "cs_in", "c_out"))
        ssc_ok, ssc_mm, rc_in, rc_ok, mix_heads, mix_hi, mix_lo = (
            sem(n) for n in ("ssc_ok", "ssc_mm", "rc_in", "rc_ok", "mix_heads", "mix_hi", "mix_lo"))
        tails_ok, tail_mm, rows_out = sem("tails_ok"), sem("tail_mm"), sem("rows_out")
        x1_ok, x1_hi, x1_sq, x1_lo, ss2_ok, ss2_mm, r2_in, r2_ok = (
            sem(n) for n in ("x1_ok", "x1_hi", "x1_sq", "x1_lo", "ss2_ok", "ss2_mm", "r2_in", "r2_ok"))
        s_ok, h_hi, h_lo = (sem(n) for n in ("s_ok", "h_hi", "h_lo"))
        zg_n, z_sq, out_t, out_read, ssf_ok, rf_mm, rf_in, rf_ok = (
            sem(n) for n in ("zg_n", "z_sq", "out_t", "out_read", "ssf_ok", "rf_mm", "rf_in",
                             "rf_ok"))
        yd_ready, ya_ready = sem("yd_ready"), sem("ya_ready")
        dve_chain, out_done, small_out = sem("dve_chain"), sem("out_done"), sem("small_out")

        by_k = lambda w: w.rearrange("l (k p) n -> p (l k) n", p=P)
        w_in_k, w_out_k, w_gate_k, w_up_k, w_down_k = map(by_k, (w_in, w_out, w_gate, w_up, w_down))
        n_dram = state_n.rearrange("l b h d -> (l b h) d")

        block = ctx.enter_context(nc.Block())

        @block.sync
        def _(sp):
            def load(i, w_k, col, k_halves, first=False):
                for half, (k0, n) in enumerate(k_halves):
                    if not first:
                        sp.wait_ge(lo_done, 4 * (i - 2) + 2 * half + 2)
                        sp.sem_inc(halves_free, 1)
                    sp.dma_start(wraw[:, half, 0:n, :], w_k[:, ds(k0, n), ds(col, P)]).then_inc(raw_in[half], 16)

            full = ((0, 8), (8, 8))
            mix_order = ((MIX_K[0], 8), (MIX_K[8], 8))
            xp = x_prompt.rearrange("l t d -> (l t) d")
            xs = x_sample.rearrange("b t d -> (b t) d")
            last = TP - (XT - 1) * XTW
            for b, (k0, n) in enumerate(X_PIECES):
                c = slice(k0 * P, (k0 + n) * P)
                sp.dma_start(xtok[:, 0:XT - 1, c],
                             xp[0:TP - last, c].rearrange("(t p) d -> p t d", p=XTW)).then_inc(x_in[b], 16)
                sp.dma_start(xtok[0:last, XT - 1, c], xp[TP - last:TP, c]).then_inc(x_in[b], 16)
                sp.dma_start(xtok[last:XTW, XT - 1, c], xs[:, c]).then_inc(x_in[b], 16)

            def head(h, first=False):
                i = h * TILES_H + 1
                cols = [h * DK + COL_Q, h * DK + COL_K, h * DV + COL_V, h * DV + (COL_V + P),
                        h * DV + COL_O, h * DV + (COL_O + P)]
                for g in range(GH):
                    cols += [h * (GH * P) + (c + g * P) for c in (COL_C, COL_X, COL_B)]
                for j, col in enumerate(cols):
                    load(i + j, w_in_k, col, full, first=first and j == 0)
                    if first and j == 0:
                        small_inputs()

            def small_inputs():
                def small(dst, src):
                    sp.dma_start(dst, src).then_inc(small_in, 16)
                rows_of = lambda v: v.rearrange("l (k p) -> (l k) p", p=P)
                small(vrows[V_G2:V_G2 + KT, :], rows_of(norm2_g))
                small(vrows[V_GF:V_GF + KT, :], final_g.rearrange("(k p) -> k p", p=P))
                small(vrows[V_MIX:V_MIX + NG, :], rows_of(conv_out_g))
                small(vrows[V_MIX + NG:V_MIX + KT, :], rows_of(mlstm_out_g))
                small(vrows[V_CW:V_CW + CW * NG, :], conv_w.rearrange("l w (k p) -> (l w k) p", p=P))
                small(vrows[V_N:V_N + NB * H, :], n_dram)
                small(srows[:], state_conv.rearrange("l b r d -> (l b r) d"))
                small(bias_c[:, 0:H], b_igate.to_broadcast([XTW, H]))
                small(bias_c[:, H:2 * H], b_fgate.to_broadcast([XTW, H]))
                sp.dma_start(m0[:], state_m.rearrange("l b h -> (l h) b"), allow_slow_non_contiguous=True).then_inc(small_in, 16)

            head(0, first=True)
            with sp.Fori(1, H) as h:
                head(h)
            with sp.Fori(0, KT) as n:
                load(n + I_OUT, w_out_k, n * P, mix_order)
            def chunk(c, downs):
                with sp.Fori(0, FC) as f:
                    i = c * PER_CH + f * 2 + I_FFN
                    load(i, w_gate_k, c * (FC * P) + f * P, full)
                    load(i + 1, w_up_k, c * (FC * P) + f * P, full)
                with sp.Fori(0, downs) as n:
                    i = c * PER_CH + n + (I_FFN + 2 * FC)
                    load(i, w_down_k, n * P, ((c * FC, 6), (c * FC + 6, 5)))

            with sp.Fori(0, NCH - 1) as c:
                chunk(c, KT)
            c = NCH - 1
            chunk(c, KT - 2)
            for j, (n, _) in enumerate(HALVES):
                i = I_FFN + c * PER_CH + 2 * FC + KT - 2 + j
                load(i, w_down_k, n * P, ((c * FC, 6), (c * FC + 6, 5)))
            yp = y_prompt.rearrange("l t d -> (l t) d")
            ys = y_sample.rearrange("b t d -> (b t) d")
            for t in range(XT):
                half, place = divmod(t, XH)
                if place == 1:
                    sp.wait_ge(ya_ready, half + 1)
                else:
                    sp.wait_ge(yd_ready, 2 * half + place // 2 + 1)
                if t < XT - 1:
                    sp.dma_start(yp[t * XTW:(t + 1) * XTW, :], otok[:, t, :]).then_inc(out_done, 16)
                else:
                    sp.dma_start(yp[TP - last:TP, :], otok[0:last, t, :]).then_inc(out_done, 16)
                    sp.dma_start(ys[:, :], otok[last:XTW, t, :]).then_inc(out_done, 16)
            sp.wait_ge(out_done, 16 * (XT + 1))

        @block.tensor
        def _(pe):
            def gemm(i, hi, lo, ks, sizes, parts, ready=None, between={}, halves=(0, 1)):
                pe.wait_ge(tile_read, i)
                where = [(out, j == 0, j == count - 1) for count, out in parts for j in range(count)]
                n = 0
                for q, size in enumerate(sizes):
                    pe.wait_ge(lo_done, 4 * (i - 1) + q + 1)
                    for s in range(size):
                        if n in between:
                            between[n]()
                        if ready:
                            ready(n)
                        k, (out, first, last) = ks[n], where[n]
                        for moving in (hi, lo):
                            for a in halves:
                                pe.matmul(out[:, a, :], whi[:, q, s, :], moving[:, 2 * k + a, :],
                                          start=first and moving is hi, stop=False)
                        for a in halves:
                            mm = pe.matmul(out[:, a, :], wlo[:, q, s, :], hi[:, 2 * k + a, :],
                                           start=False, stop=last)
                        n += 1
                    mm.then_inc(w_used, 1)

            one = lambda out, lhsT, rhs, start=True, stop=True: pe.matmul(out, lhsT, rhs, start=start, stop=stop)

            pe.wait_ge(ident_ok, 2)
            pe.wait_ge(g1_in, 16)
            pe.transpose(ps[:, 0, 0:KT], g1_rows[:], ident[0:KT, 0:KT]).then_inc(g1_t, 1)

            def gates(k):
                pe.wait_ge(x_lo, k + 1)
                for moving in (xhi, xlo):
                    for a in range(2):
                        mm = pe.matmul(pair(0)[:, a, :], gw[:, k, :], moving[:, 2 * k + a, :],
                                       start=k == 0 and moving is xhi, stop=k == KT - 1 and moving is xlo)
                if k % 4 == 3:
                    mm.then_inc(w_used, 1)

            piece = {k0: b for b, (k0, _) in enumerate(X_PIECES)}
            for k in range(KT):
                if k in piece:
                    pe.wait_ge(x_in[piece[k]], 16 * 3)
                if k >= 3:
                    pe.wait_ge(x_lo, k - 2)
                for t in range(XT):
                    p0 = 2 * (k % 3 + 1) + t // 3
                    mm = pe.transpose(ps[:, p0, (t % 3) * XTW:(t % 3 + 1) * XTW],
                                      xtok[:, t, k * P:(k + 1) * P], ident[0:XTW, 0:XTW])
                mm.then_inc(xt_done, 1)
                if k == 3:
                    pe.wait_ge(gw_lo, 1)
                if k >= 3:
                    gates(k - 3)
            for k in range(KT - 3, KT):
                gates(k)

            def gates_by_token():
                pe.wait_ge(tile_read, 2)
                zgf = flat(zg)
                for t in range(XT):
                    mm = pe.transpose(ps[0:XTW, BLK_A, t * 4 * H:(t + 1) * 4 * H], zgf[:, t * XTW:(t + 1) * XTW],
                                      ident[0:4 * H, 0:4 * H])
                mm.then_inc(zg_t, 1)
                pe.wait_ge(small_in, 16 * SMALLS)
                pe.transpose(ps[:, BLK_A + 1, 0:V_G1], vrows[:], ident[0:V_G1, 0:V_G1])
                for g in range(NG):
                    mm = pe.transpose(ps[:, BLK_A + 1, P + g * 16:P + g * 16 + 16], srows[:, g * P:(g + 1) * P],
                                      ident[0:16, 0:16])
                mm.then_inc(vec_t, 1)

            def spread_rstd():
                pe.wait_ge(diag_ok, 1)
                for t in range(XT):
                    mm = one(ps[:, BLK_B + t // 3, (t % 3) * XTW:(t % 3 + 1) * XTW], ones[0:XTW, :], diag[:, t, :])
                mm.then_inc(rb_mm, 1)

            def gates_by_head():
                pe.wait_ge(lf_c_ok, 1)
                pe.wait_ge(rstd_ok, 1)
                for src, c0, bank in ((gate, 0, BLK_A), (col["lf"], 0, BLK_B)):
                    for t in range(XT):
                        mm = pe.transpose(ps[0:H, bank + t // 3, (t % 3) * XTW:(t % 3 + 1) * XTW],
                                          src[:, t, c0:c0 + H], ident[0:XTW, 0:XTW])
                mm.then_inc(gates_t, 1)

            def columns_l():
                pe.wait_ge(l_ok, 1)
                for c in range(NC + 1):
                    n = CH if c < NC else SW
                    mm = pe.transpose(ps[0:n, BLK_A, c * H:(c + 1) * H], row["l"][:, c * CH:c * CH + n],
                                      ident[0:H, 0:H])
                mm.then_inc(l_t, 1)

            heads = range(KT)

            def head_tile(h, j, between={}):
                i = h * TILES_H + 1 + j
                gemm(i, xhi, xlo, heads, K_FULL, [(KT, pair(1 + j))], between=between)

            head_tile(0, 0, {5: gates_by_token, 9: spread_rstd, 14: gates_by_head})
            head_tile(0, 1, {10: columns_l})
            pe.wait_ge(rows_lo_ok, 1)

            def round_of_head(h, last):
                i = h * TILES_H + 1
                hv = h + 1
                qff, kff, v0ff, v1ff = map(flat, (qf, kf, v0f, v1f))

                def tile(j, between={}):
                    head_tile(h, j, between)

                pe.wait_ge(sel_ok, hv)
                for s in range(3):
                    for part in (rows_hi, rows_lo):
                        first = part is rows_hi
                        one(ps[:, BLK_A + s, 0:TP], sel[:, s, :], part[:, 0:TP], first, not first)
                        mm = one(ps[:, BLK_A + 3, s * SW:(s + 1) * SW], sel[:, s, :], part[:, TP:T], first, not first)
                mm.then_inc(bc_mm, 1)
                tile(2)
                pe.wait_ge(tile_read, i + 2)
                pe.wait_ge(bc_read, hv)
                for c in range(NC + 1):
                    n = CH if c < NC else SW
                    tok = slice(c * CH, c * CH + n)
                    b = BLK_B if c < NC else BLK_B + 1
                    col = c * P if c < NC else 0
                    pe.transpose(ps[0:n, b, col:col + P], kff[:, tok], ident[:])
                    b = BLK_A if c < NC else BLK_A + 1
                    mm = one(ps[0:n, b, col:col + n], kff[:, tok], qff[:, tok])
                mm.then_inc(k_s_mm, 1)
                tile(3)

                def v_by_token(bank, src, done):
                    for c in range(NC + 1):
                        n = CH if c < NC else SW
                        b, col = (bank, c * P) if c < NC else (bank + 1, 0)
                        mm = pe.transpose(ps[0:n, b, col:col + P], src[:, c * CH:c * CH + n], ident[:])
                    mm.then_inc(done, 1)

                pe.wait_ge(tile_read, i + 3)
                pe.wait_ge(kt_ok, hv)
                v_by_token(BLK_B, v0ff, v0_t)
                tile(4)
                pe.wait_ge(tile_read, i + 4)
                pe.wait_ge(p_ok, hv)
                v_by_token(BLK_A, v1ff, v1_t)
                tile(5)
                pe.wait_ge(v0_ok, hv)
                pe.wait_ge(v1_ok, hv)
                for c in range(NC):
                    one(ps[:, 4 + c, 0:DV + 1], kt[:, c, :], vt[:, c, :])
                one(ps[:, 4, 300:300 + NB], kt[0:SW, NC, :], wlast[:]).then_inc(u_mm, 1)
                tile(6)
                pe.wait_ge(state_ok, hv)
                pe.wait_ge(cs_in, h * 16 + 16)
                for j in range(2):
                    val = slice(j * P, (j + 1) * P)
                    for c in range(NC):
                        tok = slice(c * CH, (c + 1) * CH)
                        out = ps[:, 4 + j, tok]
                        one(out, vt[:, c, val], wgt[:, c, :], stop=c == 0)
                        if c:
                            one(out, cst[:, c - 1, val], qa[:, tok], start=False)
                    out = ps[:, 7, j * SW:(j + 1) * SW]
                    one(out, vt[0:SW, NC, val], wgt[0:SW, NC, 0:SW], stop=False)
                    for b in range(NB):
                        one(out[:, b * TS:(b + 1) * TS], cs[:, b, val],
                            qa[:, TP + b * TS:TP + (b + 1) * TS], start=False, stop=b == NB - 1)
                pe.wait_ge(den_ok, hv)
                one(ps[:, 6, 0:TP], ones[:], qn[:, 0:TP])
                one(ps[:, 7, 2 * SW:3 * SW], ones[:], qn[:, TP:T]).then_inc(num_mm, 1)
                tile(7)
                pe.wait_ge(h_ok, hv)
                for b in range(NB // 2):
                    mm = one(ps[:, 4 + b, :], kt[0:SW, NC, :],
                             vb[:, 2 * b:2 * b + 2, :].rearrange("p a b -> p (a b)"))
                mm.then_inc(us_mm, 1)
                tile(8)
                pe.wait_ge(cs_ok, hv)
                pe.wait_ge(hsum_ok, hv)
                for a in range(2):
                    mm = one(ps[:, BLK_A + a, 0:HT], ones[:], kf[:, a, :])
                mm.then_inc(hs_mm, 1)
                tile(9)
                tile(10)
                tile(11)
                if not last:
                    head_tile(h + 1, 0)
                    head_tile(h + 1, 1)

            def tails_by_row():
                pe.wait_ge(tails_ok, 1)
                pe.transpose(ps[0:(NB + 1) * H, BLK_A + 1, 384:384 + P], n_out[:], ident[:])
                for g in range(NG):
                    b, c = BLK_B + g // 4, (g % 4) * P
                    mm = pe.transpose(ps[0:2 + 2 * NB, b, c:c + P], tails[:, g, :], ident[:])
                mm.then_inc(tail_mm, 1)

            with pe.Fori(0, H - 1) as h:
                round_of_head(h, False)
            round_of_head(H - 1, True)

            def conv_squares():
                pe.wait_ge(ssc_ok, 2 * H)
                pe.wait_ge(rows_out, 1)
                for a in range(2):
                    mm = one(ps[:, BLK_A + a, 0:HT], ones[:], ssq_c[:, a, :])
                mm.then_inc(ssc_mm, 1)

            def mix_ready(n):
                pe.wait_ge(mix_lo, n + 1)
                if n == NG:
                    pe.wait_ge(rows_out, 1)

            def out_tile(i, slot, between={}, ready=None):
                gemm(i, mixhi, mixlo, MIX_K, K_FULL, [(KT - NG, pair(slot)), (NG, conv_pair(slot))],
                     ready=ready, between=between)

            out_tile(I_OUT, I_OUT, {1: tails_by_row, NG + 1: conv_squares}, mix_ready)
            out_tile(I_OUT + 1, I_OUT + 1, {NG: lambda: pe.wait_ge(rc_in, 1)})
            with pe.Fori(1, KT // 2) as n2:
                for p in range(2):
                    out_tile(n2 * 2 + (I_OUT + p), I_OUT + p)

            def up_tile(i, p, between={}, ready=None):
                gemm(i, xhi, xlo, heads, K_FULL, [(KT, pair(I_FFN + p))], ready=ready, between=between)

            def up(i):
                for p in range(2):
                    up_tile(i + p, p)

            def down(i, c, slot, halves=(0, 1), between={}):
                def ready(n):
                    if n in (0, FC - 1):
                        pe.wait_ge(h_lo, c * FC + (FC - 1 if n == 0 else FC))
                gemm(i, hhi, hlo, range(FC), K_DOWN, [(FC, pair(slot))], ready=ready,
                     halves=halves, between=between)

            def norm_squares():
                pe.wait_ge(ss2_ok, KT)
                for a in range(2):
                    mm = one(ps[:, BLK_A + a, 0:HT], ones[:], ssq2[:, a, :])
                mm.then_inc(ss2_mm, 1)

            up_tile(I_FFN, 0, {8: norm_squares}, lambda n: pe.wait_ge(x1_lo, n + 1))
            up_tile(I_FFN + 1, 1)
            with pe.Fori(0, NCH - 1) as c:
                i0 = c * PER_CH + I_FFN
                with pe.Fori(1, FC) as f:
                    up(i0 + f * 2)
                with pe.Fori(0, KT // 2) as n2:
                    for p in range(2):
                        down(i0 + n2 * 2 + (2 * FC + p), c, I_FFN + p)
                up(i0 + PER_CH)
            i0 = I_FFN + (NCH - 1) * PER_CH
            with pe.Fori(1, FC) as f:
                up(i0 + f * 2)

            def turn(n, p, halves=(0, 1)):
                pe.wait_ge(zg_n, n + 1)
                if not (isinstance(n, int) and n < 2):
                    pe.wait_ge(out_read, n - 1)
                for t in [a * XH + b for a in halves for b in range(XH)]:
                    src = zgn[:, p, t // 3, (t % 3) * XTW:(t % 3 + 1) * XTW]
                    mm = pe.transpose(ps[0:XTW, 4 + 2 * p + t // 3, (t % 3) * P:(t % 3 + 1) * P], src, ident[:])
                mm.then_inc(out_t, 1)

            i1 = i0 + 2 * FC
            down(i1, NCH - 1, I_FFN)
            down(i1 + 1, NCH - 1, I_FFN + 1)
            turn(0, 0)
            down(i1 + 2, NCH - 1, I_FFN)
            turn(1, 1)
            down(i1 + 3, NCH - 1, I_FFN + 1)
            with pe.Fori(2, KT // 2 - 1) as n2:
                turn(n2 * 2 - 2, 0)
                down(n2 * 2 + i1, NCH - 1, I_FFN)
                turn(n2 * 2 - 1, 1)
                down(n2 * 2 + (i1 + 1), NCH - 1, I_FFN + 1)

            def result_squares(a):
                pe.wait_ge(ssf_ok, KT + 2 * a)
                for t in range(a * XH, (a + 1) * XH):
                    mm = one(ps[0:XTW, 2 - 2 * a, t:t + 1], ssq_f[:, a, (t - a * XH) * XTW:(t - a * XH + 1) * XTW],
                             ones[:, 0:1])
                mm.then_inc(rf_mm, 1)

            def turn_half(j):
                turn(KT - 2 + j, j % 2, (HALVES[j][1],))

            def down_half(j, between={}):
                down(i1 + KT - 2 + j, NCH - 1, I_FFN + j, (HALVES[j][1],), between)

            def first_half_done():
                turn_half(1)
                result_squares(0)

            turn(KT - 4, 0)
            down_half(0)
            turn(KT - 3, 1)
            down_half(1)
            turn_half(0)
            down_half(2, {9: first_half_done})
            down_half(3, {8: lambda: turn_half(2)})
            turn_half(3)
            result_squares(1)

        @block.scalar
        def _(act):
            def hi(i, q, sizes=K_FULL, gain=None):
                s0, n = sum(sizes[2 * (q // 2):q]), sizes[q]
                if gain is None:
                    act.wait_ge(raw_in[q // 2], i * 16)
                else:
                    act.wait_ge(gained, gain)
                act.wait_ge(w_used, 4 * (i - 1) + q + 1)
                act.activation(whi[:, q, 0:n, :], wraw[:, q // 2, s0:s0 + n, :], ACT.Copy).then_inc(hi_done, 1)

            act.dma_start(g1_rows[:], norm1_g.rearrange("l (k p) -> (l k) p", p=P)).then_inc(g1_in, 16)
            act.dma_start(gw_raw[:], w_in_k[:, :, COL_G:COL_G + 2 * H]).then_inc(gw_in, 16)
            act.wait_ge(ident_ok, 2)
            act.activation(rstd_col[:, 0:1], ident[:, 0:1], ACT.Copy)
            act.wait_ge(gw_g, 1)
            act.activation(gw[:, :, 0:2 * H], gw_raw[:], ACT.Copy).then_inc(gw_hi, 1)

            def square(b, t):
                k0, n = X_PIECES[b]
                x = xtok[:, t, k0 * P:(k0 + n) * P]
                act.activation(x, x, ACT.Square, accum_out=ss_part[:, t, b:b + 1]).then_inc(ss_ok, 1)

            squares = []
            for k in range(KT):
                p0 = 2 * (k % 3 + 1)
                act.wait_ge(xt_done, k + 1)
                act.activation(xhi[:, 2 * k:2 * k + 2, :], ps[:, p0:p0 + 2, 0:HT], ACT.Copy).then_inc(x_hi, 1)
                if k in X_LAST:
                    squares += [(X_LAST[k], t) for t in range(SQ_ACT)]
                if squares:
                    square(*squares.pop(0))
                if k in (KT - 4, KT - 2):
                    q = (k - (KT - 4)) // 2
                    hi(1, q, gain=q + 1)
            for b, t in squares:
                square(b, t)
            hi(1, 2, gain=3)
            hi(1, 3, gain=4)
            act.wait_ge(rb_rec, 1)
            act.activation(rstd_col[0:XTW, :], ss_col[0:XTW, :], ACT.Sqrt).then_inc(rstd_c_ok, 1)
            hi(2, 0, gain=5)
            act.wait_ge(ax_ok, 1)
            act.activation(col["e"][:], col["ax"][:], ACT.Exp, scale=-1.0).then_inc(e_ok, 1)
            act.wait_ge(u_ok, 1)
            act.activation(col["ln"][:], col["u"][:], ACT.Ln).then_inc(ln_ok, 1)
            hi(2, 1, gain=6)
            act.wait_ge(m_ok, 1)
            act.activation(rows[64:64 + H, :], row["m"][:], ACT.Exp, scale=-1.0).then_inc(rows_ok, 1)
            hi(2, 2, gain=7)
            hi(2, 3, gain=8)
            act.wait_ge(pre_ok, 1)
            act.activation(rows[32:32 + H, :], row["pre"][:], ACT.Exp).then_inc(rows_ok, 1)
            act.wait_ge(rows_ok, 2)
            hi(3, 0, gain=9)
            act.activation(rows_hi[:], rows[:], ACT.Copy).then_inc(rows_hi_ok, 1)
            hi(3, 1, gain=10)
            hi(3, 2, gain=11)
            act.dma_start(p_m.rearrange("l b h -> h (l b)"), m_out[:, 0:1]).then_inc(small_out, 16)
            act.dma_start(s_m.rearrange("l b h -> (l h) b"), m_out[:, 1:1 + NB], allow_slow_non_contiguous=True).then_inc(small_out, 16)

            def load_state(h):
                act.dma_start(cs[:], state_C[0, :, ds(h, 1)].rearrange("b h k v -> k (b h) v")).then_inc(cs_in, 16)

            load_state(0)
            hi(3, 3, gain=12)

            def mix_high(n):
                k = MIX_K[n]
                act.activation(mixhi[:, 2 * k:2 * k + 2, :], mixf[:, 2 * k:2 * k + 2, :],
                               ACT.Copy).then_inc(mix_hi, 1)

            def round_of_head(h, last):
                i = h * TILES_H + 1
                hv = h + 1

                def quarter(j, q):
                    n = i + (j + 1)
                    if last and j == TILES_H - 1:
                        out_hi(0, q)
                    else:
                        hi(n, q, gain=4 * (n - 1) + q + 1)

                act.wait_ge(bc_mm, hv)
                for c in range(NC):
                    act.activation(wgt[:, c, :], side(BLK_A)[:, c * CH:(c + 1) * CH], ACT.Exp,
                                   bias=colh[:, c:c + 1])
                act.activation(wgt[0:SW, NC, 0:SW], ps[0:SW, BLK_A + 3, 0:SW], ACT.Exp,
                               bias=colh[0:SW, NC:NC + 1]).then_inc(w_exp, 1)
                for j in (2, 3, 4):
                    for q in range(4):
                        quarter(j, q)
                for o in range(2):
                    quarter(5 + o, 0)
                    quarter(5 + o, 1)
                    act.wait_ge(tile_read, i + (4 + o + 2))
                    act.activation(so[:, o], so[:, o], ACT.Sigmoid).then_inc(so_ok, 1)
                    quarter(5 + o, 2)
                    quarter(5 + o, 3)
                act.wait_ge(state_ok, hv)
                act.dma_start(p_C[0, 0, ds(h, 1)].rearrange("h k v -> (h k) v"),
                              cst[:, NC - 1, 0:DV]).then_inc(c_out, 16)
                quarter(7, 0)
                quarter(7, 1)
                quarter(7, 2)
                quarter(7, 3)
                quarter(8, 0)
                act.wait_ge(h_ok, hv)
                act.activation(kf[:], h0[:], ACT.Square)
                act.activation(qf[:], h1[:], ACT.Square).then_inc(hsq_ok, 1)
                quarter(8, 1)
                quarter(8, 2)
                quarter(8, 3)
                act.wait_ge(cs_ok, hv)
                act.dma_start(s_C[0, :, ds(h, 1)].rearrange("b h k v -> k (b h) v"), cs[:]).then_inc(c_out, 16)
                act.wait_ge(tile_read, i + (8 + 2))
                act.activation(sqy[:], mixf[:, ds(h * 4, 2), :], ACT.Square).then_inc(ysq_ok, 1)
                for q in range(4):
                    quarter(9, q)
                act.wait_ge(rh_in, hv)
                act.activation(rh[:], rh[:], ACT.Sqrt).then_inc(rh_ok, 1)
                if last:
                    act.wait_ge(c_out, H * 32)
                    mix_high(0)
                    mix_high(1)
                    quarter(10, 0)
                    mix_high(2)
                    mix_high(3)
                    quarter(10, 1)
                    mix_high(4)
                    mix_high(5)
                    quarter(10, 2)
                    quarter(10, 3)
                    act.wait_ge(mix_heads, 1)
                    mix_high(6)
                    mix_high(7)
                    for q in range(4):
                        quarter(11, q)
                        if q < 3:
                            mix_high(8 + 2 * q)
                            mix_high(9 + 2 * q)
                    mix_high(14)
                else:
                    for j in (10, 11):
                        for q in range(4):
                            quarter(j, q)
                act.wait_ge(tile_read, i + (11 + 2))
                act.activation(sqy[:], mixf[:, ds(h * 4 + 2, 2), :], ACT.Square).then_inc(ysq_ok, 1)
                if last:
                    mix_high(15)
                else:
                    act.wait_ge(c_out, h * 32 + 32)
                    load_state(h + 1)
                    for j in (12, 13):
                        for q in range(4):
                            quarter(j, q)

            def out_hi(n, q):
                if q < 2:
                    hi(n + I_OUT, q)
                else:
                    hi(n + I_OUT, q, gain=n * 2 + (4 * (I_OUT - 1) + q - 1))

            with act.Fori(0, H - 1) as h:
                round_of_head(h, False)
            round_of_head(H - 1, True)

            act.wait_ge(rows_out, 1)
            act.dma_start(s_n.rearrange("l b h d -> (l b h) d"), n_rows[0:NB * H, :]).then_inc(small_out, 16)
            act.dma_start(p_n.rearrange("l b h d -> (l b h) d"), n_rows[NB * H:(NB + 1) * H, :]).then_inc(small_out, 16)
            act.dma_start(p_conv.rearrange("l b r d -> (l b r) d"), conv_rows[0:2, :]).then_inc(small_out, 16)
            act.dma_start(s_conv.rearrange("l b r d -> (l b r) d"), conv_rows[2:, :]).then_inc(small_out, 16)

            def out_tile(n, nxt):
                for q in range(4):
                    nxt(q)
                act.wait_ge(x1_ok, n + 1)
                act.activation(xhi[:, ds(n * 2, 2), :], x1[:], ACT.Copy).then_inc(x1_hi, 1)
                act.activation(sq2[:], x1[:], ACT.Square).then_inc(x1_sq, 1)

            GB = 4 * (I_OUT - 1) + 2 * KT

            def ffn_gain(c, f, p, q):
                return GB + c * (8 * FC) + f * 8 + (4 * p + q + 1)

            for q in range(4):
                out_hi(1, q)
            act.wait_ge(rc_in, 1)
            act.activation(rh[:], rh[:], ACT.Sqrt).then_inc(rc_ok, 1)
            out_tile(0, lambda q: None)
            with act.Fori(1, KT - 1) as n:
                out_tile(n, lambda q: out_hi(n + 1, q))
            out_tile(KT - 1, lambda q: hi(I_FFN, q, gain=GB + q + 1))
            for q in range(2):
                hi(I_FFN + 1, q, gain=ffn_gain(0, 0, 1, q))
            act.wait_ge(r2_in, 1)
            act.activation(rstd[:], rstd[:], ACT.Sqrt).then_inc(r2_ok, 1)
            hi(I_FFN + 1, 2, gain=ffn_gain(0, 0, 1, 2))
            hi(I_FFN + 1, 3, gain=ffn_gain(0, 0, 1, 3))

            def up(c, f, i, nxt, begun=False):
                if not begun:
                    for q in range(4):
                        hi(i + 1, q, gain=ffn_gain(c, f, 1, q))
                act.wait_ge(tile_read, i + 2)
                act.activation(sact[:], gact[:], ACT.Sigmoid).then_inc(s_ok, 1)
                for q in range(4):
                    nxt(q)
                act.wait_ge(tile_read, i + 3)
                act.activation(hhi[:, ds(f * 2, 2), :], hf[:], ACT.Copy).then_inc(h_hi, 1)

            def up_phase(c, i0, begun=False):
                up(c, 0, i0, lambda q: hi(i0 + 2, q, gain=ffn_gain(c, 1, 0, q)), begun)
                with act.Fori(1, FC - 1) as f:
                    up(c, f, i0 + f * 2, lambda q: hi(i0 + f * 2 + 2, q, gain=ffn_gain(c, f + 1, 0, q)))
                i = i0 + 2 * (FC - 1)
                up(c, FC - 1, i, lambda q: hi(i + 2, q, K_DOWN))

            def chunk(c, first):
                i0 = c * PER_CH + I_FFN
                up_phase(c, i0, first)
                with act.Fori(0, KT - 1) as n:
                    for q in range(4):
                        hi(i0 + n + (2 * FC + 1), q, K_DOWN)
                for q in range(4):
                    hi(i0 + PER_CH, q, gain=ffn_gain(c + 1, 0, 0, q))

            chunk(0, True)
            with act.Fori(1, NCH - 1) as c:
                chunk(c, False)
            c, i0 = NCH - 1, I_FFN + (NCH - 1) * PER_CH
            up_phase(c, i0)

            def last_down(n, p, nxt, halves=slice(0, 2)):
                nxt()
                act.wait_ge(tile_read, n + (i1 + 2))
                act.activation(sqf[:, halves], zf[:, p, halves], ACT.Square).then_inc(z_sq, 1)

            def put(n, p, tile=None, halves=(0, 1)):
                act.wait_ge(out_t, n + 1)
                col = ds((n if tile is None else tile) * P, P)
                for b in halves:
                    ins = act.activation(otok[:, 3 * b:3 * b + 3, col],
                                         ps[0:XTW, 4 + 2 * p + b, 0:3 * P].rearrange("p (c f) -> p c f", f=P),
                                         ACT.Copy)
                ins.then_inc(out_read, 1)

            i1 = i0 + 2 * FC

            def all_hi(i):
                for q in range(4):
                    hi(i, q, K_DOWN)

            last_down(0, 0, lambda: all_hi(i1 + 1))
            last_down(1, 1, lambda: all_hi(i1 + 2))
            put(0, 0)
            last_down(2, 0, lambda: all_hi(i1 + 3))
            with act.Fori(1, KT // 2 - 2) as m:
                last_down(m * 2 + 1, 1, lambda: all_hi(m * 2 + (i1 + 2)))
                put(m * 2 - 1, 1)
                last_down(m * 2 + 2, 0, lambda: all_hi(m * 2 + (i1 + 3)))
                put(m * 2, 0)
            last_down(KT - 3, 1, lambda: all_hi(i1 + KT - 2))
            put(KT - 5, 1)

            def half_step(j, nxt):
                last_down(KT - 2 + j, j % 2, nxt, slice(HALVES[j][1], HALVES[j][1] + 1))

            def put_half(j):
                put(KT - 2 + j, j % 2, HALVES[j][0], (HALVES[j][1],))

            def root_half(a):
                act.wait_ge(rf_in, a + 1)
                c = ss_col[0:XTW, a * XH:(a + 1) * XH]
                act.activation(c, c, ACT.Sqrt).then_inc(rf_ok, 1)

            def scale_middle(a):
                act.wait_ge(rf_ok, a + 1)
                t = a * XH + 1
                act.mul(otok[:, t, :], otok[:, t, :], ss_col[0:XTW, t:t + 1]).then_inc(ya_ready, 1)

            half_step(0, lambda: all_hi(i1 + KT - 1))
            put(KT - 4, 0)
            half_step(1, lambda: all_hi(i1 + KT))
            put(KT - 3, 1)
            i = i1 + KT + 1
            hi(i, 0, K_DOWN)
            put_half(0)
            hi(i, 1, K_DOWN)
            hi(i, 2, K_DOWN)
            put_half(1)
            hi(i, 3, K_DOWN)
            root_half(0)
            half_step(2, lambda: None)
            scale_middle(0)
            put_half(2)
            half_step(3, lambda: None)
            put_half(3)
            root_half(1)
            scale_middle(1)
            act.wait_ge(small_out, 16 * 6)

        @block.gpsimd
        def _(pool):
            pool.memset(ident[:], 0.0).then_inc(ident_ok, 1)
            pool.wait_ge(ident_ok, 1)
            pool.affine_select(out=ident[:], in_=ident[:], compare_op=ALU.not_equal, fill=1.0, base=0,
                               pattern=[[-1, P]], channel_multiplier=1).then_inc(ident_ok, 1)
            for h in range(H):
                pool.wait_ge(w_exp, h + 1)
                wp = wgt[:, 0:NC, :]
                pool.affine_select(out=wp, in_=wp, compare_op=ALU.is_ge, fill=0.0, base=0,
                                   pattern=[[0, NC], [1, CH]], channel_multiplier=-1)
                ws = wgt[0:SW, NC, 0:SW].rearrange("p (b t) -> p b t", t=TS)
                pool.affine_select(out=ws, in_=ws, compare_op=ALU.is_ge, fill=0.0, base=0,
                                   pattern=[[TS, NB], [1, TS]], channel_multiplier=-1).then_inc(pool_chain, 1)
                pool.wait_ge(pool_chain, h + 1)
                pool.affine_select(out=ws, in_=ws, compare_op=ALU.is_ge, fill=0.0, base=0,
                                   pattern=[[-TS, NB], [0, TS]], channel_multiplier=1).then_inc(w_masked, 1)
                pool.wait_ge(state_ok, h + 1)
                pool.tensor_copy(qn[:, 0:CH], wgt[:, 0, :])
                pool.tensor_tensor(qn[:, CH:TP].rearrange("p (c t) -> p c t", t=CH),
                                   qn[:, CH:TP].rearrange("p (c t) -> p c t", t=CH), wgt[:, 1:NC, :], ALU.add)
                pool.tensor_tensor(qn[0:SW, TP:T], qn[0:SW, TP:T], wgt[0:SW, NC, 0:SW], ALU.add).then_inc(den_ok, 1)
                pool.wait_ge(hsq_ok, h + 1)
                pool.tensor_tensor(kf[:], kf[:], qf[:], ALU.add).then_inc(hsum_ok, 1)

        @block.vector
        def _(dve):
            chain = Chain(dve, dve_chain)
            LINKS = {"head": 32, "out": 4, "up": 2, "chunk": 2 * FC}
            link = chain.link
            tt, ts, stt = dve.tensor_tensor, dve.tensor_scalar, dve.scalar_tensor_tensor

            def gain(i, q, col):
                dve.wait_ge(raw_in[q // 2], i * 16)
                w = wraw[:, q // 2, 4 * (q % 2):4 * (q % 2) + 4, :]
                g = vecs[:, col + 4 * q:col + 4 * q + 4].unsqueeze(2).to_broadcast([P, 4, P])
                tt(w, w, g, ALU.mult).then_inc(gained, 1)

            def low(i, q, sizes=K_FULL):
                s0, n = sum(sizes[2 * (q // 2):q]), sizes[q]
                dve.wait_ge(hi_done, 4 * (i - 1) + q + 1)
                tt(wlo[:, q, 0:n, :], wraw[:, q // 2, s0:s0 + n, :], whi[:, q, 0:n, :].bitcast(F32),
                   ALU.subtract).then_inc(lo_done, 1)

            def split(i, q, col=None, sizes=K_FULL):
                if col is not None:
                    if q == 0:
                        gain(i, 0, col)
                    if q < 3:
                        gain(i, q + 1, col)
                low(i, q, sizes)

            def split_out(i, q):
                if q in (1, 2):
                    gain(i, q + 1, V_MIX - NG)
                low(i, q)

            def tile_done(i):
                dve.wait_ge(w_used, 4 * i + 4)

            def to_rms(out, total, n):
                link(ts(out, total, 1.0 / n, EPS, ALU.mult, ALU.add))

            link(dve.memset(gw[:].bitcast(F32), 0.0))
            dve.memset(ones[:], 1.0)
            dve.wait_ge(g1_t, 1)
            dve.tensor_copy(vecs[:, V_G1:V_G1 + KT], ps[:, 0, 0:KT]).then_inc(tile_read, 1)
            dve.wait_ge(tile_read, 1)
            dve.wait_ge(gw_in, 16)
            g1 = vecs[:, V_G1:V_G1 + KT].unsqueeze(2).to_broadcast([P, KT, 2 * H])
            tt(gw_raw[:], gw_raw[:], g1, ALU.mult).then_inc(gw_g, 1)
            dve.wait_ge(gw_hi, 1)
            tt(gw[:, :, 2 * H:4 * H], gw_raw[:], gw[:, :, 0:2 * H].bitcast(F32), ALU.subtract).then_inc(gw_lo, 1)
            dve.memset(ssq_c[:], 0.0)
            def square(b, t):
                k0, n = X_PIECES[b]
                x = xtok[:, t, k0 * P:(k0 + n) * P]
                return stt(x, x, 1.0, x, ALU.mult, ALU.mult, accum_out=ss_part[:, t, b:b + 1])

            squares = []
            for k in range(KT):
                p0 = 2 * (k % 3 + 1)
                dve.wait_ge(x_hi, k + 1)
                tt(xlo[:, 2 * k:2 * k + 2, :], ps[:, p0:p0 + 2, 0:HT],
                   xhi[:, 2 * k:2 * k + 2, :].bitcast(F32), ALU.subtract).then_inc(x_lo, 1)
                if k in X_LAST:
                    squares += [(X_LAST[k], t) for t in range(SQ_ACT, XT)]
                if squares and k % 2:
                    square(*squares.pop(0))
                if k in (KT - 4, KT - 2):
                    split(1, (k - (KT - 4)) // 2, V_G1)
            for b, t in squares:
                ins = square(b, t)
            link(ins)
            tile_done(0)
            dve.tensor_copy(zg[:], pair(0)[0:4 * H]).then_inc(tile_read, 1)
            split(1, 2, V_G1)
            split(1, 3, V_G1)
            dve.wait_ge(ss_ok, len(X_PIECES) * SQ_ACT)
            link(dve.tensor_reduce(ss_col[0:XTW, :], ss_part[:], mybir.AxisListType.X, ALU.add))
            to_rms(ss_col[0:XTW, :], ss_col[0:XTW, :], D)
            dve.reciprocal(ss_col[0:XTW, :], ss_col[0:XTW, :]).then_inc(rb_rec, 1)
            dve.wait_ge(rstd_c_ok, 1)
            for t in range(XT):
                ins = ts(diag[:, t, :], ident[0:XTW, 0:XTW], rstd_col[0:XTW, t:t + 1], None, ALU.mult)
            ins.then_inc(diag_ok, 1)
            dve.wait_ge(zg_t, 1)
            dve.wait_ge(small_in, 16 * SMALLS)
            link(dve.tensor_copy(zc[:], ps[0:XTW, BLK_A, 0:XT * 4 * H].rearrange("p (t c) -> p t c", c=4 * H)))
            link(tt(gate[:], zc[:, :, 0:2 * H], zc[:, :, 2 * H:4 * H], ALU.add))
            link(tt(gate[:], gate[:], rstd_col[0:XTW, :].unsqueeze(2).to_broadcast([XTW, XT, 2 * H]), ALU.mult))
            link(tt(gate[:], gate[:], bias_c[:].unsqueeze(1).to_broadcast([XTW, XT, 2 * H]), ALU.add))
            f = gate[:, :, H:2 * H]
            stt(col["ax"][:], f, -1.0, f, ALU.mult, ALU.max).then_inc(ax_ok, 1)
            split(2, 0, V_G1)
            r = col
            dve.wait_ge(e_ok, 1)
            ts(r["u"][:], r["e"][:], 1.0, None, ALU.add).then_inc(u_ok, 1)
            dve.wait_ge(u_ok, 1)
            link(ts(r["d"][:], r["u"][:], 1.0, None, ALU.subtract))
            link(ts(r["z"][:], r["d"][:], 0.0, None, ALU.is_equal))
            link(tt(r["d"][:], r["d"][:], r["z"][:], ALU.add))
            link(dve.reciprocal(r["rec"][:], r["d"][:]))
            link(tt(r["rec"][:], r["rec"][:], r["e"][:], ALU.mult))
            dve.wait_ge(ln_ok, 1)
            link(tt(r["z"][:], r["z"][:], r["ln"][:], ALU.add))
            link(tt(r["z"][:], r["z"][:], r["rec"][:], ALU.mult))
            stt(r["lf"][:], f, 0.0, r["z"][:], ALU.min, ALU.subtract).then_inc(lf_c_ok, 1)
            dve.wait_ge(vec_t, 1)
            dve.tensor_copy(vecs[:, 0:V_G1], ps[:, BLK_A + 1, 0:V_G1])
            dve.tensor_copy(conv_state[:], ps[:, BLK_A + 1, P:2 * P].rearrange("p (g r) -> p g r", r=16))
            split(2, 1, V_G1)
            dve.wait_ge(rb_mm, 1)
            dve.tensor_copy(rstd[:], side_halves(BLK_B)).then_inc(rstd_ok, 1)
            dve.wait_ge(rstd_ok, 1)
            dve.memset(rows[:], 0.0)
            dve.memset(vt[:, :, DV:DV + 1], 1.0)
            dve.memset(mprev[:, 0:1], 0.0)
            dve.tensor_copy(mprev[:, NC:NC + NB], m0[:])
            r = row
            link(dve.memset(r["mask"][:], 1.0))
            dve.memset(r["mask"][:, 0:TP:CH], 0.0)
            link(dve.memset(r["mask"][:, TP:T:TS], 0.0))
            dve.wait_ge(gates_t, 1)
            dve.tensor_copy(r["li"].rearrange("p (a b) -> p a b", a=2), side_halves(BLK_A)[0:H])
            link(dve.tensor_copy(r["lf"].rearrange("p (a b) -> p a b", a=2), side_halves(BLK_B)[0:H]))
            dve.tensor_tensor_scan(r["b"][:], r["mask"][:], r["lf"][:], 0.0, ALU.mult, ALU.add)
            ins = dve.tensor_tensor_scan(r["m"][:, 0:TP], r["lf"][:, 0:TP], r["li"][:, 0:TP], 0.0, ALU.add, ALU.max)
            for b in range(NB):
                s = slice(TP + b * TS, TP + (b + 1) * TS)
                ins = dve.tensor_tensor_scan(r["m"][:, s], r["lf"][:, s], r["li"][:, s], m0[:, b:b + 1],
                                             ALU.add, ALU.max)
            ins.then_inc(m_ok, 1)
            dve.wait_ge(m_ok, 1)
            split(2, 2, V_G1)
            tile_done(1)
            stt(qf[:], pair(1), QS, rstd[:], ALU.mult, ALU.mult).then_inc(tile_read, 1)
            split(2, 3, V_G1)
            dve.tensor_copy(m_out[:, 0:1], r["m"][:, TP - 1:TP])
            dve.tensor_copy(m_out[:, 1:1 + NB], r["m"][:, TP + TS - 1:T:TS])
            dve.tensor_copy(mprev[:, 1:NC], r["m"][:, CH - 1:TP - 1:CH])
            tt(r["l"][:], r["li"][:], r["b"][:], ALU.subtract).then_inc(l_ok, 1)
            tt(rows[0:H, :], r["b"][:], r["m"][:], ALU.subtract).then_inc(row_a_ok, 1)
            dve.wait_ge(row_a_ok, 1)
            tt(r["pre"][:, 0:TP].rearrange("p (c t) -> p c t", t=CH), rows[0:H, 0:TP].rearrange("p (c t) -> p c t", t=CH),
               mprev[:, 0:NC].unsqueeze(2).to_broadcast([H, NC, CH]), ALU.add)
            tt(r["pre"][:, TP:T].rearrange("p (b t) -> p b t", t=TS), rows[0:H, TP:T].rearrange("p (b t) -> p b t", t=TS),
               mprev[:, NC:].unsqueeze(2).to_broadcast([H, NB, TS]), ALU.add).then_inc(pre_ok, 1)
            split(3, 0, V_G1)
            dve.wait_ge(rows_hi_ok, 1)
            tt(rows_lo[:], rows[:], rows_hi[:].bitcast(F32), ALU.subtract).then_inc(rows_lo_ok, 1)
            dve.wait_ge(l_t, 1)
            dve.tensor_copy(colall[:, 0:NC, :], ps[:, BLK_A, 0:NC * H].rearrange("p (c h) -> p c h", h=H))
            link(dve.tensor_copy(colall[0:SW, NC, :], ps[0:SW, BLK_A, NC * H:(NC + 1) * H]))

            def head_columns(h):
                for s in range(3):
                    dve.tensor_copy(sel[:, s, :], ident[:, ds(h + 32 * s, 1)].to_broadcast([P, P]))
                dve.tensor_copy(gml[:], vecs[:, ds(h * 2 + (V_MIX + NG), 2)])
                dve.tensor_copy(colh[:, 0:NC], colall[:, 0:NC, ds(h, 1)].rearrange("p c h -> p (c h)"))
                dve.tensor_copy(colh[0:SW, NC:NC + 1], colall[0:SW, NC, ds(h, 1)]).then_inc(sel_ok, 1)

            head_columns(0)
            split(3, 1, V_G1)
            split(3, 2, V_G1)
            tile_done(2)
            tt(kf[:], pair(2), rstd[:], ALU.mult).then_inc(tile_read, 1)
            split(3, 3, V_G1)

            def round_of_head(h, last):
                i = h * TILES_H + 1
                hv = h + 1

                def quarter(j, q):
                    n = i + (j + 1)
                    if last and j == TILES_H - 1:
                        split_out(n, q)
                    else:
                        split(n, q, V_G1)

                def done(j):
                    tile_done(i + j)

                def evac(ins):
                    ins.then_inc(tile_read, 1)

                quarter(2, 0)
                dve.wait_ge(bc_mm, hv)
                dve.wait_ge(tile_read, i + 2)
                decay, low_bound, sampled = ps[:, BLK_A + 1, :], ps[:, BLK_A + 2, :], ps[:, BLK_A + 3, :]
                tt(qa[:, 0:TP], flat(qf)[:, 0:TP], decay, ALU.mult)
                dve.tensor_copy(sc[:, 0:NC], decay[:, CH - 1:TP:CH])
                dve.tensor_copy(em[:, 0:TP], low_bound)
                dve.wait_ge(w_exp, hv)
                tt(qa[:, TP:T], flat(qf)[:, TP:T], sampled[:, SW:2 * SW], ALU.mult)
                dve.tensor_copy(sc[:, NC:], sampled[:, SW + TS - 1:2 * SW:TS])
                dve.tensor_copy(em[:, TP:T], sampled[:, 2 * SW:3 * SW]).then_inc(bc_read, 1)
                quarter(2, 1)
                quarter(2, 2)
                done(2)
                evac(tt(v0f[:], pair(3), rstd[:], ALU.mult))
                quarter(2, 3)
                quarter(3, 0)
                dve.wait_ge(k_s_mm, hv)
                dve.wait_ge(w_masked, hv)
                for c in range(NC):
                    ts(kt[:, c, :], ps[:, BLK_B, c * P:(c + 1) * P], wgt[:, c, CH - 1:CH], None, ALU.mult)
                dve.tensor_copy(wlast[:], wgt[0:SW, NC, TS - 1:SW:TS])
                dve.tensor_copy(kt[0:SW, NC, :], ps[0:SW, BLK_B + 1, 0:P]).then_inc(kt_ok, 1)
                quarter(3, 1)
                dve.wait_ge(kt_ok, hv)
                tt(wgt[:, 0:NC, :], ps[:, BLK_A, :].rearrange("p (c t) -> p c t", t=CH), wgt[:, 0:NC, :], ALU.mult)
                tt(wgt[0:SW, NC, 0:SW], ps[0:SW, BLK_A + 1, 0:SW], wgt[0:SW, NC, 0:SW], ALU.mult).then_inc(p_ok, 1)
                quarter(3, 2)
                done(3)
                evac(tt(v1f[:], pair(4), rstd[:], ALU.mult))
                quarter(3, 3)

                def v_evac(half, bank, ok):
                    cols = slice(half * P, (half + 1) * P)
                    dve.tensor_copy(vt[:, 0:NC, cols], ps[:, bank, :].rearrange("p (c v) -> p c v", v=P))
                    dve.tensor_copy(vt[0:SW, NC, cols], ps[0:SW, bank + 1, 0:P]).then_inc(ok, 1)

                quarter(4, 0)
                dve.wait_ge(v0_t, hv)
                v_evac(0, BLK_B, v0_ok)
                quarter(4, 1)
                quarter(4, 2)
                done(4)
                evac(tt(so[:, 0], pair(5), rstd[:], ALU.mult))
                quarter(4, 3)
                quarter(5, 0)
                dve.wait_ge(v1_t, hv)
                v_evac(1, BLK_A, v1_ok)
                quarter(5, 1)
                quarter(5, 2)
                done(5)
                evac(tt(so[:, 1], pair(6), rstd[:], ALU.mult))
                quarter(5, 3)

                def early(n0, n1):
                    if last:
                        for n in range(n0, n1):
                            mix_low(n)

                def sum_squares():
                    tt(ssq_c[:], ssq_c[:], sqy[:], ALU.add).then_inc(ssc_ok, 1)

                def conv_columns(g):
                    for w in range(CW):
                        dve.tensor_copy(taps[:, w:w + 1], vecs[:, ds(h * 2 + (V_CW + w * NG + g), 1)])
                    link(dve.tensor_copy(cstate[:], conv_state[:, ds(h * 2 + g, 1), :].rearrange("p g r -> p (g r)")))

                def conv_gate(j):
                    done(j)
                    evac(tt(cg[:], pair(1 + j), rstd[:], ALU.mult))
                    dve.wait_ge(tile_read, i + (j + 2))
                    link(tt(cg[:], cg[:], rstd[:], ALU.mult))

                uf, cf = flat(u), flat(cv)
                us = uf[:, TP:T].rearrange("p (b t) -> p b t", t=TS)
                cvs = cf[:, TP:T].rearrange("p (b t) -> p b t", t=TS)
                st = cstate.rearrange("p (b r) -> p b r", r=2)

                def add_tap(dst, src, w):
                    link(stt(dst, src, taps[:, w:w + 1], dst, ALU.mult, ALU.add))

                def conv_input(j):
                    done(j)
                    evac(tt(u[:], pair(1 + j), cg[:], ALU.mult))
                    dve.wait_ge(tile_read, i + (j + 2))

                def conv_sum(g):
                    link(ts(cf, uf, taps[:, 2:3], None, ALU.mult))
                    add_tap(cf[:, 1:TP], uf[:, 0:TP - 1], 1)
                    add_tap(cf[:, 2:TP], uf[:, 0:TP - 2], 0)
                    add_tap(cvs[:, :, 1:TS], us[:, :, 0:TS - 1], 1)
                    add_tap(cvs[:, :, 0:1], st[:, :, 1:2], 1)
                    add_tap(cvs[:, :, 2:TS], us[:, :, 0:TS - 2], 0)
                    add_tap(cvs[:, :, 0:2], st, 0)
                    dve.tensor_copy(tails[:, ds(h * 2 + g, 1), 0:2], uf[:, TP - 2:TP].unsqueeze(1))
                    dve.tensor_copy(tails[:, ds(h * 2 + g, 1), 2:].rearrange("p g (b r) -> p (g b) r", r=2),
                                    us[:, :, TS - 2:TS])
                    ins = tt(cv[:], cv[:], rstd[:], ALU.mult)
                    if last and g == 1:
                        ins.then_inc(tails_ok, 1)
                        dve.wait_ge(tails_ok, 1)
                    else:
                        link(ins)

                def conv_out(j, g):
                    done(j)
                    evac(tt(mixf[:, ds(h * 4 + 2 * g, 2), :], pair(1 + j), cv[:], ALU.mult))

                quarter(6, 0)
                conv_columns(0)
                dve.wait_ge(u_mm, hv)
                link(dve.tensor_copy(cst[:, 0, :], ps[:, 4, 0:DV + 1]))
                for c in range(1, NC):
                    link(stt(cst[:, c, :], cst[:, c - 1, :], sc[:, c:c + 1], ps[:, 4 + c, 0:DV + 1],
                             ALU.mult, ALU.add))
                quarter(6, 1)
                n_old = vecs[:, V_N:V_N + NB * H].rearrange("p (b h) -> p b h", h=H)[:, :, ds(h, 1)]
                n_new = n_out[:, 0:NB * H].rearrange("p (b h) -> p b h", h=H)[:, :, ds(h, 1)]
                qs3 = qa[:, TP:T].rearrange("p (b t) -> p b t", t=TS)
                tt(qn[:, TP:T].rearrange("p (b t) -> p b t", t=TS), qs3, n_old.to_broadcast([P, NB, TS]), ALU.mult)
                link(tt(n_new, n_old, sc[:, NC:].unsqueeze(2), ALU.mult))
                link(tt(n_new, n_new, ps[:, 4, 300:300 + NB].unsqueeze(2), ALU.add))
                dve.tensor_copy(n_out[:, ds(h + NB * H, 1)], cst[:, NC - 1, DV:DV + 1])
                for c in range(1, NC):
                    ins = ts(qn[:, c * CH:(c + 1) * CH], qa[:, c * CH:(c + 1) * CH], cst[:, c - 1, DV:DV + 1],
                             None, ALU.mult)
                ins.then_inc(state_ok, 1)
                quarter(6, 2)
                for b in range(NB):
                    ts(vb[:, b, :], vt[0:SW, NC, 0:DV], wlast[:, b:b + 1], None, ALU.mult)
                conv_gate(6)
                quarter(6, 3)
                dve.wait_ge(num_mm, hv)
                den_p, den_s = ps[:, 6, :], ps[:, 7, 2 * SW:3 * SW]
                stt(em[:, 0:TP], den_p, -1.0, em[:, 0:TP], ALU.mult, ALU.max)
                link(stt(em[:, TP:T], den_s, -1.0, em[:, TP:T], ALU.mult, ALU.max))
                tt(em[:, 0:TP], den_p, em[:, 0:TP], ALU.max)
                link(tt(em[:, TP:T], den_s, em[:, TP:T], ALU.max))
                dve.reciprocal(em[:, 0:HT], em[:, 0:HT])
                quarter(7, 0)
                link(dve.reciprocal(em[:, HT:T], em[:, HT:T]))
                for j, hh in ((0, flat(h0)), (1, flat(h1))):
                    tt(hh[:, 0:TP], ps[:, 4 + j, :], em[:, 0:TP], ALU.mult)
                    ins = tt(hh[:, TP:T], ps[:, 7, j * SW:(j + 1) * SW], em[:, TP:T], ALU.mult)
                ins.then_inc(h_ok, 1)
                quarter(7, 1)
                quarter(7, 2)
                conv_input(7)
                quarter(7, 3)
                quarter(8, 0)
                dve.wait_ge(us_mm, hv)
                dve.wait_ge(cs_in, h * 16 + 16)
                for b in range(NB):
                    ins = stt(cs[:, b, :], cs[:, b, :], sc[:, NC + b:NC + b + 1],
                              ps[:, 4 + b // 2, (b % 2) * DV:(b % 2 + 1) * DV], ALU.mult, ALU.add)
                ins.then_inc(cs_ok, 1)
                quarter(8, 1)
                conv_sum(0)
                quarter(8, 2)
                conv_out(8, 0)
                quarter(8, 3)
                quarter(9, 0)
                conv_columns(1)
                dve.wait_ge(hs_mm, hv)
                to_rms(rh[:], side_halves(BLK_A), DV)
                dve.reciprocal(rh[:, 0, :], rh[:, 0, :])
                quarter(9, 1)
                dve.reciprocal(rh[:, 1, :], rh[:, 1, :]).then_inc(rh_in, 1)
                dve.wait_ge(ysq_ok, 2 * h + 1)
                sum_squares()
                quarter(9, 2)
                conv_gate(9)
                quarter(9, 3)
                quarter(10, 0)
                dve.wait_ge(rh_ok, hv)
                dve.wait_ge(so_ok, 2 * h + 2)
                for j, hh in ((0, h0), (1, h1)):
                    link(stt(hh[:], hh[:], gml[:, j:j + 1], rh[:], ALU.mult, ALU.mult))
                    ins = tt(mixf[:, ds(h * 4 + (2 * NG + 2 * j), 2), :], hh[:], so[:, j], ALU.mult)
                if last:
                    ins.then_inc(mix_heads, 1)
                quarter(10, 1)
                early(0, 2)
                quarter(10, 2)
                early(2, 4)
                conv_input(10)
                quarter(10, 3)
                quarter(11, 0)
                conv_sum(1)
                early(4, 6)
                quarter(11, 1)
                early(6, 8)
                quarter(11, 2)
                early(8, 10)
                conv_out(11, 1)
                quarter(11, 3)
                dve.wait_ge(ysq_ok, 2 * h + 2)
                sum_squares()
                if last:
                    rows_from_psum()
                    return
                quarter(12, 0)
                head_columns(h + 1)
                quarter(12, 1)
                quarter(12, 2)
                done(12)
                evac(stt(qf[:], pair(1), QS, rstd[:], ALU.mult, ALU.mult))
                quarter(12, 3)
                for q in range(3):
                    quarter(13, q)
                done(13)
                evac(tt(kf[:], pair(2), rstd[:], ALU.mult))
                quarter(13, 3)

            def mix_low(n):
                k = MIX_K[n]
                dve.wait_ge(mix_hi, n + 1)
                tt(mixlo[:, 2 * k:2 * k + 2, :], mixf[:, 2 * k:2 * k + 2, :],
                   mixhi[:, 2 * k:2 * k + 2, :].bitcast(F32), ALU.subtract).then_inc(mix_lo, 1)

            def rows_from_psum():
                dve.wait_ge(tail_mm, 1)
                dve.tensor_copy(n_rows[:], ps[0:(NB + 1) * H, BLK_A + 1, 384:384 + P])
                dve.tensor_copy(conv_rows[:], side(BLK_B, DC)[0:2 + 2 * NB]).then_inc(rows_out, 1)

            LINKS_H = LINKS["head"]
            with dve.Fori(0, H - 1) as h:
                start = chain.enter(h, LINKS_H)
                round_of_head(h, False)
                chain.leave(start, H - 1, "head")
            round_of_head(H - 1, True)

            for n in range(10, KT):
                mix_low(n)
                if n == 11:
                    dve.wait_ge(ssc_mm, 1)
                    to_rms(rh[:], side_halves(BLK_A), DC)
            dve.reciprocal(rh[:, 0, :], rh[:, 0, :])
            split_out(I_OUT + 1, 0)
            dve.reciprocal(rh[:, 1, :], rh[:, 1, :]).then_inc(rc_in, 1)
            for q in range(1, 4):
                split_out(I_OUT + 1, q)
            link(dve.memset(ssq2[:], 0.0))
            dve.wait_ge(rc_ok, 1)

            def out_tile(n, parity, nxt):
                i = n + I_OUT
                x_n = ds(n * 2, 2)
                for q in range(3):
                    nxt(q)
                tile_done(i)
                link(tt(t2[:], conv_pair(parity), rh[:], ALU.mult))
                tt(t2[:], t2[:], pair(parity), ALU.add).then_inc(tile_read, 1)
                dve.wait_ge(tile_read, i + 2)
                link(tt(t2[:], t2[:], xhi[:, x_n, :].bitcast(F32), ALU.add))
                tt(x1[:], t2[:], xlo[:, x_n, :].bitcast(F32), ALU.add).then_inc(x1_ok, 1)
                nxt(3)
                dve.wait_ge(x1_hi, n + 1)
                tt(xlo[:, x_n, :], x1[:], xhi[:, x_n, :].bitcast(F32), ALU.subtract).then_inc(x1_lo, 1)
                dve.wait_ge(x1_sq, n + 1)
                tt(ssq2[:], ssq2[:], sq2[:], ALU.add).then_inc(ss2_ok, 1)
                dve.wait_ge(ss2_ok, n + 1)

            out_tile(0, I_OUT, lambda q: None)
            out_tile(1, I_OUT + 1, lambda q: split_out(I_OUT + 2, q))
            with dve.Fori(1, KT // 2 - 1) as n2:
                start = chain.enter(n2 - 1, LINKS["out"])
                for p in range(2):
                    n = n2 * 2 + p
                    out_tile(n, I_OUT + p, lambda q: split_out(n + (I_OUT + 1), q))
                chain.leave(start, KT // 2 - 2, "out")
            out_tile(KT - 2, I_OUT, lambda q: split_out(I_OUT + KT - 1, q))
            out_tile(KT - 1, I_OUT + 1, lambda q: split(I_FFN, q, V_G2))
            split(I_FFN + 1, 0, V_G2)
            dve.wait_ge(ss2_mm, 1)
            to_rms(rstd[:], side_halves(BLK_A), D)
            dve.reciprocal(rstd[:, 0, :], rstd[:, 0, :])
            split(I_FFN + 1, 1, V_G2)
            dve.reciprocal(rstd[:, 1, :], rstd[:, 1, :]).then_inc(r2_in, 1)
            split(I_FFN + 1, 2, V_G2)
            dve.wait_ge(r2_ok, 1)

            def up(c, f, i, nxt, begun=False):
                if not begun:
                    for q in range(3):
                        split(i + 1, q, V_G2)
                tile_done(i)
                tt(gact[:], pair(I_FFN), rstd[:], ALU.mult).then_inc(tile_read, 1)
                split(i + 1, 3, V_G2)
                nxt(0)
                dve.wait_ge(s_ok, c * FC + (f + 1))
                link(tt(sact[:], sact[:], gact[:], ALU.mult))
                link(tt(sact[:], sact[:], rstd[:], ALU.mult))
                nxt(1)
                nxt(2)
                tile_done(i + 1)
                tt(hf[:], pair(I_FFN + 1), sact[:], ALU.mult).then_inc(tile_read, 1)
                nxt(3)
                dve.wait_ge(h_hi, c * FC + (f + 1))
                f_n = ds(f * 2, 2)
                tt(hlo[:, f_n, :], hf[:], hhi[:, f_n, :].bitcast(F32), ALU.subtract).then_inc(h_lo, 1)

            def up_phase(c, i0, begun=False):
                up(c, 0, i0, lambda q: split(i0 + 2, q, V_G2), begun)
                with dve.Fori(1, FC - 1) as f:
                    start = chain.enter(f - 1, LINKS["up"])
                    up(c, f, i0 + f * 2, lambda q: split(i0 + f * 2 + 2, q, V_G2))
                    chain.leave(start, FC - 2, "up")
                i = i0 + 2 * (FC - 1)
                up(c, FC - 1, i, lambda q: split(i + 2, q, sizes=K_DOWN))

            def down(n, i, parity, first, nxt):
                for q in range(3):
                    nxt(q)
                tile_done(i)
                a = acc[:, ds(n * 2, 2), :]
                if first:
                    tt(gact[:], pair(parity), xhi[:, ds(n * 2, 2), :].bitcast(F32), ALU.add).then_inc(tile_read, 1)
                    dve.wait_ge(tile_read, i + 2)
                    tt(a, gact[:], xlo[:, ds(n * 2, 2), :].bitcast(F32), ALU.add)
                else:
                    tt(a, pair(parity), a, ALU.add).then_inc(tile_read, 1)
                nxt(3)

            def chunk(c, first):
                i0 = c * PER_CH + I_FFN
                up_phase(c, i0, first)
                i1 = i0 + 2 * FC
                with dve.Fori(0, KT // 2 - 1) as n2:
                    for p in range(2):
                        down(n2 * 2 + p, i1 + n2 * 2 + p, I_FFN + p, first,
                             lambda q: split(i1 + n2 * 2 + (p + 1), q, sizes=K_DOWN))
                down(KT - 2, i1 + (KT - 2), I_FFN, first, lambda q: split(i1 + (KT - 1), q, sizes=K_DOWN))
                down(KT - 1, i1 + (KT - 1), I_FFN + 1, first, lambda q: split(i0 + PER_CH, q, V_G2))

            dve.wait_ge(small_out, 16 * 6)
            chunk(0, True)
            with dve.Fori(1, NCH - 1) as c:
                start = chain.enter(c - 1, LINKS["chunk"])
                chunk(c, False)
                chain.leave(start, NCH - 2, "chunk")
            c, i0 = NCH - 1, I_FFN + (NCH - 1) * PER_CH
            i1 = i0 + 2 * FC
            up_phase(c, i0)
            link(dve.memset(ssq_f[:], 0.0))

            def last_down(n, p, nxt=None, tile=None, a=None, before=None):
                if nxt:
                    for q in range(3):
                        nxt(q)
                if before:
                    before()
                tile_done(n + i1)
                n_col = n if tile is None else tile
                h = slice(0, 2) if a is None else slice(a, a + 1)
                both = ds(n_col * 2, 2) if a is None else slice(2 * n_col + a, 2 * n_col + a + 1)
                tt(zf[:, p, h], pair(I_FFN + p)[:, h], acc[:, both, :], ALU.add).then_inc(tile_read, 1)
                dve.wait_ge(tile_read, n + (i1 + 2))
                if not (isinstance(n, int) and n < 2):
                    dve.wait_ge(out_t, n - 1)
                ts(zgn[:, p, h], zf[:, p, h], vecs[:, ds(n_col + V_GF, 1)], None, ALU.mult).then_inc(zg_n, 1)
                if nxt:
                    nxt(3)
                dve.wait_ge(z_sq, n + 1)
                tt(ssq_f[:, h], ssq_f[:, h], sqf[:, h], ALU.add).then_inc(ssf_ok, 1)
                dve.wait_ge(ssf_ok, n + 1)

            for n in range(2):
                last_down(n, n, lambda q: split(i1 + n + 1, q, sizes=K_DOWN))
            with dve.Fori(1, KT // 2 - 1) as m:
                for p in range(2):
                    last_down(m * 2 + p, p, lambda q: split(m * 2 + (i1 + p + 1), q, sizes=K_DOWN))

            def rms_half(a):
                dve.wait_ge(rf_mm, a + 1)
                c = ss_col[0:XTW, a * XH:(a + 1) * XH]
                to_rms(c, ps[0:XTW, 2 - 2 * a, a * XH:(a + 1) * XH], D)
                dve.reciprocal(c, c).then_inc(rf_in, 1)

            def scale_half(a, places=(0, 2)):
                dve.wait_ge(rf_ok, a + 1)
                dve.wait_ge(out_read, KT + 2 * a)
                for t in [a * XH + b for b in places]:
                    ts(otok[:, t, :], otok[:, t, :], ss_col[0:XTW, t:t + 1], None, ALU.mult).then_inc(yd_ready, 1)

            def half_step(j, before=None):
                n = KT - 2 + j
                nxt = (lambda q: split(i1 + n + 1, q, sizes=K_DOWN)) if j < 3 else None
                last_down(n, j % 2, nxt, HALVES[j][0], HALVES[j][1], before)

            half_step(0)
            half_step(1)
            half_step(2, lambda: rms_half(0))
            scale_half(0, (0,))
            half_step(3)
            scale_half(0, (2,))
            rms_half(1)
            scale_half(1)


_INS = ["x_prompt", "x_sample", "state_conv", "state_mlstm_C", "state_mlstm_n", "state_mlstm_m",
        "norm1_g", "w_in", "b_igate", "b_fgate", "conv_w", "conv_out_g", "mlstm_out_g", "w_out",
        "norm2_g", "w_ffn_gate", "w_ffn_up", "w_ffn_down", "final_norm_g"]


def kernel(**inputs):
    import numpy as _np
    import concourse.bacc as _bacc
    from concourse import mybir as _mybir
    from concourse.bass_utils import run_bass_kernel_spmd as _run

    xp, xs = inputs["x_prompt"].shape, inputs["x_sample"].shape
    _, nb, heads, dk, dv = inputs["state_mlstm_C"].shape
    taps, dc = inputs["conv_w"].shape[1:]
    out_shapes = [xp, xs, (1, 1, taps - 1, dc), (1, 1, heads, dk, dv), (1, 1, heads, dk), (1, 1, heads),
                  (1, nb, taps - 1, dc), (1, nb, heads, dk, dv), (1, nb, heads, dk), (1, nb, heads)]
    nc = _bacc.Bacc("TRN2", target_bir_lowering=False, num_devices=1)
    arrays, args = {}, []
    for name in _INS:
        a = _np.ascontiguousarray(inputs[name])
        arrays[f"in_{name}_dram"] = a
        args.append(nc.dram_tensor(f"in_{name}_dram", a.shape, _mybir.dt.from_np(a.dtype), kind="ExternalInput").ap())
    for i, shape in enumerate(out_shapes):
        args.append(nc.dram_tensor(f"out_{i}_dram", shape, _mybir.dt.float32, kind="ExternalOutput").ap())
    hybrid_trunk_step(nc, *args)
    r = _run(nc, [arrays], core_ids=[0])
    return tuple(r.results[0][f"out_{i}_dram"] for i in range(len(out_shapes)))
```
